# Optimizing a Trainium2 kernel written in Bass

```python
import math
import jax
import jax.numpy as jnp
from jax import lax
import numpy as np

D_MODEL = 1024
BATCH = 1
SEQ = 1024
DEPTH = 1
DEC_BATCH = 8
DEC_SEQ = 1
PAST_LEN = 2048
PAGE_SIZE = 128

N_HEADS = 8
KV_HEADS = 2
HEADS_PER_GROUP = N_HEADS // KV_HEADS
HEAD_DIM = 64
Q_DIM = N_HEADS * HEAD_DIM
KV_DIM = KV_HEADS * HEAD_DIM
CMP_LEN = 32
CMP_STRIDE = 16
CMP_HID = 2 * HEAD_DIM
SEL_LEN = 64
N_SEL_BLOCKS = 16
WINDOW = 512
Q_BLOCK = 128
GM_GROUPS = 4
GM_CHUNK = 128
GM_DIM = D_MODEL // 2
GM_GROUP_DIM = GM_DIM // GM_GROUPS
D_FF = -(-8 * D_MODEL // (3 * 256)) * 256
PLE_DIM = 256
N_BUCKETS = 32
MAX_DISTANCE = 128
EPS = 1e-6
NEG_INF = -1e30
FORCE_SCORE = 1e6
IN_DIM = Q_DIM + 6 * KV_DIM + 3 * N_HEADS + 2 * GM_DIM + 2 * D_MODEL

kernel_name = 'nsa_gmlp_parallel_hybrid_step'

def rms_norm(x, g):
    xf = x.astype(jnp.float32)
    y = xf * lax.rsqrt(jnp.mean(xf * xf, axis=-1, keepdims=True) + EPS)
    return (y * g.astype(jnp.float32)).astype(x.dtype)

def layer_norm(x, g, b):
    xf = x.astype(jnp.float32)
    mu = jnp.mean(xf, axis=-1, keepdims=True)
    var = jnp.mean(jnp.square(xf - mu), axis=-1, keepdims=True)
    y = (xf - mu) * lax.rsqrt(var + EPS)
    return (y * g.astype(jnp.float32) + b.astype(jnp.float32)).astype(x.dtype)

def t5_bucket(dist):
    dist = jnp.maximum(dist, 0)
    max_exact = N_BUCKETS // 2
    ratio = jnp.log(jnp.maximum(dist, 1).astype(jnp.float32) / max_exact) / math.log(MAX_DISTANCE / max_exact)
    large = jnp.minimum(max_exact + (ratio * (N_BUCKETS - max_exact)).astype(jnp.int32), N_BUCKETS - 1)
    return jnp.where(dist < max_exact, dist, large)

def rel_bias_heads(rel_bias, dist):
    b = rel_bias[t5_bucket(dist)].astype(jnp.float32)
    return b.reshape(dist.shape + (KV_HEADS, HEADS_PER_GROUP)).transpose(2, 3, 0, 1)

def masked_softmax(s, mask):
    p = jax.nn.softmax(jnp.where(mask, s, NEG_INF), axis=-1)
    return jnp.where(mask, p, 0.0)

def compress_rows(rows, pe, w1, w2):
    bsz, t = rows.shape[:2]
    n_sub = CMP_LEN // CMP_STRIDE
    nc = (t - CMP_LEN) // CMP_STRIDE + 1
    ns = nc + n_sub - 1
    sub = rows[:, :ns * CMP_STRIDE].reshape(bsz, ns, CMP_STRIDE, KV_HEADS, HEAD_DIM)
    sub = sub.transpose(0, 1, 3, 2, 4).reshape(bsz, ns, KV_HEADS, CMP_STRIDE * HEAD_DIM)
    w1s = w1.reshape(n_sub, CMP_STRIDE * HEAD_DIM, CMP_HID)
    pre = pe.reshape(-1) @ w1
    for j in range(n_sub):
        pre = pre + sub[:, j:j + nc] @ w1s[j]
    return jax.nn.silu(pre) @ w2

def compress_kv(rows, comp_w):
    pe_k, w1_k, w2_k, pe_v, w1_v, w2_v = comp_w
    kc = compress_rows(rows[:, :, 0], pe_k, w1_k, w2_k)
    vc = compress_rows(rows[:, :, 1], pe_v, w1_v, w2_v)
    cend = jnp.arange(kc.shape[1]) * CMP_STRIDE + CMP_LEN - 1
    return kc, vc, cend

def selection_blocks(rows):
    bsz, t = rows.shape[:2]
    nsel = -(-t // SEL_LEN)
    rows = jnp.pad(rows, ((0, 0), (0, nsel * SEL_LEN - t), (0, 0), (0, 0), (0, 0)))
    blk = rows.reshape(bsz, nsel, SEL_LEN, 2, KV_HEADS, HEAD_DIM).transpose(3, 0, 4, 1, 2, 5)
    return blk[0], blk[1]

def nsa_attend(q, qpos, kc, vc, cend, ks_blk, vs_blk, kw, vw, wpos, gate, rel_bias):
    bsz, nq = q.shape[:2]
    nsel = ks_blk.shape[2]
    scale = HEAD_DIM ** -0.5
    s_c = jnp.einsum('bqghd,bngd->bghqn', q, kc).astype(jnp.float32) * scale
    s_c = s_c + rel_bias_heads(rel_bias, qpos[:, None] - cend[None, :])
    p_c = masked_softmax(s_c, cend[None, :] <= qpos[:, None])
    o_c = jnp.einsum('bghqn,bngd->bqghd', p_c.astype(vc.dtype), vc)
    ci = jnp.arange(kc.shape[1])[:, None] * CMP_STRIDE
    sj = jnp.arange(nsel)[None, :] * SEL_LEN
    overlap = ((ci <= sj + SEL_LEN - 1) & (ci + CMP_LEN - 1 >= sj)).astype(jnp.float32)
    imp = jnp.einsum('bghqn,nj->bgqj', p_c, overlap)
    blk = jnp.arange(nsel)[None, :]
    qblk = (qpos // SEL_LEN)[:, None]
    forced = (blk == 0) | (blk == qblk) | (blk == qblk - 1)
    score = jnp.where(forced, FORCE_SCORE, jnp.where(blk <= qblk, imp, -FORCE_SCORE))
    _, idx = lax.top_k(score, min(N_SEL_BLOCKS, nsel))
    bi = jnp.arange(bsz)[:, None, None, None]
    gi = jnp.arange(KV_HEADS)[None, :, None, None]
    k_sel = ks_blk[bi, gi, idx]
    v_sel = vs_blk[bi, gi, idx]
    tpos = idx[..., None] * SEL_LEN + jnp.arange(SEL_LEN)
    qp = qpos[None, None, :, None, None]
    tbl = rel_bias.reshape(N_BUCKETS, KV_HEADS, HEADS_PER_GROUP)
    b_s = tbl[t5_bucket(qp - tpos), gi[..., None]].astype(jnp.float32)
    s_s = jnp.einsum('bqghd,bgqkld->bghqkl', q, k_sel).astype(jnp.float32) * scale
    s_s = s_s + b_s.transpose(0, 1, 5, 2, 3, 4)
    nk = idx.shape[-1] * SEL_LEN
    p_s = masked_softmax(s_s.reshape(bsz, KV_HEADS, HEADS_PER_GROUP, nq, nk),
                         (tpos <= qp).reshape(bsz, KV_HEADS, 1, nq, nk))
    o_s = jnp.einsum('bghqm,bgqmd->bqghd', p_s.astype(v_sel.dtype),
                     v_sel.reshape(bsz, KV_HEADS, nq, nk, HEAD_DIM))
    dw = qpos[:, None] - wpos[None, :]
    s_w = jnp.einsum('bqghd,bkgd->bghqk', q, kw).astype(jnp.float32) * scale
    s_w = s_w + rel_bias_heads(rel_bias, dw)
    p_w = masked_softmax(s_w, (dw >= 0) & (dw <= WINDOW) & (wpos[None, :] >= 0))
    o_w = jnp.einsum('bghqk,bkgd->bqghd', p_w.astype(vw.dtype), vw)
    g = jax.nn.sigmoid(gate.astype(jnp.float32))
    o = g[..., 0:1] * o_c + g[..., 1:2] * o_s + g[..., 2:3] * o_w
    return o.astype(q.dtype).reshape(bsz, nq, Q_DIM)

def nsa_prompt(q, gate, cmp, slc, win, comp_w, rel_bias):
    bsz, seq = q.shape[:2]
    kc, vc, cend = compress_kv(cmp, comp_w)
    ks_blk, vs_blk = selection_blocks(slc)
    win_pad = jnp.pad(win, ((0, 0), (WINDOW, 0), (0, 0), (0, 0), (0, 0)))
    n_qb = seq // Q_BLOCK
    q_b = q.reshape((bsz, n_qb, Q_BLOCK) + q.shape[2:]).swapaxes(0, 1)
    g_b = gate.reshape((bsz, n_qb, Q_BLOCK) + gate.shape[2:]).swapaxes(0, 1)

    def one_block(args):
        q_blk, g_blk, b = args
        start = b * Q_BLOCK
        qpos = start + jnp.arange(Q_BLOCK)
        kv_w = lax.dynamic_slice_in_dim(win_pad, start, WINDOW + Q_BLOCK, axis=1)
        wpos = start - WINDOW + jnp.arange(WINDOW + Q_BLOCK)
        return nsa_attend(q_blk, qpos, kc, vc, cend, ks_blk, vs_blk,
                          kv_w[:, :, 0], kv_w[:, :, 1], wpos, g_blk, rel_bias)

    o = lax.map(one_block, (q_b, g_b, jnp.arange(n_qb)))
    o = o.swapaxes(0, 1).reshape(bsz, seq, Q_DIM)
    return o, win[:, seq - min(WINDOW, seq):]

def nsa_sample(q, gate, cmp_new, slc_new, win_new, cache_cmp, cache_slc, win_buf, page_table, comp_w, rel_bias):
    bsz, nq = q.shape[:2]
    past_len = page_table.shape[1] * PAGE_SIZE

    def gather_past(cache):
        return cache[page_table].reshape(bsz, past_len, 2, KV_HEADS, HEAD_DIM)

    cmp_all = jnp.concatenate([gather_past(cache_cmp), cmp_new], axis=1)
    slc_all = jnp.concatenate([gather_past(cache_slc), slc_new], axis=1)
    win_all = jnp.concatenate([win_buf, win_new], axis=1)
    w_buf = win_buf.shape[1]
    qpos = past_len + jnp.arange(nq)
    wpos = past_len - w_buf + jnp.arange(w_buf + nq)
    kc, vc, cend = compress_kv(cmp_all, comp_w)
    ks_blk, vs_blk = selection_blocks(slc_all)
    o = nsa_attend(q, qpos, kc, vc, cend, ks_blk, vs_blk,
                   win_all[:, :, 0], win_all[:, :, 1], wpos, gate, rel_bias)
    return o, win_all[:, nq:]

def chunk_spatial_mix(v, w_s, b_s):
    bsz, t = v.shape[:2]
    nch = -(-t // GM_CHUNK)
    vp = jnp.pad(v, ((0, 0), (0, nch * GM_CHUNK - t), (0, 0)))
    vp = vp.reshape(bsz, nch, GM_CHUNK, GM_GROUPS, GM_GROUP_DIM)
    w = w_s * jnp.tril(jnp.ones((GM_CHUNK, GM_CHUNK), w_s.dtype))
    s = jnp.einsum('gts,bcsgd->bctgd', w, vp) + b_s.T[None, None, :, :, None]
    return s.reshape(bsz, nch * GM_CHUNK, GM_DIM)[:, :t]

def trunk_layer(x, ple, attend, ln_mix_pre, w_in, gm_ln_g, gm_ln_b, gm_ws, gm_bs,
                w_branch_nsa, w_branch_gm, w_out, ln_mix_post, ln_ffn_pre, w_ffn_gate,
                w_ffn_up, w_ffn_down, ln_ffn_post, w_ple, w_ple_gate, ln_ple_post):
    bsz, t, _ = x.shape
    h = rms_norm(x, ln_mix_pre)
    z = h @ w_in
    sizes = [Q_DIM, 2 * KV_DIM, 2 * KV_DIM, 2 * KV_DIM, 3 * N_HEADS, 2 * GM_DIM, 2 * D_MODEL]
    q, cmp, slc, win, gate, uv, mg = jnp.split(z, np.cumsum(sizes)[:-1].tolist(), axis=-1)
    q = q.reshape(bsz, t, KV_HEADS, HEADS_PER_GROUP, HEAD_DIM)
    gate = gate.reshape(bsz, t, KV_HEADS, HEADS_PER_GROUP, 3)
    cmp = cmp.reshape(bsz, t, 2, KV_HEADS, HEAD_DIM)
    slc = slc.reshape(bsz, t, 2, KV_HEADS, HEAD_DIM)
    win = win.reshape(bsz, t, 2, KV_HEADS, HEAD_DIM)
    o_nsa, win_state = attend(q, gate, cmp, slc, win)
    u, v = jnp.split(jax.nn.gelu(uv), 2, axis=-1)
    v = layer_norm(v, gm_ln_g, gm_ln_b)
    o_gm = u * chunk_spatial_mix(v, gm_ws, gm_bs)
    g_a, g_b = jnp.split(jax.nn.sigmoid(mg), 2, axis=-1)
    mixed = (g_a * (o_nsa @ w_branch_nsa) + g_b * (o_gm @ w_branch_gm)) @ w_out
    x = x + rms_norm(mixed, ln_mix_post)
    h2 = rms_norm(x, ln_ffn_pre)
    f = (jax.nn.silu(h2 @ w_ffn_gate) * (h2 @ w_ffn_up)) @ w_ffn_down
    x = x + rms_norm(f, ln_ffn_post)
    e = ple @ w_ple
    x = x + rms_norm(jax.nn.sigmoid(x @ w_ple_gate) * e, ln_ple_post)
    return x, cmp, slc, win_state, v

def setup_inputs(seed: int = 0) -> dict:
    key = jax.random.key(seed)
    keys = iter(jax.random.split(key, 48))

    def nrm(shape, scale):
        return jax.random.normal(next(keys), shape, jnp.float32) * scale

    def gain(shape):
        return 1.0 + nrm(shape, 0.05)

    n_pages = PAST_LEN // PAGE_SIZE
    n_pool = (DEC_BATCH * n_pages * 5) // 4
    w_buf = min(WINDOW, PAST_LEN)
    x_prompt = nrm((BATCH, SEQ, D_MODEL), 1.0)
    x_sample = nrm((DEC_BATCH, DEC_SEQ, D_MODEL), 1.0)
    cache_cmp_kv = nrm((DEPTH, n_pool, PAGE_SIZE, 2, KV_HEADS, HEAD_DIM), 1.0)
    cache_slc_kv = nrm((DEPTH, n_pool, PAGE_SIZE, 2, KV_HEADS, HEAD_DIM), 1.0)
    state_win_kv = nrm((DEPTH, DEC_BATCH, w_buf, 2, KV_HEADS, HEAD_DIM), 1.0)
    perm = jax.random.permutation(next(keys), n_pool)
    page_table = perm[:DEC_BATCH * n_pages].reshape(DEC_BATCH, n_pages).astype(jnp.int32)
    p_prompt = nrm((DEPTH, BATCH, SEQ, PLE_DIM), 1.0)
    p_sample = nrm((DEPTH, DEC_BATCH, DEC_SEQ, PLE_DIM), 1.0)
    return {
        'x_prompt': x_prompt,
        'x_sample': x_sample,
        'cache_cmp_kv': cache_cmp_kv,
        'cache_slc_kv': cache_slc_kv,
        'state_win_kv': state_win_kv,
        'page_table': page_table,
        'p_prompt': p_prompt,
        'p_sample': p_sample,
        'rel_bias': nrm((N_BUCKETS, N_HEADS), 0.5),
        'ln_mix_pre': gain((DEPTH, D_MODEL)),
        'w_in': nrm((DEPTH, D_MODEL, IN_DIM), D_MODEL ** -0.5),
        'cmp_pe_k': nrm((DEPTH, CMP_LEN, HEAD_DIM), 0.1),
        'cmp_w1_k': nrm((DEPTH, CMP_LEN * HEAD_DIM, CMP_HID), (CMP_LEN * HEAD_DIM) ** -0.5),
        'cmp_w2_k': nrm((DEPTH, CMP_HID, HEAD_DIM), CMP_HID ** -0.5),
        'cmp_pe_v': nrm((DEPTH, CMP_LEN, HEAD_DIM), 0.1),
        'cmp_w1_v': nrm((DEPTH, CMP_LEN * HEAD_DIM, CMP_HID), (CMP_LEN * HEAD_DIM) ** -0.5),
        'cmp_w2_v': nrm((DEPTH, CMP_HID, HEAD_DIM), CMP_HID ** -0.5),
        'gm_ln_g': gain((DEPTH, GM_DIM)),
        'gm_ln_b': nrm((DEPTH, GM_DIM), 0.02),
        'gm_ws': nrm((DEPTH, GM_GROUPS, GM_CHUNK, GM_CHUNK), GM_CHUNK ** -0.5),
        'gm_bs': gain((DEPTH, GM_GROUPS, GM_CHUNK)),
        'w_branch_nsa': nrm((DEPTH, Q_DIM, D_MODEL), Q_DIM ** -0.5),
        'w_branch_gm': nrm((DEPTH, GM_DIM, D_MODEL), GM_DIM ** -0.5),
        'w_out': nrm((DEPTH, D_MODEL, D_MODEL), D_MODEL ** -0.5),
        'ln_mix_post': gain((DEPTH, D_MODEL)),
        'ln_ffn_pre': gain((DEPTH, D_MODEL)),
        'w_ffn_gate': nrm((DEPTH, D_MODEL, D_FF), D_MODEL ** -0.5),
        'w_ffn_up': nrm((DEPTH, D_MODEL, D_FF), D_MODEL ** -0.5),
        'w_ffn_down': nrm((DEPTH, D_FF, D_MODEL), D_FF ** -0.5),
        'ln_ffn_post': gain((DEPTH, D_MODEL)),
        'w_ple': nrm((DEPTH, PLE_DIM, D_MODEL), PLE_DIM ** -0.5),
        'w_ple_gate': nrm((DEPTH, D_MODEL, D_MODEL), D_MODEL ** -0.5),
        'ln_ple_post': gain((DEPTH, D_MODEL)),
    }

def reference(x_prompt, x_sample, cache_cmp_kv, cache_slc_kv, state_win_kv, page_table,
              p_prompt, p_sample, rel_bias, ln_mix_pre, w_in, cmp_pe_k, cmp_w1_k, cmp_w2_k,
              cmp_pe_v, cmp_w1_v, cmp_w2_v, gm_ln_g, gm_ln_b, gm_ws, gm_bs, w_branch_nsa,
              w_branch_gm, w_out, ln_mix_post, ln_ffn_pre, w_ffn_gate, w_ffn_up, w_ffn_down,
              ln_ffn_post, w_ple, w_ple_gate, ln_ple_post):
    xp = x_prompt
    xs = x_sample
    pc, ps, pw, sc, ss, sw, sv = [], [], [], [], [], [], []
    for i in range(DEPTH):
        comp_w = (cmp_pe_k[i], cmp_w1_k[i], cmp_w2_k[i], cmp_pe_v[i], cmp_w1_v[i], cmp_w2_v[i])
        layer_w = (ln_mix_pre[i], w_in[i], gm_ln_g[i], gm_ln_b[i], gm_ws[i], gm_bs[i],
                   w_branch_nsa[i], w_branch_gm[i], w_out[i], ln_mix_post[i], ln_ffn_pre[i],
                   w_ffn_gate[i], w_ffn_up[i], w_ffn_down[i], ln_ffn_post[i], w_ple[i],
                   w_ple_gate[i], ln_ple_post[i])

        def attend_prompt(q, gate, cmp, slc, win, comp_w=comp_w):
            return nsa_prompt(q, gate, cmp, slc, win, comp_w, rel_bias)

        def attend_sample(q, gate, cmp, slc, win, comp_w=comp_w, i=i):
            return nsa_sample(q, gate, cmp, slc, win, cache_cmp_kv[i], cache_slc_kv[i],
                              state_win_kv[i], page_table, comp_w, rel_bias)

        xp, c_p, s_p, w_p, _ = trunk_layer(xp, p_prompt[i], attend_prompt, *layer_w)
        xs, c_s, s_s, w_s, v_s = trunk_layer(xs, p_sample[i], attend_sample, *layer_w)
        pc.append(c_p)
        ps.append(s_p)
        pw.append(w_p)
        sc.append(c_s)
        ss.append(s_s)
        sw.append(w_s)
        sv.append(v_s)
    return (xp, xs, jnp.stack(pc), jnp.stack(ps), jnp.stack(pw), jnp.stack(sc), jnp.stack(ss), jnp.stack(sw), jnp.stack(sv))


_drawn_inputs = setup_inputs


def setup_inputs(seed=0):
    import zlib

    import numpy as np

    out = dict(_drawn_inputs(seed))
    spreads = {}
    factors = {'cmp_pe_k': 27.781, 'gm_ln_b': 3.001}
    for name, (base, spread) in spreads.items():
        noise = np.random.default_rng([zlib.crc32(name.encode()), seed]).standard_normal(out[name].shape)
        drawn = base * np.exp(spread * noise) if base else spread * noise
        out[name] = jnp.asarray(drawn.astype(out[name].dtype))
    for name, factor in factors.items():
        out[name] = (out[name] * factor).astype(out[name].dtype)
    return out
```

```python
from contextlib import ExitStack

import concourse.bass as bass
from concourse import mybir

F32 = mybir.dt.float32
I32 = mybir.dt.int32
ALU = mybir.AluOpType
ACT = mybir.ActivationFunctionType
AX = mybir.AxisListType.X

P = 128
D = 1024
T = 1024
B = 8
N = T + B
NT = 3
NW = N // NT
DC = D // P
TT = T // P
FH = 11
KV = 768
H = 8
HD = 64
NCP = 63
NCS = 127
NSEL = 33
TOPK = 16
EPS = 1e-6
NEG = -1e30
FORCE = 1e6
Q0, KV0, GATE0, U0, V0, GA0, GB0 = 0, 512, 1280, 1304, 1816, 2328, 3352
GM = 512
OH_CMP, OH_SELF, OH_NEAR, OH_WIN = 0, 127, 128, 256


def tokens(ap):
    return ap.rearrange("p (n w) -> p n w", n=NT)


def chunks(ap, n):
    return ap.rearrange("p (c t) -> p c t", c=n)


class Core:
    pass


class Stage:

    def __init__(self, k, name):
        self.k, self.name, self.stack, self.mine = k, name, ExitStack(), []

    def __enter__(self):
        self.stack.__enter__()
        return self

    def sems(self, names):
        new = [self.k.nc.alloc_semaphore(f"{self.name}_{n}") for n in names.split()]
        self.mine += new
        return new

    def psum(self, what, shape):
        return self.stack.enter_context(self.k.nc.psum_tensor(f"{self.name}_{what}", shape, F32))

    def block(self):
        return self.stack.enter_context(self.k.nc.Block())

    def __exit__(self, *a):
        self.stack.__exit__(*a)
        self.k.used += self.mine


def build(nc, g, out, scratch):
    with ExitStack() as ctx:
        k = Core()
        k.nc, k.g, k.out, k.scratch = nc, g, out, scratch

        def sb(name, shape, dt=F32):
            return ctx.enter_context(nc.sbuf_tensor(name, shape, dt))

        k.X = sb("X", [P, DC, N])
        k.Hr = sb("Hr", [P, DC * N])
        k.H = chunks(k.Hr[:], DC)
        k.Z = sb("Z", [P, 21360])
        k.W = sb("W", [P, 2, FH, P])
        k.CW = sb("CW", [P, 4096])
        k.E = sb("E", [P, 5632])
        k.R1 = sb("R1", [P, N])
        k.ident = sb("ident", [P, P])
        k.ones = sb("ones", [P, P])
        k.gains = sb("gains", [P, 5, DC])
        k.gtok = sb("gtok", [P, TT, 24])
        k.gfm = sb("gfm", [24, B])
        k.pid = sb("pid", [P, B], I32)
        k.relb = sb("relb", [33, H])
        k.tiny = sb("tiny", [P, 16])
        k.kvtok = k.Z[:, 0:9 * KV].rearrange("p (t f) -> p t f", f=KV)
        o = 9 * KV
        k.Q = chunks(k.Z[:, o:o + 4 * N], 4)
        k.KT3 = chunks(k.Z[:, o + 3 * N:o + 6 * N], 3)
        o += 4 * N
        k.KT = chunks(k.Z[:, o:o + 2 * N], 2)
        o += 2 * N
        k.OG = chunks(k.Z[:, o:o + 4 * N], 4)
        o += 4 * N
        k.ON = chunks(k.Z[:, o:o + 4 * N], 4)
        k.ONr = k.Z[:, o:o + 4 * N]
        k.MT = chunks(k.Z[:, 0:8 * N], 8)
        k.MX = chunks(k.Z[:, 8 * N:16 * N], 8)
        k.A = chunks(k.Z[:, 0:FH * N], FH)
        k.F = chunks(k.Z[:, FH * N:(FH + 8) * N], 8)
        k.wfull = [ctx.enter_context(nc.semaphore(f"weights_full_{i}")) for i in range(2)]
        k.wcount = [0, 0]
        k.vtok = k.E[:, 0:9 * GM].rearrange("p (t f) -> p t f", f=GM)
        k.KC = k.E[:, 0:9 * P].rearrange("p (b n) -> p b n", b=9)
        k.VC = k.E[:, 9 * P:18 * P].rearrange("p (b n) -> p b n", b=9)
        k.small = sb("small", [P, 32])
        k.QS8 = k.Hr[:, 8192:8256].rearrange("p (b h) -> p b h", b=B)
        k.MG = k.E[0:H, 4888:5176].rearrange("p (b x) -> p b x", b=B)
        k.OC = k.E[:, 5176:5240].rearrange("p (b h) -> p b h", b=B)
        k.near_b = k.E[0:H, 5240:5369]
        k.e8 = k.E[0:B, 5376:5440].rearrange("p (a b) -> p a b", a=B)
        k.NB = k.E[:, 2304:4352].rearrange("p (h j) -> p h j", h=H)
        k.BC = k.E[:, 4352:5304].rearrange("p (h m) -> p h m", h=H)
        k.WM = k.E[:, 5304:5432]
        k.win_b = k.CW[0:H, 3584:4096]
        k.used = []
        load_x(k)
        norm_stage(k, "norm1", k.X, None, None, 0)
        project_kv(k)
        project_quv(k)
        spatial_gate(k)
        compress(k)
        select_blocks(k)
        sample_attention(k)
        bias_tables(k)
        prompt_attention(k)
        nc.clear_and_free_semaphores(k.used)
        nc.all_engine_barrier()
        k.used = []
        apply_norm1(k)
        merge(k)
        out_projection(k)
        norm_stage(k, "mix_post", k.MX, 1, None, None)
        norm_stage(k, "ffn_pre", k.X, None, None, 2)
        ffn(k, 0)
        ffn(k, 1)
        norm_stage(k, "ffn_post", k.F, 3, None, None)
        ple(k)
        norm_stage(k, "ple_post", k.F, 4, None, None)
        store_y(k)


def load_x(k):
    nc, g = k.nc, k.g
    with Stage(k, "load") as st:
        xtok = k.Z[:, 0:9 * D].rearrange("p (t f) -> p t f", f=D)
        ps = st.psum("ps", [P, 4, 1024])
        x_in = st.sems(" ".join(f"x_in_{t}" for t in range(9)))
        eye_in, const_in, ones_set, transposed, copied, rel_in, rel_sub, pid_in, pid_mul = st.sems(
            "eye_in const_in ones_set transposed copied rel_in rel_sub pid_in pid_mul")
        pid1 = st.stack.enter_context(nc.sbuf_tensor("pid1", [P, B + 1], I32))
        far = st.stack.enter_context(nc.sbuf_tensor("far", [32, H], F32))
        block = st.block()

        @block.sync
        def _(sp):
            sp.dma_start(k.ident[:], g["eye"]).then_inc(eye_in, 16)
            for t in range(TT):
                sp.dma_start(xtok[:, t, :], g["x_prompt"][t * P:(t + 1) * P, :]).then_inc(x_in[t], 16)
            sp.dma_start(xtok[0:B, TT, :], g["x_sample"]).then_inc(x_in[TT], 16)
            for i, n in enumerate(("ln_mix_pre", "ln_mix_post", "ln_ffn_pre", "ln_ffn_post", "ln_ple_post")):
                sp.dma_start(k.gains[:, i, :], g[n].rearrange("a (c p) -> p (a c)", p=P),
                             allow_slow_non_contiguous=True).then_inc(const_in, 16)
            sp.wait_ge(const_in, 5 * 16)

        @block.scalar
        def _(act):
            act.dma_start(k.relb[0:32, :], g["rel_bias"]).then_inc(rel_in, 16)
            act.dma_start(far[:], g["rel_bias"][31:32, :].to_broadcast([32, H])).then_inc(rel_in, 16)
            for i in range(16):
                act.dma_start(pid1[8 * i:8 * i + 8, 0:B],
                              g["page_table"][:, i:i + 1].rearrange("b i -> i b").to_broadcast([8, B]),
                              allow_slow_non_contiguous=True).then_inc(pid_in, 16)
            act.dma_start(pid1[:, B:B + 1], g["sixteenth"]).then_inc(pid_in, 16)

        @block.gpsimd
        def _(pool):
            pool.wait_ge(pid_in, 17 * 16)
            nc.gpsimd.tensor_scalar(pid1[:, 0:B], pid1[:, 0:B], 8, None, ALU.mult).then_inc(pid_mul, 1)
            pool.wait_ge(pid_mul, 1)
            nc.gpsimd.tensor_tensor(k.pid[:], pid1[:, 0:B], pid1[:, B:B + 1].to_broadcast([P, B]),
                                    ALU.add).then_inc(pid_mul, 1)
            pool.wait_ge(pid_mul, 2)

        @block.tensor
        def _(pe):
            pe.wait_ge(eye_in, 16)
            for t in range(9):
                m = P if t < TT else B
                pe.wait_ge(x_in[t], 16)
                if t >= 4:
                    pe.wait_ge(copied, t - 3)
                for c in range(DC):
                    last = nc.tensor.transpose(ps[:, t % 4, c * P:c * P + m], xtok[0:m, t, c * P:(c + 1) * P],
                                               k.ident[0:m, 0:m])
                last.then_inc(transposed, 1)

        @block.vector
        def _(dve):
            nc.vector.memset(k.ones[:], 1.0 / D).then_inc(ones_set, 1)
            nc.vector.memset(k.relb[32:33, :], NEG).then_inc(ones_set, 1)
            for t in range(9):
                m = P if t < TT else B
                dve.wait_ge(transposed, t + 1)
                nc.vector.tensor_copy(k.X[:, :, t * P:t * P + m],
                                      ps[:, t % 4].rearrange("p (c t) -> p c t", c=DC)[:, :, 0:m]).then_inc(copied, 1)
            dve.wait_ge(rel_in, 32)
            nc.vector.tensor_tensor(k.relb[0:32, :], k.relb[0:32, :], far[:], ALU.subtract).then_inc(rel_sub, 1)
            dve.wait_ge(rel_sub, 1)
            dve.wait_ge(ones_set, 2)
            dve.wait_ge(copied, 9)


def norm_stage(k, name, src, residual, _, scaled):
    nc = k.nc
    with Stage(k, name) as st:
        ps = st.psum("ps", [P, NT, 512])
        squared, summed, mean, inverse, root, scaled_s, added = st.sems("squared summed mean inverse root scaled added")
        sq = chunks(k.E[:, 2 * N:4 * N], 2)
        ssq = k.E[:, N:2 * N]
        rstd = k.R1[:] if name == "norm1" else k.E[:, 0:N]
        block = st.block()

        @block.scalar
        def _(act):
            for c in range(DC):
                if c >= 2:
                    act.wait_ge(summed, c - 1)
                nc.scalar.activation(sq[:, c % 2, :], src[:, c, :], ACT.Square).then_inc(squared, 1)
            act.wait_ge(inverse, 2)
            nc.scalar.activation(rstd, rstd, ACT.Sqrt).then_inc(root, 1)

        @block.tensor
        def _(pe):
            pe.wait_ge(summed, DC)
            for n in range(NT):
                last = nc.tensor.matmul(ps[:, n, 0:NW], k.ones[:], ssq[:, n * NW:(n + 1) * NW], start=True, stop=True)
            last.then_inc(mean, 1)

        @block.vector
        def _(dve):
            for c in range(DC):
                dve.wait_ge(squared, c + 1)
                if c == 0:
                    nc.vector.tensor_copy(ssq, sq[:, 0, :]).then_inc(summed, 1)
                else:
                    dve.wait_ge(summed, c)
                    nc.vector.tensor_tensor(ssq, ssq, sq[:, c % 2, :], ALU.add).then_inc(summed, 1)
            dve.wait_ge(mean, 1)
            nc.vector.tensor_scalar(tokens(rstd), ps[:, :, 0:NW], EPS, None, ALU.add).then_inc(inverse, 1)
            dve.wait_ge(inverse, 1)
            nc.vector.reciprocal(rstd, rstd).then_inc(inverse, 1)
            dve.wait_ge(root, 1)
            for c in range(DC):
                if residual is None:
                    nc.vector.scalar_tensor_tensor(out=k.H[:, c, :], in0=src[:, c, :], scalar=k.gains[:, scaled, c:c + 1],
                                                   in1=rstd, op0=ALU.mult, op1=ALU.mult).then_inc(scaled_s, 1)
                else:
                    if c >= 2:
                        dve.wait_ge(added, c - 1)
                    nc.vector.scalar_tensor_tensor(out=sq[:, c % 2, :], in0=src[:, c, :], scalar=k.gains[:, residual, c:c + 1],
                                                   in1=rstd, op0=ALU.mult, op1=ALU.mult).then_inc(scaled_s, 1)
            dve.wait_ge(scaled_s, DC)

        @block.gpsimd
        def _(pool):
            if residual is not None:
                for c in range(DC):
                    pool.wait_ge(scaled_s, c + 1)
                    nc.gpsimd.tensor_tensor(k.X[:, c, :], k.X[:, c, :], sq[:, c % 2, :], ALU.add).then_inc(added, 1)
                pool.wait_ge(added, DC)


def apply_norm1(k):
    nc = k.nc
    with Stage(k, "norm1_again") as st:
        scaled, = st.sems("scaled")
        block = st.block()

        @block.vector
        def _(dve):
            for c in range(DC):
                nc.vector.scalar_tensor_tensor(out=k.H[:, c, :], in0=k.X[:, c, :], scalar=k.gains[:, 0, c:c + 1],
                                               in1=k.R1[:], op0=ALU.mult, op1=ALU.mult).then_inc(scaled, 1)
            dve.wait_ge(scaled, DC)


def weight(ap, at, cols=P):
    return ap[:, bass.ds(at, cols)].rearrange("(c p) m -> p c m", p=P)


def gemm_tile(k, acc, s, src, nk, m=P, k0=0):
    for c in range(nk):
        for n in range(NT):
            last = k.nc.tensor.matmul(acc[0:m, s, n, 0:NW], k.W[:, s, k0 + c, 0:m], src[:, c, n * NW:(n + 1) * NW],
                                      start=(c == 0), stop=(c == nk - 1))
    return last


def project_kv(k):
    nc, g, out, w = k.nc, k.g, k.out, k.g["w_in"]
    with Stage(k, "kv") as st:
        acc = st.psum("acc", [P, 2, NT, 512])
        tp = st.psum("tp", [P, 2, 512])
        mm_done, acc_free, evacuated, tr_done, tp_free, samples_copied, stores = st.sems(
            "mm_done acc_free evacuated tr_done tp_free samples_copied stores")
        tmp = chunks(k.E[:, 0:2 * N], 2)
        base = list(k.wcount)
        k.wcount[0] += 4 * 16
        k.wcount[1] += 3 * 16
        block = st.block()

        @block.sync
        def _(sp):
            with sp.Fori(0, 3) as i:
                for s in range(2):
                    sp.wait_ge(mm_done, 2 * i + s + 1)
                    sp.dma_start(k.W[:, s, 0:8, :], weight(w, KV0 + (2 * i + s) * P)).then_inc(k.wfull[s], 16)
            sp.wait_ge(mm_done, 7)
            sp.dma_start(k.W[:, 0, 0:8, 0:24], weight(w, GATE0, 24)).then_inc(k.wfull[0], 16)
            sp.wait_ge(tp_free, 2 + 18)
            for j, n in enumerate(("cmp_p", "slc_p")):
                sp.dma_start(out[n].rearrange("(t p) f -> p t f", p=P),
                             k.kvtok[:, 0:TT, 256 * j:256 * j + 256]).then_inc(stores, 16)
            sp.dma_start(out["win_p"].rearrange("(t p) f -> p t f", p=P), k.kvtok[:, 4:TT, 512:768]).then_inc(stores, 16)
            for j, n in enumerate(("cmp_s", "slc_s")):
                sp.dma_start(out[n], k.kvtok[0:B, TT, 256 * j:256 * j + 256]).then_inc(stores, 16)
            sp.dma_start(out["win_s"][:, 511, :], k.kvtok[0:B, TT, 512:768]).then_inc(stores, 16)
            sp.dma_start(out["win_s"][:, 0:511, :], g["state_win_kv"][:, 1:512, :]).then_inc(stores, 16)
            sp.wait_ge(stores, 7 * 16)

        def transposes(pe, b, m, first_bank, j):
            for q in range(3):
                bank = (first_bank + q) % 2
                pe.wait_ge(tp_free, j + q + 1)
                if q < 2:
                    for t in range(4):
                        last = nc.tensor.transpose(tp[:, bank, t * P:t * P + m],
                                                   tmp[0:m, b, (4 * q + t) * P:(4 * q + t + 1) * P], k.ident[0:m, 0:m])
                else:
                    last = nc.tensor.transpose(tp[0:B, bank, 0:m], tmp[0:m, b, T:N], k.ident[0:m, 0:m])
                last.then_inc(tr_done, 1)

        @block.tensor
        def _(pe):
            pe.sem_inc(mm_done, 2)
            pe.sem_inc(tr_done, 6)
            with pe.Fori(0, 3) as i:
                for s in range(2):
                    pe.wait_ge(k.wfull[s], 16 * i + base[s] + 16)
                    pe.wait_ge(acc_free, 2 * i + s + 1)
                    gemm_tile(k, acc, s, k.H, DC).then_inc(mm_done, 1)
                for s in range(2):
                    pe.wait_ge(evacuated, 2 * i + s + 1)
                    transposes(pe, s, P, s, 6 * i + 3 * s)
            pe.wait_ge(k.wfull[0], base[0] + 64)
            pe.wait_ge(acc_free, 7)
            gemm_tile(k, acc, 0, k.H, DC, 24).then_inc(mm_done, 1)
            pe.wait_ge(evacuated, 7)
            transposes(pe, 0, 24, 0, 18)

        @block.scalar
        def _(act):
            act.sem_inc(acc_free, 2)
            with act.Fori(0, 3) as i:
                for s in range(2):
                    act.wait_ge(mm_done, 2 * i + s + 3)
                    act.wait_ge(tr_done, 6 * i + 3 * s + 3)
                    nc.scalar.activation(tokens(tmp[:, s, :]), acc[:, s, :, 0:NW], ACT.Copy).then_inc(evacuated, 1)
                    if s == 0:
                        nc.scalar.activation(tokens(k.KT3[:, i, :]), acc[:, s, :, 0:NW], ACT.Copy).then_inc(acc_free, 1)
                    else:
                        act.wait_ge(evacuated, 2 * i + s + 1)
                        act.sem_inc(acc_free, 1)
            act.wait_ge(mm_done, 9)
            act.wait_ge(tr_done, 6 + 15)
            nc.scalar.activation(tokens(tmp[0:24, 0, :]), acc[0:24, 0, :, 0:NW], ACT.Sigmoid).then_inc(evacuated, 1)

        @block.vector
        def _(dve):
            dve.sem_inc(tp_free, 2)
            with dve.Fori(0, 3) as i:
                for s in range(2):
                    f = bass.ds((2 * i + s) * P, P)
                    for q in range(3):
                        dve.wait_ge(tr_done, 6 * i + 3 * s + q + 7)
                        if q < 2:
                            nc.vector.tensor_copy(k.kvtok[:, 4 * q:4 * q + 4, f],
                                                  tp[:, (s + q) % 2, :].rearrange("p (t f) -> p t f", t=4)).then_inc(tp_free, 1)
                        else:
                            nc.vector.tensor_copy(k.kvtok[0:B, TT, f], tp[0:B, (s + q) % 2, 0:P]).then_inc(tp_free, 1)
            for q in range(2):
                dve.wait_ge(tr_done, 18 + q + 7)
                nc.vector.tensor_copy(k.gtok[:, 4 * q:4 * q + 4, :],
                                      tp[:, q, :].rearrange("p (t f) -> p t f", t=4)[:, :, 0:24]).then_inc(tp_free, 1)
            dve.wait_ge(evacuated, 7)
            nc.vector.tensor_copy(k.gfm[:], tmp[0:24, 0, T:N]).then_inc(samples_copied, 1)
            dve.wait_ge(samples_copied, 1)
            dve.wait_ge(tp_free, 22)


def project_quv(k):
    nc, w = k.nc, k.g["w_in"]
    with Stage(k, "quv") as st:
        acc = st.psum("acc", [P, 2, NT, 512])
        tp = st.psum("tp", [P, 2, 512])
        mm_done, acc_free, tr_done, tp_free = st.sems("mm_done acc_free tr_done tp_free")
        tmp = chunks(k.ONr[:, 0:2 * N], 2)
        base = list(k.wcount)
        for s in range(2):
            k.wcount[s] += 2 * 32 + 4 * 16
        block = st.block()

        @block.sync
        def _(sp):
            with sp.Fori(0, 2) as i:
                for s in range(2):
                    sp.wait_ge(mm_done, 2 * i + s + 1)
                    for half in range(2):
                        sp.dma_start(k.W[:, s, 0:8, half * HD:(half + 1) * HD],
                                     weight(w, (2 * i + s) * HD + 4 * HD * half, HD)).then_inc(k.wfull[s], 16)
            with sp.Fori(0, 4) as i:
                for s in range(2):
                    sp.wait_ge(mm_done, 2 * i + s + 5)
                    sp.dma_start(k.W[:, s, 0:8, :], weight(w, U0 + (2 * i + s) * P)).then_inc(k.wfull[s], 16)

        @block.tensor
        def _(pe):
            pe.sem_inc(mm_done, 2)
            pe.sem_inc(tr_done, 6)
            with pe.Fori(0, 2) as i:
                for s in range(2):
                    pe.wait_ge(k.wfull[s], 32 * i + base[s] + 32)
                    pe.wait_ge(acc_free, 2 * i + s + 1)
                    gemm_tile(k, acc, s, k.H, DC).then_inc(mm_done, 1)
            with pe.Fori(0, 2) as i:
                for s in range(2):
                    pe.wait_ge(k.wfull[s], 16 * i + base[s] + 64 + 16)
                    pe.wait_ge(acc_free, 2 * i + s + 5)
                    gemm_tile(k, acc, s, k.H, DC).then_inc(mm_done, 1)
            with pe.Fori(0, 2) as i:
                for s in range(2):
                    pe.wait_ge(k.wfull[s], 16 * i + base[s] + 96 + 16)
                    pe.wait_ge(acc_free, 2 * i + s + 9)
                    gemm_tile(k, acc, s, k.H, DC).then_inc(mm_done, 1)
                for s in range(2):
                    pe.wait_ge(acc_free, 2 * i + s + 2 + 8 + 1)
                    for q in range(3):
                        bank = (s + q) % 2
                        pe.wait_ge(tp_free, 6 * i + 3 * s + q + 1)
                        if q < 2:
                            for t in range(4):
                                last = nc.tensor.transpose(tp[:, bank, t * P:(t + 1) * P],
                                                           tmp[:, s, (4 * q + t) * P:(4 * q + t + 1) * P], k.ident[:])
                        else:
                            last = nc.tensor.transpose(tp[0:B, bank, 0:P], tmp[:, s, T:N], k.ident[:])
                        last.then_inc(tr_done, 1)

        @block.scalar
        def _(act):
            act.sem_inc(acc_free, 2)
            with act.Fori(0, 2) as i:
                for s in range(2):
                    act.wait_ge(mm_done, 2 * i + s + 3)
                    nc.scalar.activation(tokens(k.Q[:, 2 * i + s, :]), acc[:, s, :, 0:NW], ACT.Copy,
                                         scale=HD ** -0.5).then_inc(acc_free, 1)
            with act.Fori(0, 2) as i:
                for s in range(2):
                    act.wait_ge(mm_done, 2 * i + s + 7)
                    nc.scalar.activation(tokens(k.OG[:, 2 * i + s, :]), acc[:, s, :, 0:NW],
                                         ACT.Gelu_apprx_tanh).then_inc(acc_free, 1)
            with act.Fori(0, 2) as i:
                for s in range(2):
                    act.wait_ge(mm_done, 2 * i + s + 11)
                    act.wait_ge(tr_done, 6 * i + 3 * s + 3)
                    nc.scalar.activation(tokens(tmp[:, s, :]), acc[:, s, :, 0:NW],
                                         ACT.Gelu_apprx_tanh).then_inc(acc_free, 1)

        @block.vector
        def _(dve):
            dve.sem_inc(tp_free, 2)
            with dve.Fori(0, 2) as i:
                for s in range(2):
                    f = bass.ds((2 * i + s) * P, P)
                    for q in range(3):
                        dve.wait_ge(tr_done, 6 * i + 3 * s + q + 7)
                        if q < 2:
                            nc.vector.tensor_copy(k.vtok[:, 4 * q:4 * q + 4, f],
                                                  tp[:, (s + q) % 2, :].rearrange("p (t f) -> p t f", t=4)).then_inc(tp_free, 1)
                        else:
                            nc.vector.tensor_copy(k.vtok[0:B, TT, f], tp[0:B, (s + q) % 2, 0:P]).then_inc(tp_free, 1)
            dve.wait_ge(tp_free, 14)


def spatial_gate(k):
    nc, g, out = k.nc, k.g, k.out
    NG = 4
    with Stage(k, "gm") as st:
        ps = st.psum("ps", [P, 2, 1024])
        wp = st.psum("wp", [P, 512])
        sp_ = st.psum("sp", [P, 512])
        const_in, w_turned, w_masked, stats, norm, v_ready, mixed, biased, mixed_free, smp_t, smp, stores = st.sems(
            "const_in w_turned w_masked stats norm v_ready mixed biased mixed_free smp_t smp stores")
        gb = k.Hr[:, 0:GM]
        bb = k.Hr[:, GM:2 * GM]
        wraw = k.Hr[:, 1024:1536].rearrange("p (g s) -> p g s", g=NG)
        wT = k.Hr[:, 1536:2048].rearrange("p (g s) -> p g s", g=NG)
        upper = k.Hr[:, 2048:2176]
        bs = k.Hr[:, 2176:2688].rearrange("p (g t) -> p g t", g=NG)
        mix = k.Hr[:, 2688:4736].rearrange("p (b t) -> p b t", b=2)
        bst = k.Hr[:, 4736:4736 + 54].rearrange("p (t s) -> p t s", s=6)
        mv = k.Hr[:, 4800:4818].rearrange("p (t s) -> p t s", s=2)
        rs = k.Hr[:, 4832:4841]
        w00 = k.Hr[:, 4848:4852]
        vs = k.Hr[:, 4864:4896].rearrange("p (g b) -> p g b", g=NG)
        block = st.block()

        @block.sync
        def _(sp):
            sp.dma_start(gb, g["gm_ln_g"].to_broadcast([P, GM])).then_inc(const_in, 16)
            sp.dma_start(bb, g["gm_ln_b"].to_broadcast([P, GM])).then_inc(const_in, 16)
            sp.dma_start(wraw, g["gm_ws"].rearrange("(g t) s -> t g s", g=NG)).then_inc(const_in, 16)
            sp.dma_start(upper, g["upper"]).then_inc(const_in, 16)
            sp.dma_start(bs, g["gm_bs"].rearrange("g t -> (g t)").unsqueeze(0).to_broadcast([P, 512])
                         .rearrange("p (g t) -> p g t", g=NG)).then_inc(const_in, 16)
            sp.dma_start(w00, g["gm_ws"].rearrange("(g t) s -> g t s", g=NG)[:, 0, 0].unsqueeze(0).to_broadcast([P, NG]),
                         allow_slow_non_contiguous=True).then_inc(const_in, 16)
            sp.wait_ge(v_ready, 1)
            sp.dma_start(out["gm_v"], k.vtok[0:B, TT, :]).then_inc(stores, 16)
            sp.wait_ge(stores, 16)

        @block.tensor
        def _(pe):
            pe.wait_ge(const_in, 96)
            for q in range(NG):
                last = nc.tensor.transpose(wp[:, q * P:(q + 1) * P], wraw[:, q, :], k.ident[:])
            last.then_inc(w_turned, 1)
            pe.wait_ge(w_masked, 1)
            pe.wait_ge(v_ready, 1)
            for q in range(NG):
                if q >= 2:
                    pe.wait_ge(mixed_free, q - 1)
                for t in range(TT):
                    last = nc.tensor.matmul(ps[:, q % 2, t * P:(t + 1) * P], k.vtok[:, t, q * P:(q + 1) * P], wT[:, q, :],
                                            start=True, stop=True)
                last.then_inc(mixed, 1)
            for q in range(NG):
                last = nc.tensor.transpose(sp_[:, q * B:(q + 1) * B], k.vtok[0:B, TT, q * P:(q + 1) * P], k.ident[0:B, 0:B])
            last.then_inc(smp_t, 1)

        @block.scalar
        def _(act):
            act.wait_ge(norm, 2)
            nc.scalar.activation(rs, rs, ACT.Sqrt).then_inc(norm, 1)

        @block.vector
        def _(dve):
            for t in range(9):
                m = P if t < TT else B
                nc.vector.bn_stats(bst[0:m, t, :], k.vtok[0:m, t, :]).then_inc(stats, 1)
            dve.wait_ge(stats, 9)
            nc.vector.memset(mv[:, TT, :], 1.0).then_inc(stats, 1)
            dve.wait_ge(stats, 10)
            for t in range(9):
                m = P if t < TT else B
                nc.vector.bn_aggr(mv[0:m, t, :], bst[0:m, t, :]).then_inc(stats, 1)
            dve.wait_ge(stats, 19)
            nc.vector.tensor_scalar(rs, mv[:, :, 1], EPS, None, ALU.add).then_inc(norm, 1)
            dve.wait_ge(norm, 1)
            nc.vector.reciprocal(rs, rs).then_inc(norm, 1)
            dve.wait_ge(const_in, 96)
            dve.wait_ge(w_turned, 1)
            nc.vector.tensor_tensor(wT, wp[:].rearrange("p (g t) -> p g t", g=NG),
                                    upper.unsqueeze(1).to_broadcast([P, NG, P]), ALU.mult).then_inc(w_masked, 1)
            dve.wait_ge(norm, 3)
            for t in range(9):
                m = P if t < TT else B
                nc.vector.tensor_scalar(k.vtok[0:m, t, :], k.vtok[0:m, t, :], mv[0:m, t, 0:1], rs[0:m, t:t + 1],
                                        ALU.subtract, ALU.mult).then_inc(stats, 1)
            dve.wait_ge(stats, 28)
            for a, b, m in ((0, TT, P), (TT, 9, B)):
                v = k.vtok[0:m, a:b, :]
                nc.vector.tensor_tensor(v, v, gb[0:m, :].unsqueeze(1).to_broadcast([m, b - a, GM]), ALU.mult).then_inc(stats, 1)
            dve.wait_ge(stats, 30)
            for a, b, m in ((0, TT, P), (TT, 9, B)):
                v = k.vtok[0:m, a:b, :]
                last = nc.vector.tensor_tensor(v, v, bb[0:m, :].unsqueeze(1).to_broadcast([m, b - a, GM]), ALU.add)
                last.then_inc(stats if a == 0 else v_ready, 1)
            dve.wait_ge(stats, 31)
            for q in range(NG):
                dve.wait_ge(mixed, q + 1)
                nc.vector.tensor_tensor(mix[:, q % 2, :].rearrange("p (c t) -> p c t", c=TT),
                                        ps[:, q % 2].rearrange("p (c t) -> p c t", c=TT),
                                        bs[:, q, :].unsqueeze(1).to_broadcast([P, TT, P]), ALU.add).then_inc(mixed_free, 1)
                dve.wait_ge(mixed_free, q + 1)
                nc.vector.tensor_tensor(k.OG[:, q, 0:T], k.OG[:, q, 0:T], mix[:, q % 2, :], ALU.mult).then_inc(biased, 1)
            dve.wait_ge(smp_t, 1)
            for q in range(NG):
                nc.vector.tensor_scalar(vs[:, q, :], sp_[:, q * B:(q + 1) * B], w00[:, q:q + 1], bs[:, q, 0:1],
                                        ALU.mult, ALU.add).then_inc(smp, 1)
            dve.wait_ge(smp, NG)
            nc.vector.tensor_tensor(k.OG[:, :, T:N], k.OG[:, :, T:N], vs, ALU.mult).then_inc(smp, 1)
            dve.wait_ge(smp, NG + 1)
            dve.wait_ge(biased, NG)


def compress(k):
    nc, g = k.nc, k.g
    with Stage(k, "cmp") as st:
        tp = st.psum("tp", [P, 4, 512])
        pre = st.psum("pre", [P, 2, 512])
        kv = st.psum("kv", [P, 2, 512])
        gathered = st.sems("gathered_0 gathered_1")
        prompt_in, regrouped_k, regrouped_v, w_in, w2_cleared, w2_placed, pe_done, pe_copied, tr_done, tp_copied, pre_done, silu_done, kv_done, kv_copied = st.sems(
            "prompt_in regrouped_k regrouped_v w_in w2_cleared w2_placed pe_done pe_copied tr_done tp_copied pre_done silu_done kv_done kv_copied")
        G = [k.Hr[:, 0:4096].rearrange("p (r f) -> p r f", r=16), k.ONr[:, 0:4096].rearrange("p (r f) -> p r f", r=16)]
        RG = [k.W[:].rearrange("p a c m -> p (a c m)")[:, 0:2048], k.E[:, 3584:5632]]
        TR = k.Hr[:, 4096:8192].rearrange("p (kv c g n) -> p kv c g n", kv=2, c=8, g=2)
        w1 = k.CW[:].rearrange("p (kv c m) -> p kv c m", kv=2, c=16)
        sh = k.E[:, 2304:2816].rearrange("p (kv g n) -> p kv g n", kv=2, g=2)
        w2k = k.E[:, 2816:3072].rearrange("p (g m) -> p g m", g=2)
        w2v = k.E[:, 3072:3136]
        pos = k.E[:, 3136:3168].rearrange("p (kv c) -> p kv c", kv=2)
        pe_b = k.tiny[:, 0:2]
        block = st.block()

        @block.gpsimd
        def _(pool):
            for b in range(B):
                pool.wait_ge(regrouped_k, b + 1)
                pool.wait_ge(regrouped_v, b + 1)
                pool.indirect_dma_start(
                    out=(k.Hr[:, 0:4096], k.ONr[:, 0:4096])[b % 2], out_offset=None, in_=g["cache_cmp_kv"],
                    in_offset=bass.IndirectOffsetOnAxis(ap=k.pid[:, b:b + 1], axis=0)).then_inc(gathered[b % 2], 16)

        @block.sync
        def _(sp):
            for i, n in enumerate("kv"):
                sp.dma_start(w1[:, i], g[f"cmp_w1_{n}"].rearrange("(c p) m -> p c m", p=P)).then_inc(w_in, 16)
                sp.dma_start(pos[:, i, :], g[f"cmp_pe_{n}"].rearrange("a (c p) -> p (a c)", p=P),
                             allow_slow_non_contiguous=True).then_inc(w_in, 16)
            sp.dma_start(w2v, g["cmp_w2_v"]).then_inc(w_in, 16)
            sp.wait_ge(w2_cleared, 1)
            for i in range(2):
                sp.dma_start(w2k[:, i, i * HD:(i + 1) * HD], g["cmp_w2_k"]).then_inc(w2_placed, 16)
            sp.wait_ge(regrouped_k, 2 + 7)
            sp.wait_ge(regrouped_v, 2 + 7)
            sp.dma_start(k.Hr[0:64, 0:4096], k.out["cmp_p"].rearrange("(n r) f -> n (r f)", r=16)).then_inc(prompt_in, 16)

        def turn(pe, b, n):
            for q in range(8):
                if q % 4 == 0:
                    pe.wait_ge((regrouped_k, regrouped_v)[q // 4], b + 3)
                pe.wait_ge(tp_copied, 8 * b + q + 1)
                for j in range(4):
                    f = (j % 2) * 1024 + (2 * (q % 4) + j // 2) * P
                    last = nc.tensor.transpose(tp[:, q % 4, j * P:j * P + n], RG[q // 4][0:n, f:f + P],
                                               k.ident[0:n, 0:n])
                last.then_inc(tr_done, 1)

        def hidden(pe, b, n):
            for i in range(2):
                pe.wait_ge(tp_copied, 8 * b + 4 * i + 8)
                pe.wait_ge(silu_done, 2 * b + i + 1)
                for c in range(16):
                    last = nc.tensor.matmul(pre[:, i, 0:2 * n].rearrange("p (g n) -> p g n", g=2), w1[:, i, c, :],
                                            TR[:, i, c % 8, :, c // 8:c // 8 + n], start=(c == 0), stop=(c == 15))
                last.then_inc(pre_done, 1)
            pe.wait_ge(silu_done, 2 * b + 4)
            pe.wait_ge(kv_copied, 2 * b + 1)
            for gr in range(2):
                last = nc.tensor.matmul(kv[:, 0, 0:n], w2k[:, gr, :], sh[:, 0, gr, 0:n], start=(gr == 0), stop=(gr == 1))
            last.then_inc(kv_done, 1)
            pe.wait_ge(kv_copied, 2 * b + 2)
            for gr in range(2):
                last = nc.tensor.matmul(kv[0:n, 1, gr * HD:(gr + 1) * HD], sh[:, 1, gr, 0:n], w2v, start=True, stop=True)
            last.then_inc(kv_done, 1)

        @block.tensor
        def _(pe):
            pe.sem_inc(tr_done, 16)
            pe.wait_ge(w_in, 80)
            for i in range(2):
                for c in range(16):
                    last = nc.tensor.matmul(pre[:, i, 0:1], w1[:, i, c, :], pos[:, i, c:c + 1], start=(c == 0), stop=(c == 15))
            last.then_inc(pe_done, 1)
            pe.wait_ge(pe_copied, 1)
            pe.wait_ge(w2_placed, 32)
            with pe.Fori(0, 4) as i:
                for s in range(2):
                    turn(pe, 2 * i + s, P)
                    hidden(pe, 2 * i + s, NCS)
            turn(pe, 8, 64)
            hidden(pe, 8, NCP)

        @block.scalar
        def _(act):
            act.sem_inc(silu_done, 2)
            act.sem_inc(kv_copied, 2)
            act.sem_inc(regrouped_k, 2)
            act.wait_ge(pe_copied, 1)

            def batch(s, b, rows_in, full, m, n, kc, vc):
                act.wait_ge(rows_in, full)
                act.wait_ge(tr_done, 8 * b + 12)
                nc.scalar.activation(RG[0][0:m].rearrange("p (g r d) -> p g r d", g=2, r=16),
                                     G[s][0:m, :, 0:P].rearrange("p r (g d) -> p g r d", g=2), ACT.Copy).then_inc(regrouped_k, 1)
                for i in range(2):
                    act.wait_ge(pre_done, 2 * b + i + 1)
                    act.wait_ge(kv_done, 2 * b + 2)
                    nc.scalar.activation(sh[:, i, :, 0:n], pre[:, i, 0:2 * n].rearrange("p (g n) -> p g n", g=2), ACT.Silu,
                                         bias=pe_b[:, i:i + 1]).then_inc(silu_done, 1)
                act.wait_ge(kv_done, 2 * b + 3)
                nc.scalar.activation(kc, kv[:, 0, 0:n], ACT.Copy).then_inc(kv_copied, 1)
                act.wait_ge(kv_done, 2 * b + 4)
                nc.scalar.activation(vc, kv[0:n, 1, 0:P], ACT.Copy).then_inc(kv_copied, 1)

            act.sem_inc(kv_done, 2)
            with act.Fori(0, 4) as i:
                for s in range(2):
                    b = 2 * i + s
                    batch(s, b, gathered[s], 16 * i + 16, P, NCS, k.KC[:, b, 0:NCS], k.VC[0:NCS, b, :])
            batch(0, 8, prompt_in, 16, 64, NCP, k.KC[:, 8, 0:NCP], k.VC[0:NCP, 8, :])
            act.wait_ge(kv_copied, 20)

        @block.vector
        def _(dve):
            dve.sem_inc(tp_copied, 4)
            dve.sem_inc(regrouped_v, 2)
            nc.vector.memset(w2k, 0.0).then_inc(w2_cleared, 1)
            dve.wait_ge(pe_done, 1)
            nc.vector.tensor_copy(pe_b, pre[:, :, 0]).then_inc(pe_copied, 1)

            def batch(s, b, rows_in, full, n):
                dve.wait_ge(rows_in, full)
                dve.wait_ge(tr_done, 8 * b + 16)
                nc.vector.tensor_copy(RG[1][0:n].rearrange("p (g r d) -> p g r d", g=2, r=16),
                                      G[s][0:n, :, P:2 * P].rearrange("p r (g d) -> p g r d", g=2)).then_inc(regrouped_v, 1)
                for q in range(8):
                    dve.wait_ge(tr_done, 8 * b + q + 17)
                    dve.wait_ge(silu_done, 2 * b + q // 4 + 1)
                    nc.vector.tensor_copy(TR[:, q // 4, 2 * (q % 4):2 * (q % 4) + 2, :, 0:n],
                                          tp[:, q % 4, :].rearrange("p (c g n) -> p c g n", c=2, g=2)[:, :, :, 0:n]).then_inc(tp_copied, 1)

            with dve.Fori(0, 4) as i:
                for s in range(2):
                    batch(s, 2 * i + s, gathered[s], 16 * i + 16, P)
            batch(0, 8, prompt_in, 16, 64)
            dve.wait_ge(tp_copied, 76)


def select_blocks(k):
    nc, g = k.nc, k.g
    R = B * H
    with Stage(k, "sel") as st:
        ps = st.psum("ps", [P, 8, 512])
        cleared, q_placed, const_in, scored, negated, exped, inverted, scaled, turned, turned_out, imp1, imp1_out, imp, imp_out, placed, out_c, ranked, row, mg, mg_out, bias_out, lg, qf = st.sems(
            "cleared q_placed const_in scored negated exped inverted scaled turned turned_out imp1 imp1_out imp imp_out placed "
            "out_c ranked row mg mg_out bias_out lg qf")
        at = [0]

        def room(words, rows=P):
            a = at[0]
            at[0] += words
            return k.Hr[0:rows, a:a + words]

        QS = room(576)
        relb64 = room(64, 33)
        oh = room(768, 33)
        LG = room(64, 24)
        head_of, branch_of = room(8, 24), room(4, 24)[:, 0:3]
        S = room(128, R)[:, 0:NCS]
        SG = room(128, R)[:, 0:NCS]
        PCT, PCG = room(64, NCS), room(64, NCS)
        OV = room(36, NCS)[:, 0:NSEL]
        G64 = room(64, R)
        IM = room(36, R)[:, 0:NSEL]
        SC = room(36, R)[:, 0:NSEL]
        before = room(NSEL * NSEL, R)
        C1, C2 = room(NSEL * NSEL, R), room(NSEL * NSEL, R)
        cnt = room(36, R)[:, 0:NSEL]
        row_ = room(36, R)
        nm, l, li = room(1, R), room(1, R), room(1, R)
        block = st.block()
        sq = "p (j i) -> p j i"

        @block.sync
        def _(sp):
            for dst, n in ((oh, "oh_samples"), (head_of, "head_of"), (branch_of, "branch_of"), (OV, "overlap"), (G64, "same_group")):
                sp.dma_start(dst, g[n]).then_inc(const_in, 16)
            sp.dma_start(before, g["before"].to_broadcast([R, NSEL * NSEL])).then_inc(const_in, 16)
            sp.dma_start(k.e8, g["eye"][0:B, 0:B].unsqueeze(0).to_broadcast([B, B, B])).then_inc(const_in, 16)

        @block.tensor
        def _(pe):
            pe.wait_ge(const_in, 112)
            pe.wait_ge(qf, 1)
            pe.wait_ge(lg, 2)
            for b in range(B):
                nc.tensor.matmul(ps[0:R, 0, 0:NCS], QS[:, b * R:(b + 1) * R], k.KC[:, b, 0:NCS], start=(b == 0), stop=False)
            nc.tensor.matmul(ps[0:R, 0, 0:NCS], relb64, oh[:, OH_CMP:OH_CMP + NCS], start=False, stop=True).then_inc(scored, 1)
            nc.tensor.matmul(ps[0:R, 1, 0:3], LG, branch_of, start=True, stop=True).then_inc(scored, 1)
            nc.tensor.matmul(ps[0:H, 2, 0:129], k.relb[:], oh[:, OH_SELF:OH_WIN], start=True, stop=True).then_inc(scored, 1)
            nc.tensor.matmul(ps[0:H, 3, :], k.relb[:], oh[:, OH_WIN:768], start=True, stop=True).then_inc(scored, 1)
            pe.wait_ge(scaled, 1)
            nc.tensor.transpose(ps[0:NCS, 4, 0:R], S, k.ident[0:R, 0:R]).then_inc(turned, 1)
            pe.wait_ge(scaled, 2)
            nc.tensor.transpose(ps[0:NCS, 5, 0:R], SG, k.ident[0:R, 0:R]).then_inc(turned, 1)
            pe.wait_ge(turned_out, 1)
            nc.tensor.matmul(ps[0:R, 6, 0:NSEL], PCT, OV, start=True, stop=True).then_inc(imp1, 1)
            pe.wait_ge(imp1_out, 1)
            nc.tensor.matmul(ps[0:R, 7, 0:NSEL], G64, IM, start=True, stop=True).then_inc(imp, 1)
            pe.wait_ge(turned_out, 2)
            for b in range(B):
                last = nc.tensor.matmul(ps[:, 4, b * H:(b + 1) * H], k.VC[0:NCS, b, :], PCG[:, b * H:(b + 1) * H],
                                        start=True, stop=True)
            last.then_inc(out_c, 1)
            pe.wait_ge(row, 2)
            for b in range(B):
                last = nc.tensor.matmul(ps[0:H, 5, b * 36:(b + 1) * 36], k.ident[0:R, b * H:(b + 1) * H], row_, start=True, stop=True)
            last.then_inc(mg, 1)

        @block.scalar
        def _(act):
            act.wait_ge(negated, 1)
            nc.scalar.activation(S, ps[0:R, 0, 0:NCS], ACT.Exp, bias=nm, accum_out=l).then_inc(exped, 1)

        @block.vector
        def _(dve):
            nc.vector.memset(QS, 0.0).then_inc(cleared, 1)
            nc.vector.memset(k.QS8, 0.0).then_inc(cleared, 1)
            nc.vector.tensor_copy(relb64.rearrange("p (b h) -> p b h", b=B), k.relb[:].unsqueeze(1).to_broadcast([33, B, H])).then_inc(lg, 1)
            dve.wait_ge(cleared, 2)
            for i in range(2):
                nc.vector.tensor_copy(k.QS8[i * HD:(i + 1) * HD, :, 4 * i:4 * i + 4],
                                      k.Q[i * HD:(i + 1) * HD, :, T:N].rearrange("p c b -> p b c")).then_inc(q_placed, 1)
            dve.wait_ge(q_placed, 2)
            nc.vector.tensor_copy(QS.rearrange("p (b x) -> p b x", b=B)[:, :, 0:H], k.QS8).then_inc(qf, 1)
            dve.wait_ge(const_in, 112)
            nc.vector.tensor_tensor(LG.rearrange("p (b h) -> p b h", b=B), k.gfm[:].unsqueeze(2).to_broadcast([24, B, H]),
                                    head_of.unsqueeze(1).to_broadcast([24, B, H]), ALU.mult).then_inc(lg, 1)
            dve.wait_ge(scored, 1)
            nc.vector.tensor_reduce(nm, ps[0:R, 0, 0:NCS], AX, ALU.max, negate=True).then_inc(negated, 1)
            dve.wait_ge(scored, 4)
            nc.vector.tensor_copy(row_[:, 33:36], ps[0:R, 1, 0:3]).then_inc(row, 1)
            nc.vector.tensor_copy(k.near_b, ps[0:H, 2, 0:129]).then_inc(bias_out, 1)
            nc.vector.tensor_copy(k.win_b, ps[0:H, 3, :]).then_inc(bias_out, 1)
            dve.wait_ge(exped, 1)
            nc.vector.reciprocal(li, l).then_inc(inverted, 1)
            dve.wait_ge(inverted, 1)
            nc.vector.tensor_scalar(S, S, li, None, ALU.mult).then_inc(scaled, 1)
            dve.wait_ge(scaled, 1)
            dve.wait_ge(row, 1)
            nc.vector.tensor_scalar(SG, S, row_[:, 33:34], None, ALU.mult).then_inc(scaled, 1)
            dve.wait_ge(turned, 1)
            nc.vector.tensor_copy(PCT, ps[0:NCS, 4, 0:R]).then_inc(turned_out, 1)
            dve.wait_ge(turned, 2)
            nc.vector.tensor_copy(PCG, ps[0:NCS, 5, 0:R]).then_inc(turned_out, 1)
            dve.wait_ge(imp1, 1)
            nc.vector.tensor_copy(IM, ps[0:R, 6, 0:NSEL]).then_inc(imp1_out, 1)
            dve.wait_ge(imp, 1)
            nc.vector.tensor_copy(SC, ps[0:R, 7, 0:NSEL]).then_inc(imp_out, 1)
            dve.wait_ge(imp_out, 1)
            nc.vector.memset(SC[:, 0:1], FORCE).then_inc(placed, 1)
            nc.vector.memset(SC[:, NSEL - 2:NSEL], FORCE).then_inc(placed, 1)
            dve.wait_ge(placed, 2)
            one = SC.unsqueeze(1).to_broadcast([R, NSEL, NSEL])
            other = SC.unsqueeze(2).to_broadcast([R, NSEL, NSEL])
            nc.vector.tensor_tensor(C1.rearrange(sq, j=NSEL), one, other, ALU.is_gt).then_inc(ranked, 1)
            nc.vector.tensor_tensor(C2.rearrange(sq, j=NSEL), one, other, ALU.is_equal).then_inc(ranked, 1)
            dve.wait_ge(ranked, 2)
            nc.vector.tensor_tensor(C2, C2, before, ALU.mult).then_inc(ranked, 1)
            dve.wait_ge(ranked, 3)
            nc.vector.tensor_tensor(C1, C1, C2, ALU.add).then_inc(ranked, 1)
            dve.wait_ge(ranked, 4)
            nc.vector.tensor_reduce(cnt, C1.rearrange(sq, j=NSEL), AX, ALU.add).then_inc(ranked, 1)
            dve.wait_ge(ranked, 5)
            nc.vector.tensor_scalar(row_[:, 0:NSEL], cnt, float(TOPK) - 0.5, NEG, ALU.is_ge, ALU.mult).then_inc(row, 1)
            dve.wait_ge(out_c, 1)
            nc.vector.tensor_copy(k.OC, ps[:, 4, 0:64].rearrange("p (b h) -> p b h", b=B)).then_inc(mg_out, 1)
            dve.wait_ge(mg, 1)
            nc.vector.tensor_copy(k.MG, ps[0:H, 5, 0:288].rearrange("p (b x) -> p b x", b=B)).then_inc(mg_out, 1)
            dve.wait_ge(mg_out, 2)
            dve.wait_ge(bias_out, 2)


def sample_attention(k):
    nc, g = k.nc, k.g
    with Stage(k, "smp") as st:
        tp = st.psum("tp", [P, 2, 512])
        sc = st.psum("sc", [P, 4, 512])
        wsc = st.psum("wsc", [P, 512])
        misc = st.psum("misc", [P, 512])
        gathered = st.sems("gathered_0 gathered_1")
        turn_now, win_in, tr_done, tp_copied, q_staged, scored, summed, negated, exped, inverted, scaled, diag, turned, turned_out, pv_done, o_done, near = st.sems(
            "turn_now win_in tr_done tp_copied q_staged scored summed negated exped inverted scaled diag turned turned_out pv_done o_done near")
        Gr = [k.Hr[:, 0:4096], k.Hr[:, 4096:8192]]
        G = [x.rearrange("p (r f) -> p r f", r=16) for x in Gr]
        kT = k.CW[:, 0:2560].rearrange("p (q n) -> p q n", q=5)
        GW = k.CW[:, 2560:3584].rearrange("p (r f) -> p r f", r=4)
        S, SW = k.E[0:H, 2304:2304 + 2049], k.E[0:H, 4368:4368 + 513]
        PT, MS, MD = k.E[:, 5456:5616], k.tiny[0:B, 0:16], k.small[0:H, 0:16]
        nm, l, cc = k.small[0:H, 16:18], k.small[0:H, 18:20], k.small[0:H, 20:22]
        QB = k.small[:, 24:32]
        vnew = [k.kvtok[0:B, TT, 384:512], k.kvtok[0:B, TT, 640:768]]
        block = st.block()

        @block.gpsimd
        def _(pool):
            for b in range(B):
                pool.wait_ge(pv_done, b + 1)
                pool.indirect_dma_start(
                    out=Gr[b % 2], out_offset=None, in_=g["cache_slc_kv"],
                    in_offset=bass.IndirectOffsetOnAxis(ap=k.pid[:, b:b + 1], axis=0)).then_inc(gathered[b % 2], 16)

        @block.sync
        def _(sp):
            with sp.Fori(0, 8) as b:
                sp.wait_ge(pv_done, b + 2)
                sp.dma_start(GW, g["state_win_kv"][bass.ds(b, 1), :, :].rearrange("b (n r) f -> n (b r) f", r=4)).then_inc(win_in, 16)

        @block.tensor
        def _(pe):
            pe.sem_inc(pv_done, 2)
            with pe.Fori(0, 4) as i:
                for s in range(2):
                    b = 2 * i + s
                    pe.wait_ge(gathered[s], 16 * i + 16)
                    for q in range(5):
                        if q == 4:
                            pe.wait_ge(win_in, 16 * b + 16)
                        pe.wait_ge(tp_copied, 5 * b + q + 1)
                        for j in range(4):
                            src = G[s][:, 4 * q + j, 0:P] if q < 4 else GW[:, j, 0:P]
                            last = nc.tensor.transpose(tp[:, (5 * s + q) % 2, j * P:(j + 1) * P], src, k.ident[:])
                        last.then_inc(tr_done, 1)
                    pe.wait_ge(tp_copied, 5 * b + 7)
                    pe.wait_ge(q_staged, b + 1)
                    pe.wait_ge(summed, b + 1)
                    pe.wait_ge(o_done, 2 * b + 2)
                    for q in range(4):
                        nc.tensor.matmul(sc[0:H, q, :], QB, kT[:, q, :], start=True, stop=True)
                    nc.tensor.matmul(wsc[0:H, :], QB, kT[:, 4, :], start=True, stop=True)
                    nc.tensor.matmul(misc[0:H, 0:2], QB, k.KT[:, :, bass.ds(b + T, 1)].rearrange("p a t -> p (a t)"),
                                     start=True, stop=True).then_inc(scored, 1)
                    pe.wait_ge(scaled, 2 * b + 2)
                    pe.wait_ge(diag, 2 * b + 2)
                    pe.sem_inc(turn_now, 1)
                    for r in range(16):
                        nc.tensor.transpose(misc[:, r * H:(r + 1) * H], S[:, r * P:(r + 1) * P], k.ident[0:H, 0:H])
                    for r in range(4):
                        nc.tensor.transpose(misc[:, P + r * H:P + (r + 1) * H], SW[:, r * P:(r + 1) * P], k.ident[0:H, 0:H])
                    for r in range(2):
                        last = nc.tensor.transpose(misc[0:B, 160 + r * B:160 + (r + 1) * B], MD[:, r * B:(r + 1) * B], k.ident[0:H, 0:H])
                    last.then_inc(turned, 1)
                    pe.wait_ge(turned_out, 2 * b + 2)
                    for r in range(16):
                        nc.tensor.matmul(misc[:, 256:264], G[s][:, r, P:2 * P], PT[:, r * H:(r + 1) * H], start=(r == 0), stop=False)
                    for r in range(4):
                        nc.tensor.matmul(misc[:, 256:264], GW[:, r, P:2 * P], PT[:, P + r * H:P + (r + 1) * H], start=False, stop=False)
                    for r in range(2):
                        last = nc.tensor.matmul(misc[:, 256:264], vnew[r], MS[:, r * H:(r + 1) * H], start=False, stop=(r == 1))
                    last.then_inc(pv_done, 1)

        @block.scalar
        def _(act):
            with act.Fori(0, 8) as b:
                act.wait_ge(negated, 2 * b + 1)
                nc.scalar.activation(S, S, ACT.Exp, bias=nm[:, 0:1], accum_out=l[:, 0:1]).then_inc(exped, 1)
                act.wait_ge(negated, 2 * b + 2)
                nc.scalar.activation(SW, SW, ACT.Exp, bias=nm[:, 1:2], accum_out=l[:, 1:2]).then_inc(exped, 1)

        @block.vector
        def _(dve):
            dve.sem_inc(tp_copied, 2)
            dve.sem_inc(summed, 1)
            dve.sem_inc(o_done, 2)
            dve.sem_inc(near, 1)
            with dve.Fori(0, 4) as i:
                for s in range(2):
                    b = 2 * i + s
                    nc.vector.tensor_copy(QB, k.QS8[:, b, :]).then_inc(q_staged, 1)
                    for q in range(5):
                        dve.wait_ge(tr_done, 5 * b + q + 1)
                        nc.vector.tensor_copy(kT[:, q, :], tp[:, (5 * s + q) % 2, :]).then_inc(tp_copied, 1)
                    dve.wait_ge(scored, b + 1)
                    nc.vector.tensor_tensor(S[:, 0:2048].rearrange("p (r j x) -> p r j x", r=16, x=4),
                                            sc[0:H].rearrange("p a (r j x) -> p (a r) j x", r=4, x=4),
                                            k.MG[:, b, 0:32].unsqueeze(2).unsqueeze(1).to_broadcast([H, 16, 32, 4]),
                                            ALU.add).then_inc(near, 1)
                    nc.vector.tensor_tensor(SW[:, 0:512], wsc[0:H, :], k.win_b, ALU.add).then_inc(near, 1)
                    nc.vector.tensor_scalar(S[:, 2048:2049], misc[0:H, 0:1], k.near_b[:, 0:1], None, ALU.add).then_inc(near, 1)
                    nc.vector.tensor_scalar(SW[:, 512:513], misc[0:H, 1:2], k.near_b[:, 0:1], None, ALU.add).then_inc(summed, 1)
                    dve.wait_ge(near, 4 * b + 4)
                    sn = S[:, 0:2048].rearrange("p (r n) -> p r n", r=16)[:, :, 120:128]
                    nc.vector.tensor_tensor(sn, sn, k.near_b[:, 1:129].rearrange("p (r n) -> p r n", r=16), ALU.add).then_inc(near, 1)
                    dve.wait_ge(near, 4 * b + 5)
                    dve.wait_ge(summed, b + 2)
                    nc.vector.tensor_reduce(nm[:, 0:1], S, AX, ALU.max, negate=True).then_inc(negated, 1)
                    nc.vector.tensor_reduce(nm[:, 1:2], SW, AX, ALU.max, negate=True).then_inc(negated, 1)
                    dve.wait_ge(exped, 2 * b + 2)
                    nc.vector.reciprocal(cc, l).then_inc(inverted, 1)
                    dve.wait_ge(inverted, 2 * b + 1)
                    nc.vector.tensor_tensor(cc, cc, k.MG[:, b, 34:36], ALU.mult).then_inc(inverted, 1)
                    dve.wait_ge(inverted, 2 * b + 2)
                    nc.vector.tensor_scalar(S, S, cc[:, 0:1], None, ALU.mult).then_inc(scaled, 1)
                    nc.vector.tensor_scalar(SW, SW, cc[:, 1:2], None, ALU.mult).then_inc(scaled, 1)
                    dve.wait_ge(scaled, 2 * b + 2)
                    nc.vector.tensor_scalar(MD[:, 0:B], k.e8[:, b, :], S[:, 2048:2049], None, ALU.mult).then_inc(diag, 1)
                    nc.vector.tensor_scalar(MD[:, B:2 * B], k.e8[:, b, :], SW[:, 512:513], None, ALU.mult).then_inc(diag, 1)
                    dve.wait_ge(turned, b + 1)
                    nc.vector.tensor_copy(PT, misc[:, 0:160]).then_inc(turned_out, 1)
                    nc.vector.tensor_copy(MS, misc[0:B, 160:176]).then_inc(turned_out, 1)
                    dve.wait_ge(pv_done, b + 3)
                    for gr in range(2):
                        h0 = slice(gr * HD, (gr + 1) * HD)
                        nc.vector.tensor_tensor(k.ON[h0, :, bass.ds(b + T, 1)].rearrange("p c t -> p (c t)"),
                                                misc[h0, 256 + 4 * gr:260 + 4 * gr], k.OC[h0, b, 4 * gr:4 * gr + 4],
                                                ALU.add).then_inc(o_done, 1)
            dve.wait_ge(o_done, 18)


def bias_tables(k):
    nc, g = k.nc, k.g
    with Stage(k, "bias") as st:
        ps = st.psum("ps", [P, 4, 512])
        pc = st.psum("pc", [P, 512])
        const_in, repeated, row_done, row_out, shifted, turned_in, cmp_done, cmp_set, cmp_out, gates = st.sems(
            "const_in repeated row_done row_out shifted turned_in cmp_done cmp_set cmp_out gates")
        RB = k.Hr[0:33, 0:1024].rearrange("p (h m) -> p h m", h=H)
        ohn = k.Hr[0:33, 1024:1408]
        TB = k.Hr[:, 1408:4480].rearrange("p (h x) -> p h x", h=H)
        ohc = k.Hr[0:33, 4480:6400]
        hb = k.tiny[:, 0:1]
        block = st.block()

        @block.sync
        def _(sp):
            sp.dma_start(ohn, g["oh_near"]).then_inc(const_in, 16)
            sp.dma_start(ohc, g["oh_cmp"]).then_inc(const_in, 16)
            sp.dma_start(k.WM, g["window_edge"]).then_inc(const_in, 16)
            sp.dma_start(hb, g["has_block"]).then_inc(const_in, 16)
            sp.wait_ge(row_out, H)
            sp.dma_start(k.scratch.rearrange("h (i x) -> i h x", i=P), TB).then_inc(shifted, 16)
            sp.wait_ge(shifted, 16)
            sp.dma_start(k.NB, k.scratch[:, 127:127 + P * 383].rearrange("h (i w) -> i h w", w=383)[:, :, 0:256]).then_inc(turned_in, 16)
            sp.wait_ge(turned_in, 16)

        @block.tensor
        def _(pe):
            pe.wait_ge(const_in, 64)
            for m in range(15):
                last = nc.tensor.matmul(pc[:, m * H:(m + 1) * H], ohc[:, m * P:(m + 1) * P], k.relb[:], start=True, stop=True)
            last.then_inc(cmp_done, 1)
            pe.wait_ge(repeated, 1)
            for h in range(H):
                if h >= 4:
                    pe.wait_ge(row_out, h - 3)
                nc.tensor.matmul(ps[:, h % 4, 0:384], RB[:, h, :], ohn, start=True, stop=True).then_inc(row_done, 1)

        @block.scalar
        def _(act):
            for h in range(H):
                act.wait_ge(row_done, h + 1)
                nc.scalar.activation(TB[:, h, :], ps[:, h % 4, 0:384], ACT.Copy).then_inc(row_out, 1)

        @block.vector
        def _(dve):
            nc.vector.tensor_copy(RB, k.relb[:].unsqueeze(2).to_broadcast([33, H, P])).then_inc(repeated, 1)
            nc.vector.memset(k.BC[:, :, 0:48], 0.0).then_inc(cmp_set, 1)
            nc.vector.memset(k.BC[:, :, 63:119], NEG).then_inc(cmp_set, 1)
            dve.wait_ge(cmp_done, 1)
            nc.vector.tensor_copy(k.BC[:, :, 48:63], pc[:, 0:120].rearrange("p (m h) -> p h m", h=H)).then_inc(cmp_set, 1)
            dve.wait_ge(const_in, 64)
            g0 = k.gtok[:, 0, :].rearrange("p (h r) -> p h r", r=3)[:, :, 0]
            nc.vector.tensor_scalar(g0, g0, hb, None, ALU.mult).then_inc(gates, 1)
            dve.wait_ge(gates, 1)
            dve.wait_ge(cmp_set, 3)


def prompt_attention(k):
    nc = k.nc
    with Stage(k, "att") as st:
        sS = st.psum("slc", [P, 1024])
        sW = st.psum("win", [P, 1024])
        tp = st.psum("tp", [P, 2, 512])
        op = st.psum("op", [P, 512])
        q_ready, scored_s, scored_w, exp_s, exp_w, exp_c, biased, negated, factor, p_ready, pt_done, pt_copied, pv_done, o_copied, turn_cmp = st.sems(
            "q_ready scored_s scored_w exp_s exp_w exp_c biased negated factor p_ready pt_done pt_copied pv_done o_copied turn_cmp")
        PR = [k.Hr[:, 0:1728], k.Hr[:, 1728:3456]]
        PT = [k.Hr[:, 3456:5248], k.Hr[:, 5248:7040]]
        QB = k.Hr[:, 7040:7168]
        nm = [k.Hr[:, 7168:7171], k.Hr[:, 7176:7179]]
        l = [k.Hr[:, 7184:7187], k.Hr[:, 7192:7195]]
        cc = [k.Hr[:, 7200:7203], k.Hr[:, 7208:7211]]
        CMP = 640
        plan, groups = [], 0
        for t in range(TT):
            wb = list(range(max(0, t - 4), t + 1))
            ng = -(-(t + 1 + len(wb)) // 4) + 1
            plan.append((t, wb, ng, groups))
            groups += 8 * ng
        block = st.block()

        @block.tensor
        def _(pe):
            pe.sem_inc(scored_w, 1)
            pe.sem_inc(pv_done, 2)
            for t, wb, ng, g0 in plan:
                with pe.Fori(0, 4) as c:
                    for gr in range(2):
                        s = 2 * c + gr + 8 * t
                        rows = slice(gr * HD, (gr + 1) * HD)
                        if gr == 0:
                            pe.wait_ge(q_ready, c + 4 * t + 1)
                        pe.wait_ge(exp_s, s + 1)
                        w = (t + 1) * P
                        for a in range(0, w, 512):
                            e = min(w, a + 512)
                            last = nc.tensor.matmul(sS[:, a:e], QB[rows, :], k.KT[rows, 0, a:e], start=True, stop=True)
                        last.then_inc(scored_s, 1)
                        pe.wait_ge(exp_w, s + 1)
                        pe.wait_ge(exp_c, s + 1)
                        w = len(wb) * P
                        for a in range(0, w, 512):
                            e = min(w, a + 512)
                            nc.tensor.matmul(sW[:, a:e], QB[rows, :], k.KT[rows, 1, wb[0] * P + a:wb[0] * P + e], start=True, stop=True)
                        nc.tensor.matmul(sW[:, CMP:CMP + NCP], QB[rows, :], k.KC[rows, 8, 0:NCP], start=True, stop=True).then_inc(scored_w, 1)
                    for gr in range(2):
                        s = 2 * c + gr + 8 * t
                        pe.wait_ge(p_ready, 3 * s + 3)
                        cols = [P * j for j in range(t + 1)] + [1024 + P * j for j in range(len(wb))]
                        for q in range(ng):
                            pe.wait_ge(pt_copied, (2 * c + gr) * ng + (g0 + q + 1))
                            bank = (gr * ng + q) % 2
                            if q < ng - 1:
                                for j, a in enumerate(cols[4 * q:4 * q + 4]):
                                    last = nc.tensor.transpose(tp[:, bank, j * P:(j + 1) * P], PR[gr][:, a:a + P], k.ident[:])
                            else:
                                pe.sem_inc(turn_cmp, 1)
                                last = nc.tensor.transpose(tp[0:NCP, bank, 0:P], PR[gr][:, 1664:1664 + NCP], k.ident[:])
                            last.then_inc(pt_done, 1)
                        pe.wait_ge(pt_copied, (2 * c + gr + 1) * ng + g0 + 2)
                        if gr == 0:
                            pe.wait_ge(o_copied, c + 4 * t + 1)
                        o = op[gr * HD:(gr + 1) * HD, 0:P]
                        kv = [(b, 384) for b in range(t + 1)] + [(b, 640) for b in wb]
                        for j, (b, f) in enumerate(kv):
                            nc.tensor.matmul(o, k.kvtok[:, b, f + gr * HD:f + (gr + 1) * HD], PT[gr][:, j * P:(j + 1) * P],
                                             start=(j == 0), stop=False)
                        nc.tensor.matmul(o, k.VC[0:NCP, 8, gr * HD:(gr + 1) * HD], PT[gr][0:NCP, len(kv) * P:(len(kv) + 1) * P],
                                         start=False, stop=True).then_inc(pv_done, 1)

        @block.scalar
        def _(act):
            for x in (exp_s, exp_w, exp_c, o_copied):
                act.sem_inc(x, 1)
            act.sem_inc(pt_copied, 2)
            for t, wb, ng, g0 in plan:
                nb = t + 1 + len(wb)
                with act.Fori(0, 4) as c:
                    for gr in range(2):
                        s = 2 * c + gr + 8 * t
                        act.wait_ge(pv_done, s + 1)
                        for j, (done, src, dst) in enumerate((
                                (exp_s, sS[:, 0:(t + 1) * P], PR[gr][:, 0:(t + 1) * P]),
                                (exp_w, sW[:, 0:len(wb) * P], PR[gr][:, 1024:1024 + len(wb) * P]),
                                (exp_c, sW[:, CMP:CMP + NCP], PR[gr][:, 1664:1664 + NCP]))):
                            act.wait_ge(negated, 3 * s + (1, 3, 3)[j])
                            nc.scalar.activation(dst, src, ACT.Exp, bias=nm[gr][:, j:j + 1],
                                                 accum_out=l[gr][:, (j + 1) % 3:(j + 1) % 3 + 1]).then_inc(done, 1)
                    for gr in range(2):
                        for q in range(ng):
                            act.wait_ge(pt_done, (2 * c + gr) * ng + (g0 + q + 1))
                            bank = (gr * ng + q) % 2
                            if q < ng - 1:
                                m = min(4, nb - 4 * q) * P
                                nc.scalar.activation(PT[gr][:, 512 * q:512 * q + m], tp[:, bank, 0:m], ACT.Copy).then_inc(pt_copied, 1)
                            else:
                                nc.scalar.activation(PT[gr][0:NCP, nb * P:(nb + 1) * P], tp[0:NCP, bank, 0:P], ACT.Copy).then_inc(pt_copied, 1)
                    act.wait_ge(pv_done, 2 * c + 8 * t + 4)
                    nc.scalar.activation(k.ON[:, bass.ds(c, 1), t * P:(t + 1) * P].rearrange("p a t -> p (a t)"), op[:, 0:P],
                                         ACT.Copy).then_inc(o_copied, 1)

        @block.vector
        def _(dve):
            for t, wb, ng, g0 in plan:
                with dve.Fori(0, 4) as c:
                    dve.wait_ge(scored_w, 2 * c + 8 * t + 1)
                    nc.vector.tensor_copy(QB, k.Q[:, bass.ds(c, 1), t * P:(t + 1) * P].rearrange("p a t -> p (a t)")).then_inc(q_ready, 1)
                    near = min(t + 1, 2) * P
                    adds = 3 + (len(wb) == 5)
                    a0 = sum(8 * (3 + (x >= 4)) for x in range(t))
                    for gr in range(2):
                        s = 2 * c + gr + 8 * t
                        ab = (2 * c + gr) * adds + a0
                        hd = bass.ds(c + 4 * gr, 1)
                        nb = k.NB[:, hd, 256 - near:256].rearrange("p a j -> p (a j)")
                        dve.wait_ge(scored_s, s + 1)
                        x = sS[:, (t + 1) * P - near:(t + 1) * P]
                        nc.vector.tensor_tensor(x, x, nb, ALU.add).then_inc(biased, 1)
                        dve.wait_ge(biased, ab + 1)
                        nc.vector.tensor_reduce(nm[gr][:, 0:1], sS[:, 0:(t + 1) * P], AX, ALU.max, negate=True).then_inc(negated, 1)
                        dve.wait_ge(scored_w, s + 2)
                        w = len(wb) * P
                        x = sW[:, w - near:w]
                        nc.vector.tensor_tensor(x, x, nb, ALU.add).then_inc(biased, 1)
                        if len(wb) == 5:
                            nc.vector.tensor_tensor(sW[:, 0:P], sW[:, 0:P], k.WM, ALU.add).then_inc(biased, 1)
                        x = sW[:, CMP:CMP + NCP]
                        a = 56 - 8 * t
                        nc.vector.tensor_tensor(x, x, k.BC[:, hd, a:a + NCP].rearrange("p a m -> p (a m)"), ALU.add).then_inc(biased, 1)
                        dve.wait_ge(biased, ab + adds)
                        nc.vector.tensor_reduce(nm[gr][:, 1:2], sW[:, 0:w], AX, ALU.max, negate=True).then_inc(negated, 1)
                        nc.vector.tensor_reduce(nm[gr][:, 2:3], x, AX, ALU.max, negate=True).then_inc(negated, 1)
                    for gr in range(2):
                        s = 2 * c + gr + 8 * t
                        for done in (exp_s, exp_w, exp_c):
                            dve.wait_ge(done, s + 2)
                        nc.vector.reciprocal(cc[gr], l[gr]).then_inc(factor, 1)
                        dve.wait_ge(factor, 2 * s + 1)
                        gates = k.gtok[:, t, :].rearrange("p (h r) -> p h r", r=3)[:, bass.ds(c + 4 * gr, 1), :]
                        nc.vector.tensor_tensor(cc[gr], cc[gr], gates.rearrange("p a r -> p (a r)"), ALU.mult).then_inc(factor, 1)
                        dve.wait_ge(factor, 2 * s + 2)
                        for j, (a, w) in enumerate(((0, (t + 1) * P), (1024, len(wb) * P), (1664, NCP))):
                            x = PR[gr][:, a:a + w]
                            f = (j + 1) % 3
                            nc.vector.tensor_scalar(x, x, cc[gr][:, f:f + 1], None, ALU.mult).then_inc(p_ready, 1)


def merge(k):
    nc, g, w = k.nc, k.g, k.g["w_in"]
    with Stage(k, "merge") as st:
        acc = st.psum("acc", [P, 2, NT, 512])
        mm = st.sems("gates_done branch_done")
        sig, gated, merged, slot_open = st.sems("sig gated merged slot_open")
        SA = chunks(k.E[:, 0:2 * N], 2)
        TM = chunks(k.E[:, 2 * N:4 * N], 2)
        base = list(k.wcount)
        k.wcount[0] += 8 * 32
        k.wcount[1] += 8 * 48
        nsa = g["w_branch_nsa"].rearrange("(gr c d) m -> gr d c m", gr=2, d=HD)
        block = st.block()

        @block.sync
        def _(sp):
            with sp.Fori(0, 8) as m:
                for j in range(2):
                    sp.wait_ge(mm[0], 2 * m + j + 1)
                    sp.dma_start(k.W[:, 0, 0:8, :], weight(w, m * P + (GA0, GB0)[j])).then_inc(k.wfull[0], 16)
                    sp.wait_ge(mm[1], 2 * m + j + 1)
                    sp.sem_inc(slot_open, 1)
                    if j == 0:
                        for gr in range(2):
                            sp.dma_start(k.W[gr * HD:(gr + 1) * HD, 1, 0:4, :], nsa[gr][:, :, bass.ds(m * P, P)]).then_inc(k.wfull[1], 16)
                    else:
                        sp.dma_start(k.W[:, 1, 0:4, :], weight(g["w_branch_gm"], m * P)).then_inc(k.wfull[1], 16)

        @block.tensor
        def _(pe):
            pe.sem_inc(mm[0], 1)
            pe.sem_inc(mm[1], 1)
            with pe.Fori(0, 8) as m:
                for j in range(2):
                    pe.wait_ge(k.wfull[0], 32 * m + base[0] + 16 * j + 16)
                    pe.wait_ge(sig, 2 * m + j + 1)
                    gemm_tile(k, acc, 0, k.H, DC).then_inc(mm[0], 1)
                    pe.wait_ge(k.wfull[1], 48 * m + base[1] + (32, 48)[j])
                    pe.wait_ge(gated, 2 * m + j + 2)
                    gemm_tile(k, acc, 1, (k.ON, k.OG)[j], 4).then_inc(mm[1], 1)

        @block.scalar
        def _(act):
            act.sem_inc(sig, 1)
            with act.Fori(0, 8) as m:
                for j in range(2):
                    act.wait_ge(mm[0], 2 * m + j + 2)
                    act.wait_ge(gated, 2 * m + j + 1)
                    nc.scalar.activation(tokens(SA[:, j, :]), acc[:, 0, :, 0:NW], ACT.Sigmoid).then_inc(sig, 1)

        @block.vector
        def _(dve):
            dve.sem_inc(gated, 2)
            dve.sem_inc(merged, 1)
            with dve.Fori(0, 8) as m:
                dve.wait_ge(merged, m + 1)
                for j in range(2):
                    dve.wait_ge(sig, 2 * m + j + 2)
                    dve.wait_ge(mm[1], 2 * m + j + 2)
                    nc.vector.tensor_tensor(tokens(TM[:, j, :]), tokens(SA[:, j, :]), acc[:, 1, :, 0:NW], ALU.mult).then_inc(gated, 1)
                dve.wait_ge(gated, 2 * m + 4)
                nc.vector.tensor_tensor(k.MT[:, bass.ds(m, 1), :].rearrange("p a t -> p (a t)"), TM[:, 0, :], TM[:, 1, :],
                                        ALU.add).then_inc(merged, 1)
            dve.wait_ge(merged, 9)


def one(ap, m):
    return tokens(ap[:, bass.ds(m, 1), :].rearrange("p a t -> p (a t)"))


def out_projection(k):
    nc, g = k.nc, k.g
    with Stage(k, "out") as st:
        acc = st.psum("acc", [P, 2, NT, 512])
        mm_done, acc_free = st.sems("mm_done acc_free")
        base = list(k.wcount)
        for s in range(2):
            k.wcount[s] += 4 * 16
        block = st.block()

        @block.sync
        def _(sp):
            with sp.Fori(0, 4) as i:
                for s in range(2):
                    sp.wait_ge(mm_done, 2 * i + s + 1)
                    sp.dma_start(k.W[:, s, 0:8, :], weight(g["w_out"], (2 * i + s) * P)).then_inc(k.wfull[s], 16)

        @block.tensor
        def _(pe):
            pe.sem_inc(mm_done, 2)
            with pe.Fori(0, 4) as i:
                for s in range(2):
                    pe.wait_ge(k.wfull[s], 16 * i + base[s] + 16)
                    pe.wait_ge(acc_free, 2 * i + s + 1)
                    gemm_tile(k, acc, s, k.MT, DC).then_inc(mm_done, 1)

        @block.scalar
        def _(act):
            act.sem_inc(acc_free, 2)
            with act.Fori(0, 4) as i:
                for s in range(2):
                    act.wait_ge(mm_done, 2 * i + s + 3)
                    nc.scalar.activation(one(k.MX, 2 * i + s), acc[:, s, :, 0:NW], ACT.Copy).then_inc(acc_free, 1)
            act.wait_ge(acc_free, 10)


def ffn(k, half):
    nc, g = k.nc, k.g
    with Stage(k, f"ffn{half}") as st:
        acc = st.psum("acc", [P, 2, NT, 512])
        gate_done, up_done, silu_done, gated, down_done, acc_free = st.sems(
            "gate_done up_done silu_done gated down_done acc_free")
        done = (gate_done, up_done)
        free = (silu_done, gated)
        SL = k.E[:, 0:N]
        base = list(k.wcount)
        for s in range(2):
            k.wcount[s] += (FH + 4) * 16
        at = half * FH * P
        block = st.block()

        @block.sync
        def _(sp):
            with sp.Fori(0, FH) as m:
                for s in range(2):
                    sp.wait_ge(done[s], m + 1)
                    sp.dma_start(k.W[:, s, 0:8, :], weight(g[("w_ffn_gate", "w_ffn_up")[s]], m * P + at)).then_inc(k.wfull[s], 16)
            for s in range(2):
                sp.wait_ge(done[s], FH + 1)
            with sp.Fori(0, 4) as i:
                for s in range(2):
                    sp.wait_ge(down_done, 2 * i + s + 1)
                    sp.dma_start(k.W[:, s, :, :], weight(g["w_ffn_down"][at:at + FH * P, :], (2 * i + s) * P)).then_inc(k.wfull[s], 16)

        @block.tensor
        def _(pe):
            pe.sem_inc(gate_done, 1)
            pe.sem_inc(up_done, 1)
            pe.sem_inc(down_done, 2)
            with pe.Fori(0, FH) as m:
                for s in range(2):
                    pe.wait_ge(k.wfull[s], 16 * m + base[s] + 16)
                    pe.wait_ge(free[s], m + 1)
                    gemm_tile(k, acc, s, k.H, DC).then_inc(done[s], 1)
            for s in range(2):
                pe.wait_ge(free[s], FH + 1)
            with pe.Fori(0, 4) as i:
                for s in range(2):
                    pe.wait_ge(k.wfull[s], 16 * i + base[s] + FH * 16 + 16)
                    pe.wait_ge(acc_free, 2 * i + s + 1)
                    gemm_tile(k, acc, s, k.A, FH).then_inc(down_done, 1)

        @block.scalar
        def _(act):
            act.sem_inc(silu_done, 1)
            with act.Fori(0, FH) as m:
                act.wait_ge(gate_done, m + 2)
                act.wait_ge(gated, m + 1)
                nc.scalar.activation(tokens(SL), acc[:, 0, :, 0:NW], ACT.Silu).then_inc(silu_done, 1)
            if half == 0:
                act.sem_inc(acc_free, 2)
                with act.Fori(0, 4) as i:
                    for s in range(2):
                        act.wait_ge(down_done, 2 * i + s + 3)
                        nc.scalar.activation(one(k.F, 2 * i + s), acc[:, s, :, 0:NW], ACT.Copy).then_inc(acc_free, 1)
                act.wait_ge(acc_free, 10)

        @block.vector
        def _(dve):
            dve.sem_inc(gated, 1)
            with dve.Fori(0, FH) as m:
                dve.wait_ge(silu_done, m + 2)
                dve.wait_ge(up_done, m + 2)
                nc.vector.tensor_tensor(one(k.A, m), tokens(SL), acc[:, 1, :, 0:NW], ALU.mult).then_inc(gated, 1)
            if half == 1:
                dve.sem_inc(acc_free, 2)
                with dve.Fori(0, 4) as i:
                    for s in range(2):
                        dve.wait_ge(down_done, 2 * i + s + 3)
                        nc.vector.tensor_tensor(one(k.F, 2 * i + s), one(k.F, 2 * i + s), acc[:, s, :, 0:NW],
                                                ALU.add).then_inc(acc_free, 1)
                dve.wait_ge(acc_free, 10)


def ple(k):
    nc, g = k.nc, k.g
    with Stage(k, "ple") as st:
        acc = st.psum("acc", [P, 2, NT, 512])
        tp = st.psum("tp", [P, 2, 512])
        p_in, tr_done, tr_copied, gate_done, e_done, sig, gated = st.sems("p_in tr_done tr_copied gate_done e_done sig gated")
        done, free = (gate_done, e_done), (sig, gated)
        ptok = k.Z[:, 0:9 * 256].rearrange("p (t f) -> p t f", f=256)
        pT = chunks(k.Z[:, 2304:2304 + 2 * N], 2)
        SA = k.E[:, 0:N]
        base = list(k.wcount)
        for s in range(2):
            k.wcount[s] += 8 * 16
        block = st.block()

        @block.sync
        def _(sp):
            sp.dma_start(ptok[:, 0:TT, :], g["p_prompt"].rearrange("(t p) f -> p t f", p=P)).then_inc(p_in, 16)
            sp.dma_start(ptok[0:B, TT, :], g["p_sample"]).then_inc(p_in, 16)
            with sp.Fori(0, 8) as m:
                sp.wait_ge(gate_done, m + 1)
                sp.dma_start(k.W[:, 0, 0:8, :], weight(g["w_ple_gate"], m * P)).then_inc(k.wfull[0], 16)
                sp.wait_ge(e_done, m + 1)
                sp.dma_start(k.W[:, 1, 0:2, :], weight(g["w_ple"], m * P)).then_inc(k.wfull[1], 16)

        @block.tensor
        def _(pe):
            pe.sem_inc(gate_done, 1)
            pe.sem_inc(e_done, 1)
            pe.wait_ge(p_in, 32)
            for c in range(2):
                for q in range(3):
                    n = 3 * c + q
                    if n >= 2:
                        pe.wait_ge(tr_copied, n - 1)
                    if q < 2:
                        for t in range(4):
                            last = nc.tensor.transpose(tp[:, n % 2, t * P:(t + 1) * P], ptok[:, 4 * q + t, c * P:(c + 1) * P], k.ident[:])
                    else:
                        last = nc.tensor.transpose(tp[:, n % 2, 0:B], ptok[0:B, TT, c * P:(c + 1) * P], k.ident[0:B, 0:B])
                    last.then_inc(tr_done, 1)
            pe.wait_ge(tr_copied, 6)
            with pe.Fori(0, 8) as m:
                for s in range(2):
                    pe.wait_ge(k.wfull[s], 16 * m + base[s] + 16)
                    pe.wait_ge(free[s], m + 1)
                    gemm_tile(k, acc, s, (k.X, pT)[s], (8, 2)[s]).then_inc(done[s], 1)

        @block.scalar
        def _(act):
            act.sem_inc(sig, 1)
            with act.Fori(0, 8) as m:
                act.wait_ge(gate_done, m + 2)
                act.wait_ge(gated, m + 1)
                nc.scalar.activation(tokens(SA), acc[:, 0, :, 0:NW], ACT.Sigmoid).then_inc(sig, 1)

        @block.vector
        def _(dve):
            dve.sem_inc(gated, 1)
            for c in range(2):
                for q in range(3):
                    n = 3 * c + q
                    dve.wait_ge(tr_done, n + 1)
                    a, w = (q * 512, 512) if q < 2 else (T, B)
                    nc.vector.tensor_copy(pT[:, c, a:a + w], tp[:, n % 2, 0:w]).then_inc(tr_copied, 1)
            with dve.Fori(0, 8) as m:
                dve.wait_ge(sig, m + 2)
                dve.wait_ge(e_done, m + 2)
                nc.vector.tensor_tensor(one(k.F, m), tokens(SA), acc[:, 1, :, 0:NW], ALU.mult).then_inc(gated, 1)
            dve.wait_ge(gated, 9)


def store_y(k):
    nc = k.nc
    with Stage(k, "store") as st:
        ps = st.psum("ps", [P, 4, 1024])
        turned, copied, stores = st.sems("turned copied stores")
        yt = k.Z[:, 0:9 * D].rearrange("p (t f) -> p t f", f=D)
        block = st.block()

        @block.tensor
        def _(pe):
            for t in range(9):
                m = P if t < TT else B
                if t >= 4:
                    pe.wait_ge(copied, t - 3)
                for c in range(DC):
                    last = nc.tensor.transpose(ps[0:m, t % 4, c * P:(c + 1) * P], k.X[:, c, t * P:t * P + m], k.ident[:])
                last.then_inc(turned, 1)

        @block.vector
        def _(dve):
            for t in range(9):
                m = P if t < TT else B
                dve.wait_ge(turned, t + 1)
                nc.vector.tensor_copy(yt[0:m, t, :], ps[0:m, t % 4, :]).then_inc(copied, 1)

        @block.sync
        def _(sp):
            for t in range(9):
                sp.wait_ge(copied, t + 1)
                if t < TT:
                    sp.dma_start(k.out["y_p"][t * P:(t + 1) * P, :], yt[:, t, :]).then_inc(stores, 16)
                else:
                    sp.dma_start(k.out["y_s"], yt[0:B, TT, :]).then_inc(stores, 16)
            sp.wait_ge(stores, 9 * 16)


def _bucket(dist):
    import numpy as np
    dist = np.asarray(dist)
    near = np.maximum(dist, 0)
    ratio = np.log(np.maximum(near, 1).astype(np.float32) / np.float32(16)) / np.float32(np.log(128 / 16))
    large = np.minimum(16 + (ratio * 16).astype(np.int32), 31)
    return np.where(dist < 0, 32, np.where(near < 16, near, large))


def _one_hot(dist):
    import numpy as np
    b = _bucket(dist)
    return np.ascontiguousarray((np.arange(33).reshape((33,) + (1,) * b.ndim) == b[None]).astype(np.float32))


def _constants():
    import numpy as np
    f = np.float32
    i, j = np.arange(128)[:, None], np.arange(128)[None, :]
    n33 = np.arange(33)
    row = np.arange(64)
    kk = np.arange(24)
    ci, sj = np.arange(127)[:, None] * 16, n33[None, :] * 64
    r, n = np.arange(16)[:, None], np.arange(120, 128)[None, :]
    wr, wn = np.arange(4)[:, None], np.arange(128)[None, :]
    smp = np.concatenate([2048 - (16 * np.arange(127) + 31), [0], (2048 - 16 * n - r).ravel(), (512 - 4 * wn - wr).ravel()])
    m = np.arange(48, 63)
    return {
        "eye": np.eye(128, dtype=f),
        "sixteenth": (np.arange(128) % 8).astype(np.int32)[:, None],
        "upper": (i <= j).astype(f),
        "oh_samples": _one_hot(smp),
        "oh_near": _one_hot(255 - np.arange(384)),
        "oh_cmp": _one_hot(np.arange(128)[None, :] - 16 * (m[:, None] - 56) - 31).reshape(33, 15 * 128),
        "overlap": ((ci <= sj + 63) & (ci + 31 >= sj)).astype(f),
        "same_group": (row[:, None] // 4 == row[None, :] // 4).astype(f),
        "before": (n33[None, :] < n33[:, None]).astype(f).reshape(1, 33 * 33),
        "head_of": (kk[:, None] // 3 == np.arange(8)[None, :]).astype(f),
        "branch_of": (kk[:, None] % 3 == np.arange(3)[None, :]).astype(f),
        "window_edge": np.where(j >= i, 0, -1e30).astype(f),
        "has_block": (np.arange(128) >= 31).astype(f)[:, None],
    }


_VIEWS = {
    "x_prompt": (1024, 1024), "x_sample": (8, 1024), "cache_cmp_kv": (160 * 8, 4096), "cache_slc_kv": (160 * 8, 4096),
    "state_win_kv": (8, 512, 256), "page_table": (8, 16), "p_prompt": (1024, 256), "p_sample": (8, 256),
    "rel_bias": (32, 8), "ln_mix_pre": (1, 1024), "w_in": (1024, 4376), "cmp_pe_k": (1, 2048), "cmp_w1_k": (2048, 128),
    "cmp_w2_k": (128, 64), "cmp_pe_v": (1, 2048), "cmp_w1_v": (2048, 128), "cmp_w2_v": (128, 64), "gm_ln_g": (1, 512),
    "gm_ln_b": (1, 512), "gm_ws": (512, 128), "gm_bs": (4, 128), "w_branch_nsa": (512, 1024), "w_branch_gm": (512, 1024),
    "w_out": (1024, 1024), "ln_mix_post": (1, 1024), "ln_ffn_pre": (1, 1024), "w_ffn_gate": (1024, 2816),
    "w_ffn_up": (1024, 2816), "w_ffn_down": (2816, 1024), "ln_ffn_post": (1, 1024), "w_ple": (256, 1024),
    "w_ple_gate": (1024, 1024), "ln_ple_post": (1, 1024),
}
_OUTS = [
    ("y_p", (1024, 1024), (1, 1024, 1024)), ("y_s", (8, 1024), (8, 1, 1024)),
    ("cmp_p", (1024, 256), (1, 1, 1024, 2, 2, 64)), ("slc_p", (1024, 256), (1, 1, 1024, 2, 2, 64)),
    ("win_p", (512, 256), (1, 1, 512, 2, 2, 64)), ("cmp_s", (8, 256), (1, 8, 1, 2, 2, 64)),
    ("slc_s", (8, 256), (1, 8, 1, 2, 2, 64)), ("win_s", (8, 512, 256), (1, 8, 512, 2, 2, 64)),
    ("gm_v", (8, 512), (1, 8, 1, 512)),
]


def kernel(**inputs):
    import numpy as _np
    import concourse.bacc as _bacc
    from concourse import mybir as _mybir
    from concourse.bass_utils import run_bass_kernel_spmd as _run

    nc = _bacc.Bacc("TRN2", target_bir_lowering=False, num_devices=1)
    arrays, g, out = {}, {}, {}
    data = {n: _np.ascontiguousarray(inputs[n]).reshape(s) for n, s in _VIEWS.items()}
    data.update(_constants())
    for n, a in data.items():
        arrays[f"in_{n}"] = a
        g[n] = nc.dram_tensor(f"in_{n}", a.shape, _mybir.dt.from_np(a.dtype), kind="ExternalInput").ap()
    for n, shape, _ in _OUTS:
        out[n] = nc.dram_tensor(f"out_{n}", shape, _mybir.dt.float32, kind="ExternalOutput").ap()
    scratch = nc.dram_tensor("bias_rows", (8, 128 * 384), _mybir.dt.float32, kind="Internal").ap()
    build(nc, g, out, scratch)
    r = _run(nc, [arrays], core_ids=[0])
    return tuple(_np.asarray(r.results[0][f"out_{n}"]).reshape(full) for n, _, full in _OUTS)
```

```python
from contextlib import ExitStack

import concourse.bass as bass
from concourse import mybir

F32 = mybir.dt.float32
F32R = mybir.dt.float32r
I32 = mybir.dt.int32
ALU = mybir.AluOpType
ACT = mybir.ActivationFunctionType
AX = mybir.AxisListType.X

P = 128
D = 1024
T = 1024
B = 8
N = T + B
NT = 3
NW = N // NT
DC = D // P
TT = T // P
FFN_PARTS = (6, 6, 5, 5)
FP = max(FFN_PARTS)
KV = 768
H = 8
HD = 64
NCP = 63
NCS = 127
NSEL = 33
TOPK = 16
EPS = 1e-6
NEG = -1e30
FORCE = 1e6
Q0, KV0, GATE0, U0, V0, GA0, GB0 = 0, 512, 1280, 1304, 1816, 2328, 3352
GM = 512
OH_CMP, OH_SELF, OH_NEAR, OH_WIN = 0, 127, 128, 256


def tokens(ap):
    return ap.rearrange("p (n w) -> p n w", n=NT)


def chunks(ap, n):
    return ap.rearrange("p (c t) -> p c t", c=n)


class Core:
    pass


class Stage:

    def __init__(self, k, name):
        self.k, self.name, self.stack, self.mine = k, name, ExitStack(), []

    def __enter__(self):
        self.stack.__enter__()
        return self

    def sems(self, names):
        new = [self.k.nc.alloc_semaphore(f"{self.name}_{n}") for n in names.split()]
        self.mine += new
        return new

    def psum(self, what, shape):
        return self.stack.enter_context(self.k.nc.psum_tensor(f"{self.name}_{what}", shape, F32))

    def block(self):
        return self.stack.enter_context(self.k.nc.Block())

    def __exit__(self, *a):
        self.stack.__exit__(*a)
        self.k.used += self.mine


def build(nc, g, out, scratch, kept):
    with ExitStack() as ctx:
        k = Core()
        k.nc, k.g, k.out, k.scratch, k.kept = nc, g, out, scratch, kept

        def sb(name, shape, dt=F32):
            return ctx.enter_context(nc.sbuf_tensor(name, shape, dt))

        base = -(-nc.sbuf_base // 32) * 32
        sizes = {"X": DC * N, "H": DC * N, "Z": 21360, "W": 2048, "CW": 4096}
        sb("slab", [P, sum(sizes.values()) + 8])
        start, at = {}, base
        for n, words in sizes.items():
            start[n] = at
            at += 4 * words

        def place(name, region, shape, dt=F32, skip=0):
            return nc.alloc_sbuf_tensor_at(name, shape, dt, offset=start[region] + 4 * skip)

        k.X = place("X", "X", [P, DC, N])
        k.HL = place("HL", "X", [P, DC, N], F32R)
        k.Hr = place("Hr", "H", [P, DC * N])
        k.HH = place("HH", "H", [P, DC, N], F32R)
        k.Z = place("Z", "Z", [P, 21360])
        k.AH = place("AH", "Z", [P, FP, N], F32R)
        k.AL = place("AL", "Z", [P, FP, N], F32R, FP * N)
        k.XL = place("XL", "Z", [P, DC, N], F32R)
        k.W = place("W", "W", [P, 2, DC, P])
        k.CW = place("CW", "CW", [P, 4096])
        k.WS = place("WS", "CW", [P, 2, 2, DC, P], F32R)
        k.E = sb("E", [P, 5632])
        k.R1 = sb("R1", [P, N])
        k.ident = sb("ident", [P, P])
        k.ones = sb("ones", [P, P])
        k.gains = sb("gains", [P, 5, DC])
        k.gtok = sb("gtok", [P, TT, 24])
        k.gfm = sb("gfm", [24, B])
        k.pid = sb("pid", [P, B], I32)
        k.relb = sb("relb", [33, H])
        k.tiny = sb("tiny", [P, 16])
        k.kvtok = k.Z[:, 0:9 * KV].rearrange("p (t f) -> p t f", f=KV)
        o = 9 * KV
        k.Q = chunks(k.Z[:, o:o + 4 * N], 4)
        k.KT3 = chunks(k.Z[:, o + 3 * N:o + 6 * N], 3)
        o += 4 * N
        k.KT = chunks(k.Z[:, o:o + 2 * N], 2)
        o += 2 * N
        k.OG = chunks(k.Z[:, o:o + 4 * N], 4)
        o += 4 * N
        k.ON = chunks(k.Z[:, o:o + 4 * N], 4)
        k.ONr = k.Z[:, o:o + 4 * N]
        k.MT = chunks(k.Z[:, 0:8 * N], 8)
        k.MX = chunks(k.Z[:, 8 * N:16 * N], 8)
        k.MTX = k.MT
        k.F = chunks(k.Z[:, 2 * FP * N:(2 * FP + 8) * N], 8)
        k.wfull = [ctx.enter_context(nc.semaphore(f"weights_full_{i}")) for i in range(2)]
        k.wcount = [0, 0]
        k.vtok = k.E[:, 0:9 * GM].rearrange("p (t f) -> p t f", f=GM)
        k.KC = k.E[:, 0:9 * P].rearrange("p (b n) -> p b n", b=9)
        k.VC = k.E[:, 9 * P:18 * P].rearrange("p (b n) -> p b n", b=9)
        k.small = sb("small", [P, 32])
        k.QS8 = k.Hr[:, 8192:8256].rearrange("p (b h) -> p b h", b=B)
        k.MG = k.E[0:H, 4888:5176].rearrange("p (b x) -> p b x", b=B)
        k.OC = k.E[:, 5176:5240].rearrange("p (b h) -> p b h", b=B)
        k.near_b = k.E[0:H, 5240:5369]
        k.e8 = k.E[0:B, 5376:5440].rearrange("p (a b) -> p a b", a=B)
        k.NB = k.E[:, 2304:4352].rearrange("p (h j) -> p h j", h=H)
        k.BC = k.E[:, 4352:5304].rearrange("p (h m) -> p h m", h=H)
        k.WM = k.E[:, 5304:5432]
        k.win_b = k.CW[0:H, 3584:4096]
        k.used = []
        load_x(k)
        norm_stage(k, "norm1", k.X, scaled=0, spill=True)
        project_kv(k)
        project_quv(k)
        spatial_gate(k)
        compress(k)
        select_blocks(k)
        sample_attention(k)
        bias_tables(k)
        prompt_attention(k)
        nc.clear_and_free_semaphores(k.used)
        nc.all_engine_barrier()
        k.used = []
        norm_stage(k, "norm1_again", k.X, scaled=0, known=True)
        merge(k)
        out_projection(k)
        norm_stage(k, "mix_post", k.MX, residual=1, onto=k.MT)
        norm_stage(k, "ffn_pre", k.X, scaled=2, spill=True)
        for part in range(len(FFN_PARTS)):
            ffn(k, part)
        norm_stage(k, "ffn_post", k.F, residual=3, onto=k.X)
        ple(k)
        norm_stage(k, "ple_post", k.F, residual=4, onto=k.X)
        store_y(k)


def load_x(k):
    nc, g = k.nc, k.g
    with Stage(k, "load") as st:
        xtok = k.Z[:, 0:9 * D].rearrange("p (t f) -> p t f", f=D)
        ps = st.psum("ps", [P, 4, 1024])
        x_in = st.sems(" ".join(f"x_in_{t}" for t in range(9)))
        eye_in, const_in, ones_set, transposed, copied, rel_in, rel_sub, pid_in, pid_mul = st.sems(
            "eye_in const_in ones_set transposed copied rel_in rel_sub pid_in pid_mul")
        pid1 = st.stack.enter_context(nc.sbuf_tensor("pid1", [P, B + 1], I32))
        far = st.stack.enter_context(nc.sbuf_tensor("far", [32, H], F32))
        block = st.block()

        @block.sync
        def _(sp):
            sp.dma_start(k.ident[:], g["eye"]).then_inc(eye_in, 16)
            for t in range(TT):
                sp.dma_start(xtok[:, t, :], g["x_prompt"][t * P:(t + 1) * P, :]).then_inc(x_in[t], 16)
            sp.dma_start(xtok[0:B, TT, :], g["x_sample"]).then_inc(x_in[TT], 16)
            for i, n in enumerate(("ln_mix_pre", "ln_mix_post", "ln_ffn_pre", "ln_ffn_post", "ln_ple_post")):
                sp.dma_start(k.gains[:, i, :], g[n].rearrange("a (c p) -> p (a c)", p=P),
                             allow_slow_non_contiguous=True).then_inc(const_in, 16)
            sp.wait_ge(const_in, 5 * 16)

        @block.scalar
        def _(act):
            act.dma_start(k.relb[0:32, :], g["rel_bias"]).then_inc(rel_in, 16)
            act.dma_start(far[:], g["rel_bias"][31:32, :].to_broadcast([32, H])).then_inc(rel_in, 16)
            for i in range(16):
                act.dma_start(pid1[8 * i:8 * i + 8, 0:B],
                              g["page_table"][:, i:i + 1].rearrange("b i -> i b").to_broadcast([8, B]),
                              allow_slow_non_contiguous=True).then_inc(pid_in, 16)
            act.dma_start(pid1[:, B:B + 1], g["sixteenth"]).then_inc(pid_in, 16)

        @block.gpsimd
        def _(pool):
            pool.wait_ge(pid_in, 17 * 16)
            nc.gpsimd.tensor_scalar(pid1[:, 0:B], pid1[:, 0:B], 8, None, ALU.mult).then_inc(pid_mul, 1)
            pool.wait_ge(pid_mul, 1)
            nc.gpsimd.tensor_tensor(k.pid[:], pid1[:, 0:B], pid1[:, B:B + 1].to_broadcast([P, B]),
                                    ALU.add).then_inc(pid_mul, 1)
            pool.wait_ge(pid_mul, 2)

        @block.tensor
        def _(pe):
            pe.wait_ge(eye_in, 16)
            for t in range(9):
                m = P if t < TT else B
                pe.wait_ge(x_in[t], 16)
                if t >= 4:
                    pe.wait_ge(copied, t - 3)
                for c in range(DC):
                    last = nc.tensor.transpose(ps[:, t % 4, c * P:c * P + m], xtok[0:m, t, c * P:(c + 1) * P],
                                               k.ident[0:m, 0:m])
                last.then_inc(transposed, 1)

        @block.vector
        def _(dve):
            nc.vector.memset(k.ones[:], 1.0 / D).then_inc(ones_set, 1)
            nc.vector.memset(k.relb[32:33, :], NEG).then_inc(ones_set, 1)
            for t in range(9):
                m = P if t < TT else B
                dve.wait_ge(transposed, t + 1)
                nc.vector.tensor_copy(k.X[:, :, t * P:t * P + m],
                                      ps[:, t % 4].rearrange("p (c t) -> p c t", c=DC)[:, :, 0:m]).then_inc(copied, 1)
            dve.wait_ge(rel_in, 32)
            nc.vector.tensor_tensor(k.relb[0:32, :], k.relb[0:32, :], far[:], ALU.subtract).then_inc(rel_sub, 1)
            dve.wait_ge(rel_sub, 1)
            dve.wait_ge(ones_set, 2)
            dve.wait_ge(copied, 9)


def norm_stage(k, name, src, residual=None, onto=None, scaled=None, spill=False, known=False):
    nc = k.nc
    with Stage(k, name) as st:
        ps = st.psum("ps", [P, NT, 512])
        squared, summed, mean, inverse, root, scaled_s, hi_done, lo_done, added, spilled = st.sems(
            "squared summed mean inverse root scaled hi_done lo_done added spilled")
        sq = chunks(k.E[:, 2 * N:4 * N], 2)
        ssq = k.E[:, N:2 * N]
        rstd = k.R1[:] if name.startswith("norm1") else k.E[:, 0:N]
        block = st.block()

        @block.sync
        def _(sp):
            if spill:
                sp.dma_start(k.kept, k.X[:].rearrange("p c t -> p (c t)")).then_inc(spilled, 16)
                sp.wait_ge(spilled, 16)

        @block.scalar
        def _(act):
            if not known:
                for c in range(DC):
                    if c >= 2:
                        act.wait_ge(summed, c - 1)
                    nc.scalar.activation(sq[:, c % 2, :], src[:, c, :], ACT.Square).then_inc(squared, 1)
                act.wait_ge(inverse, 2)
                nc.scalar.activation(rstd, rstd, ACT.Sqrt).then_inc(root, 1)
            if scaled is not None:
                for c in range(DC):
                    act.wait_ge(scaled_s, c + 1)
                    nc.scalar.activation(k.HH[:, c, :], sq[:, c % 2, :], ACT.Copy).then_inc(hi_done, 1)

        @block.tensor
        def _(pe):
            if not known:
                pe.wait_ge(summed, DC)
                for n in range(NT):
                    last = nc.tensor.matmul(ps[:, n, 0:NW], k.ones[:], ssq[:, n * NW:(n + 1) * NW], start=True, stop=True)
                last.then_inc(mean, 1)

        @block.vector
        def _(dve):
            if not known:
                for c in range(DC):
                    dve.wait_ge(squared, c + 1)
                    if c == 0:
                        nc.vector.tensor_copy(ssq, sq[:, 0, :]).then_inc(summed, 1)
                    else:
                        dve.wait_ge(summed, c)
                        nc.vector.tensor_tensor(ssq, ssq, sq[:, c % 2, :], ALU.add).then_inc(summed, 1)
                dve.wait_ge(mean, 1)
                nc.vector.tensor_scalar(tokens(rstd), ps[:, :, 0:NW], EPS, None, ALU.add).then_inc(inverse, 1)
                dve.wait_ge(inverse, 1)
                nc.vector.reciprocal(rstd, rstd).then_inc(inverse, 1)
                dve.wait_ge(root, 1)
            if spill:
                dve.wait_ge(spilled, 16)
            gain = k.gains[:, scaled if residual is None else residual, :]

            def scale(c):
                nc.vector.scalar_tensor_tensor(out=sq[:, c % 2, :], in0=src[:, c, :], scalar=gain[:, c:c + 1],
                                               in1=rstd, op0=ALU.mult, op1=ALU.mult).then_inc(scaled_s, 1)

            if residual is None:
                scale(0)
                for c in range(DC):
                    if c + 1 < DC:
                        if c >= 1:
                            dve.wait_ge(lo_done, c)
                        scale(c + 1)
                    dve.wait_ge(hi_done, c + 1)
                    nc.vector.tensor_tensor(k.HL[:, c, :], sq[:, c % 2, :], k.HH[:, c, :].bitcast(F32),
                                            ALU.subtract).then_inc(lo_done, 1)
                dve.wait_ge(lo_done, DC)
            else:
                for c in range(DC):
                    if c >= 2:
                        dve.wait_ge(added, c - 1)
                    scale(c)
                dve.wait_ge(scaled_s, DC)

        @block.gpsimd
        def _(pool):
            if residual is not None:
                for c in range(DC):
                    pool.wait_ge(scaled_s, c + 1)
                    nc.gpsimd.tensor_tensor(k.X[:, c, :], onto[:, c, :], sq[:, c % 2, :], ALU.add).then_inc(added, 1)
                pool.wait_ge(added, DC)


def weight(ap, at, cols=P):
    return ap[:, bass.ds(at, cols)].rearrange("(c p) m -> p c m", p=P)


def gemm_tile(k, acc, s, src, nk):
    for c in range(nk):
        for n in range(NT):
            last = k.nc.tensor.matmul(acc[:, s, n, 0:NW], k.W[:, s, c, :], src[:, c, n * NW:(n + 1) * NW],
                                      start=(c == 0), stop=(c == nk - 1))
    return last


def split_tile(k, acc, s, ws, hi, lo, nk):
    for c in range(nk):
        for part, src in ((0, hi), (0, lo), (1, hi)):
            for n in range(NT):
                last = k.nc.tensor.matmul(acc[:, s, n, 0:NW], k.WS[:, ws, part, c, :], src[:, c, n * NW:(n + 1) * NW],
                                          start=(c == 0 and part == 0 and src is hi), stop=(c == nk - 1 and part == 1))
    return last


def split_weights(k, pool, s, ws, nk, hi_done, count, split_done):
    w = k.W[:, s, 0:nk, :]
    k.nc.gpsimd.tensor_copy(k.WS[:, ws, 0, 0:nk, :], w).then_inc(hi_done, 1)
    pool.wait_ge(hi_done, count + 1)
    k.nc.gpsimd.tensor_tensor(k.WS[:, ws, 1, 0:nk, :], w, k.WS[:, ws, 0, 0:nk, :].bitcast(F32),
                              ALU.subtract).then_inc(split_done, 1)


def project_kv(k):
    nc, g, out, w = k.nc, k.g, k.out, k.g["w_in"]
    with Stage(k, "kv") as st:
        acc = st.psum("acc", [P, 2, NT, 512])
        tp = st.psum("tp", [P, 2, 512])
        mm_done, acc_free, evacuated, tr_done, tp_free, samples_copied, stores, hi_done, split_done, slot_ok = st.sems(
            "mm_done acc_free evacuated tr_done tp_free samples_copied stores hi_done split_done slot_ok")
        tmp = chunks(k.E[:, 0:2 * N], 2)
        base = list(k.wcount)
        k.wcount[0] += 4 * 16
        k.wcount[1] += 3 * 16
        block = st.block()

        @block.sync
        def _(sp):
            with sp.Fori(0, 3) as i:
                for s in range(2):
                    sp.wait_ge(split_done, 2 * i + s + 1)
                    sp.dma_start(k.W[:, s, 0:8, :], weight(w, KV0 + (2 * i + s) * P)).then_inc(k.wfull[s], 16)
            sp.wait_ge(split_done, 7)
            sp.dma_start(k.W[:, 0, 0:8, :], weight(w, GATE0)).then_inc(k.wfull[0], 16)
            sp.wait_ge(tp_free, 2 + 18)
            for j, n in enumerate(("cmp_p", "slc_p")):
                sp.dma_start(out[n].rearrange("(t p) f -> p t f", p=P),
                             k.kvtok[:, 0:TT, 256 * j:256 * j + 256]).then_inc(stores, 16)
            sp.dma_start(out["win_p"].rearrange("(t p) f -> p t f", p=P), k.kvtok[:, 4:TT, 512:768]).then_inc(stores, 16)
            for j, n in enumerate(("cmp_s", "slc_s")):
                sp.dma_start(out[n], k.kvtok[0:B, TT, 256 * j:256 * j + 256]).then_inc(stores, 16)
            sp.dma_start(out["win_s"][:, 511, :], k.kvtok[0:B, TT, 512:768]).then_inc(stores, 16)
            sp.dma_start(out["win_s"][:, 0:511, :], g["state_win_kv"][:, 1:512, :]).then_inc(stores, 16)
            sp.wait_ge(stores, 7 * 16)

        def transposes(pe, b, m, first_bank, j):
            for q in range(3):
                bank = (first_bank + q) % 2
                pe.wait_ge(tp_free, j + q + 1)
                if q < 2:
                    for t in range(4):
                        last = nc.tensor.transpose(tp[:, bank, t * P:t * P + m],
                                                   tmp[0:m, b, (4 * q + t) * P:(4 * q + t + 1) * P], k.ident[0:m, 0:m])
                else:
                    last = nc.tensor.transpose(tp[0:B, bank, 0:m], tmp[0:m, b, T:N], k.ident[0:m, 0:m])
                last.then_inc(tr_done, 1)

        @block.tensor
        def _(pe):
            pe.sem_inc(mm_done, 2)
            pe.sem_inc(tr_done, 6)
            with pe.Fori(0, 3) as i:
                for s in range(2):
                    pe.wait_ge(split_done, 2 * i + s + 3)
                    pe.wait_ge(acc_free, 2 * i + s + 1)
                    split_tile(k, acc, s, s, k.HH, k.HL, DC).then_inc(mm_done, 1)
                for s in range(2):
                    pe.wait_ge(evacuated, 2 * i + s + 1)
                    transposes(pe, s, P, s, 6 * i + 3 * s)
            pe.wait_ge(split_done, 9)
            pe.wait_ge(acc_free, 7)
            split_tile(k, acc, 0, 0, k.HH, k.HL, DC).then_inc(mm_done, 1)
            pe.wait_ge(evacuated, 7)
            transposes(pe, 0, 24, 0, 18)

        @block.gpsimd
        def _(pool):
            pool.sem_inc(split_done, 2)
            with pool.Fori(0, 3) as i:
                for s in range(2):
                    pool.wait_ge(k.wfull[s], 16 * i + base[s] + 16)
                    pool.wait_ge(mm_done, 2 * i + s + 1)
                    pool.sem_inc(slot_ok, 1)
                    split_weights(k, pool, s, s, DC, hi_done, 2 * i + s, split_done)
            pool.wait_ge(k.wfull[0], base[0] + 64)
            pool.wait_ge(mm_done, 7)
            split_weights(k, pool, 0, 0, DC, hi_done, 6, split_done)

        @block.scalar
        def _(act):
            act.sem_inc(acc_free, 2)
            with act.Fori(0, 3) as i:
                for s in range(2):
                    act.wait_ge(mm_done, 2 * i + s + 3)
                    act.wait_ge(tr_done, 6 * i + 3 * s + 3)
                    nc.scalar.activation(tokens(tmp[:, s, :]), acc[:, s, :, 0:NW], ACT.Copy).then_inc(evacuated, 1)
                    if s == 0:
                        nc.scalar.activation(tokens(k.KT3[:, i, :]), acc[:, s, :, 0:NW], ACT.Copy).then_inc(acc_free, 1)
                    else:
                        act.wait_ge(evacuated, 2 * i + s + 1)
                        act.sem_inc(acc_free, 1)
            act.wait_ge(mm_done, 9)
            act.wait_ge(tr_done, 6 + 15)
            nc.scalar.activation(tokens(tmp[0:24, 0, :]), acc[0:24, 0, :, 0:NW], ACT.Sigmoid).then_inc(evacuated, 1)

        @block.vector
        def _(dve):
            dve.sem_inc(tp_free, 2)
            with dve.Fori(0, 3) as i:
                for s in range(2):
                    f = bass.ds((2 * i + s) * P, P)
                    for q in range(3):
                        dve.wait_ge(tr_done, 6 * i + 3 * s + q + 7)
                        if q < 2:
                            nc.vector.tensor_copy(k.kvtok[:, 4 * q:4 * q + 4, f],
                                                  tp[:, (s + q) % 2, :].rearrange("p (t f) -> p t f", t=4)).then_inc(tp_free, 1)
                        else:
                            nc.vector.tensor_copy(k.kvtok[0:B, TT, f], tp[0:B, (s + q) % 2, 0:P]).then_inc(tp_free, 1)
            for q in range(2):
                dve.wait_ge(tr_done, 18 + q + 7)
                nc.vector.tensor_copy(k.gtok[:, 4 * q:4 * q + 4, :],
                                      tp[:, q, :].rearrange("p (t f) -> p t f", t=4)[:, :, 0:24]).then_inc(tp_free, 1)
            dve.wait_ge(evacuated, 7)
            nc.vector.tensor_copy(k.gfm[:], tmp[0:24, 0, T:N]).then_inc(samples_copied, 1)
            dve.wait_ge(samples_copied, 1)
            dve.wait_ge(tp_free, 22)


def project_quv(k):
    nc, w = k.nc, k.g["w_in"]
    with Stage(k, "quv") as st:
        acc = st.psum("acc", [P, 2, NT, 512])
        tp = st.psum("tp", [P, 2, 512])
        mm_done, acc_free, tr_done, tp_free, hi_done, split_done, slot_ok = st.sems(
            "mm_done acc_free tr_done tp_free hi_done split_done slot_ok")
        tmp = chunks(k.ONr[:, 0:2 * N], 2)
        base = list(k.wcount)
        for s in range(2):
            k.wcount[s] += 2 * 32 + 4 * 16
        block = st.block()

        @block.sync
        def _(sp):
            with sp.Fori(0, 2) as i:
                for s in range(2):
                    sp.wait_ge(split_done, 2 * i + s + 1)
                    sp.sem_inc(slot_ok, 1)
                    for half in range(2):
                        sp.dma_start(k.W[:, s, 0:8, half * HD:(half + 1) * HD],
                                     weight(w, (2 * i + s) * HD + 4 * HD * half, HD)).then_inc(k.wfull[s], 16)
            with sp.Fori(0, 4) as i:
                for s in range(2):
                    sp.wait_ge(split_done, 2 * i + s + 5)
                    sp.dma_start(k.W[:, s, 0:8, :], weight(w, U0 + (2 * i + s) * P)).then_inc(k.wfull[s], 16)

        @block.tensor
        def _(pe):
            pe.sem_inc(mm_done, 2)
            pe.sem_inc(tr_done, 6)
            with pe.Fori(0, 2) as i:
                for s in range(2):
                    pe.wait_ge(split_done, 2 * i + s + 3)
                    pe.wait_ge(acc_free, 2 * i + s + 1)
                    split_tile(k, acc, s, s, k.HH, k.HL, DC).then_inc(mm_done, 1)
            with pe.Fori(0, 2) as i:
                for s in range(2):
                    pe.wait_ge(split_done, 2 * i + s + 7)
                    pe.wait_ge(acc_free, 2 * i + s + 5)
                    split_tile(k, acc, s, s, k.HH, k.HL, DC).then_inc(mm_done, 1)
            with pe.Fori(0, 2) as i:
                for s in range(2):
                    pe.wait_ge(split_done, 2 * i + s + 11)
                    pe.wait_ge(acc_free, 2 * i + s + 9)
                    split_tile(k, acc, s, s, k.HH, k.HL, DC).then_inc(mm_done, 1)
                for s in range(2):
                    pe.wait_ge(acc_free, 2 * i + s + 2 + 8 + 1)
                    for q in range(3):
                        bank = (s + q) % 2
                        pe.wait_ge(tp_free, 6 * i + 3 * s + q + 1)
                        if q < 2:
                            for t in range(4):
                                last = nc.tensor.transpose(tp[:, bank, t * P:(t + 1) * P],
                                                           tmp[:, s, (4 * q + t) * P:(4 * q + t + 1) * P], k.ident[:])
                        else:
                            last = nc.tensor.transpose(tp[0:B, bank, 0:P], tmp[:, s, T:N], k.ident[:])
                        last.then_inc(tr_done, 1)

        @block.gpsimd
        def _(pool):
            pool.sem_inc(split_done, 2)
            for n, first, step, tiles in ((2, 0, 32, 0), (4, 64, 16, 4)):
                with pool.Fori(0, n) as i:
                    for s in range(2):
                        pool.wait_ge(k.wfull[s], step * i + (base[s] + first + step))
                        pool.wait_ge(mm_done, 2 * i + s + 1 + tiles)
                        pool.sem_inc(slot_ok, 1)
                        split_weights(k, pool, s, s, DC, hi_done, 2 * i + s + tiles, split_done)

        @block.scalar
        def _(act):
            act.sem_inc(acc_free, 2)
            with act.Fori(0, 2) as i:
                for s in range(2):
                    act.wait_ge(mm_done, 2 * i + s + 3)
                    nc.scalar.activation(tokens(k.Q[:, 2 * i + s, :]), acc[:, s, :, 0:NW], ACT.Copy,
                                         scale=HD ** -0.5).then_inc(acc_free, 1)
            with act.Fori(0, 2) as i:
                for s in range(2):
                    act.wait_ge(mm_done, 2 * i + s + 7)
                    nc.scalar.activation(tokens(k.OG[:, 2 * i + s, :]), acc[:, s, :, 0:NW],
                                         ACT.Gelu_apprx_tanh).then_inc(acc_free, 1)
            with act.Fori(0, 2) as i:
                for s in range(2):
                    act.wait_ge(mm_done, 2 * i + s + 11)
                    act.wait_ge(tr_done, 6 * i + 3 * s + 3)
                    nc.scalar.activation(tokens(tmp[:, s, :]), acc[:, s, :, 0:NW],
                                         ACT.Gelu_apprx_tanh).then_inc(acc_free, 1)

        @block.vector
        def _(dve):
            dve.sem_inc(tp_free, 2)
            with dve.Fori(0, 2) as i:
                for s in range(2):
                    f = bass.ds((2 * i + s) * P, P)
                    for q in range(3):
                        dve.wait_ge(tr_done, 6 * i + 3 * s + q + 7)
                        if q < 2:
                            nc.vector.tensor_copy(k.vtok[:, 4 * q:4 * q + 4, f],
                                                  tp[:, (s + q) % 2, :].rearrange("p (t f) -> p t f", t=4)).then_inc(tp_free, 1)
                        else:
                            nc.vector.tensor_copy(k.vtok[0:B, TT, f], tp[0:B, (s + q) % 2, 0:P]).then_inc(tp_free, 1)
            dve.wait_ge(tp_free, 14)


def spatial_gate(k):
    nc, g, out = k.nc, k.g, k.out
    NG = 4
    with Stage(k, "gm") as st:
        ps = st.psum("ps", [P, 2, 1024])
        wp = st.psum("wp", [P, 512])
        sp_ = st.psum("sp", [P, 512])
        const_in, w_turned, w_masked, stats, norm, v_ready, mixed, biased, mixed_free, smp_t, smp, stores = st.sems(
            "const_in w_turned w_masked stats norm v_ready mixed biased mixed_free smp_t smp stores")
        gb = k.Hr[:, 0:GM]
        bb = k.Hr[:, GM:2 * GM]
        wraw = k.Hr[:, 1024:1536].rearrange("p (g s) -> p g s", g=NG)
        wT = k.Hr[:, 1536:2048].rearrange("p (g s) -> p g s", g=NG)
        upper = k.Hr[:, 2048:2176]
        bs = k.Hr[:, 2176:2688].rearrange("p (g t) -> p g t", g=NG)
        mix = k.Hr[:, 2688:4736].rearrange("p (b t) -> p b t", b=2)
        bst = k.Hr[:, 4736:4736 + 54].rearrange("p (t s) -> p t s", s=6)
        mv = k.Hr[:, 4800:4818].rearrange("p (t s) -> p t s", s=2)
        rs = k.Hr[:, 4832:4841]
        w00 = k.Hr[:, 4848:4852]
        vs = k.Hr[:, 4864:4896].rearrange("p (g b) -> p g b", g=NG)
        block = st.block()

        @block.sync
        def _(sp):
            sp.dma_start(gb, g["gm_ln_g"].to_broadcast([P, GM])).then_inc(const_in, 16)
            sp.dma_start(bb, g["gm_ln_b"].to_broadcast([P, GM])).then_inc(const_in, 16)
            sp.dma_start(wraw, g["gm_ws"].rearrange("(g t) s -> t g s", g=NG)).then_inc(const_in, 16)
            sp.dma_start(upper, g["upper"]).then_inc(const_in, 16)
            sp.dma_start(bs, g["gm_bs"].rearrange("g t -> (g t)").unsqueeze(0).to_broadcast([P, 512])
                         .rearrange("p (g t) -> p g t", g=NG)).then_inc(const_in, 16)
            sp.dma_start(w00, g["gm_ws"].rearrange("(g t) s -> g t s", g=NG)[:, 0, 0].unsqueeze(0).to_broadcast([P, NG]),
                         allow_slow_non_contiguous=True).then_inc(const_in, 16)
            sp.wait_ge(v_ready, 1)
            sp.dma_start(out["gm_v"], k.vtok[0:B, TT, :]).then_inc(stores, 16)
            sp.wait_ge(stores, 16)

        @block.tensor
        def _(pe):
            pe.wait_ge(const_in, 96)
            for q in range(NG):
                last = nc.tensor.transpose(wp[:, q * P:(q + 1) * P], wraw[:, q, :], k.ident[:])
            last.then_inc(w_turned, 1)
            pe.wait_ge(w_masked, 1)
            pe.wait_ge(v_ready, 1)
            for q in range(NG):
                if q >= 2:
                    pe.wait_ge(mixed_free, q - 1)
                for t in range(TT):
                    last = nc.tensor.matmul(ps[:, q % 2, t * P:(t + 1) * P], k.vtok[:, t, q * P:(q + 1) * P], wT[:, q, :],
                                            start=True, stop=True)
                last.then_inc(mixed, 1)
            for q in range(NG):
                last = nc.tensor.transpose(sp_[:, q * B:(q + 1) * B], k.vtok[0:B, TT, q * P:(q + 1) * P], k.ident[0:B, 0:B])
            last.then_inc(smp_t, 1)

        @block.scalar
        def _(act):
            act.wait_ge(norm, 2)
            nc.scalar.activation(rs, rs, ACT.Sqrt).then_inc(norm, 1)

        @block.vector
        def _(dve):
            for t in range(9):
                m = P if t < TT else B
                nc.vector.bn_stats(bst[0:m, t, :], k.vtok[0:m, t, :]).then_inc(stats, 1)
            dve.wait_ge(stats, 9)
            nc.vector.memset(mv[:, TT, :], 1.0).then_inc(stats, 1)
            dve.wait_ge(stats, 10)
            for t in range(9):
                m = P if t < TT else B
                nc.vector.bn_aggr(mv[0:m, t, :], bst[0:m, t, :]).then_inc(stats, 1)
            dve.wait_ge(stats, 19)
            nc.vector.tensor_scalar(rs, mv[:, :, 1], EPS, None, ALU.add).then_inc(norm, 1)
            dve.wait_ge(norm, 1)
            nc.vector.reciprocal(rs, rs).then_inc(norm, 1)
            dve.wait_ge(const_in, 96)
            dve.wait_ge(w_turned, 1)
            nc.vector.tensor_tensor(wT, wp[:].rearrange("p (g t) -> p g t", g=NG),
                                    upper.unsqueeze(1).to_broadcast([P, NG, P]), ALU.mult).then_inc(w_masked, 1)
            dve.wait_ge(norm, 3)
            for t in range(9):
                m = P if t < TT else B
                nc.vector.tensor_scalar(k.vtok[0:m, t, :], k.vtok[0:m, t, :], mv[0:m, t, 0:1], rs[0:m, t:t + 1],
                                        ALU.subtract, ALU.mult).then_inc(stats, 1)
            dve.wait_ge(stats, 28)
            for a, b, m in ((0, TT, P), (TT, 9, B)):
                v = k.vtok[0:m, a:b, :]
                nc.vector.tensor_tensor(v, v, gb[0:m, :].unsqueeze(1).to_broadcast([m, b - a, GM]), ALU.mult).then_inc(stats, 1)
            dve.wait_ge(stats, 30)
            for a, b, m in ((0, TT, P), (TT, 9, B)):
                v = k.vtok[0:m, a:b, :]
                last = nc.vector.tensor_tensor(v, v, bb[0:m, :].unsqueeze(1).to_broadcast([m, b - a, GM]), ALU.add)
                last.then_inc(stats if a == 0 else v_ready, 1)
            dve.wait_ge(stats, 31)
            for q in range(NG):
                dve.wait_ge(mixed, q + 1)
                nc.vector.tensor_tensor(mix[:, q % 2, :].rearrange("p (c t) -> p c t", c=TT),
                                        ps[:, q % 2].rearrange("p (c t) -> p c t", c=TT),
                                        bs[:, q, :].unsqueeze(1).to_broadcast([P, TT, P]), ALU.add).then_inc(mixed_free, 1)
                dve.wait_ge(mixed_free, q + 1)
                nc.vector.tensor_tensor(k.OG[:, q, 0:T], k.OG[:, q, 0:T], mix[:, q % 2, :], ALU.mult).then_inc(biased, 1)
            dve.wait_ge(smp_t, 1)
            for q in range(NG):
                nc.vector.tensor_scalar(vs[:, q, :], sp_[:, q * B:(q + 1) * B], w00[:, q:q + 1], bs[:, q, 0:1],
                                        ALU.mult, ALU.add).then_inc(smp, 1)
            dve.wait_ge(smp, NG)
            nc.vector.tensor_tensor(k.OG[:, :, T:N], k.OG[:, :, T:N], vs, ALU.mult).then_inc(smp, 1)
            dve.wait_ge(smp, NG + 1)
            dve.wait_ge(biased, NG)


def compress(k):
    nc, g = k.nc, k.g
    with Stage(k, "cmp") as st:
        tp = st.psum("tp", [P, 4, 512])
        pre = st.psum("pre", [P, 2, 512])
        kv = st.psum("kv", [P, 2, 512])
        gathered = st.sems("gathered_0 gathered_1")
        prompt_in, regrouped_k, regrouped_v, w_in, w2_cleared, w2_placed, pe_done, pe_copied, tr_done, tp_copied, pre_done, silu_done, kv_done, kv_copied = st.sems(
            "prompt_in regrouped_k regrouped_v w_in w2_cleared w2_placed pe_done pe_copied tr_done tp_copied pre_done silu_done kv_done kv_copied")
        G = [k.Hr[:, 0:4096].rearrange("p (r f) -> p r f", r=16), k.ONr[:, 0:4096].rearrange("p (r f) -> p r f", r=16)]
        RG = [k.W[:].rearrange("p a c m -> p (a c m)")[:, 0:2048], k.E[:, 3584:5632]]
        TR = k.Hr[:, 4096:8192].rearrange("p (kv c g n) -> p kv c g n", kv=2, c=8, g=2)
        w1 = k.CW[:].rearrange("p (kv c m) -> p kv c m", kv=2, c=16)
        sh = k.E[:, 2304:2816].rearrange("p (kv g n) -> p kv g n", kv=2, g=2)
        w2k = k.E[:, 2816:3072].rearrange("p (g m) -> p g m", g=2)
        w2v = k.E[:, 3072:3136]
        pos = k.E[:, 3136:3168].rearrange("p (kv c) -> p kv c", kv=2)
        pe_b = k.tiny[:, 0:2]
        block = st.block()

        @block.gpsimd
        def _(pool):
            for b in range(B):
                pool.wait_ge(regrouped_k, b + 1)
                pool.wait_ge(regrouped_v, b + 1)
                pool.indirect_dma_start(
                    out=(k.Hr[:, 0:4096], k.ONr[:, 0:4096])[b % 2], out_offset=None, in_=g["cache_cmp_kv"],
                    in_offset=bass.IndirectOffsetOnAxis(ap=k.pid[:, b:b + 1], axis=0)).then_inc(gathered[b % 2], 16)

        @block.sync
        def _(sp):
            for i, n in enumerate("kv"):
                sp.dma_start(w1[:, i], g[f"cmp_w1_{n}"].rearrange("(c p) m -> p c m", p=P)).then_inc(w_in, 16)
                sp.dma_start(pos[:, i, :], g[f"cmp_pe_{n}"].rearrange("a (c p) -> p (a c)", p=P),
                             allow_slow_non_contiguous=True).then_inc(w_in, 16)
            sp.dma_start(w2v, g["cmp_w2_v"]).then_inc(w_in, 16)
            sp.wait_ge(w2_cleared, 1)
            for i in range(2):
                sp.dma_start(w2k[:, i, i * HD:(i + 1) * HD], g["cmp_w2_k"]).then_inc(w2_placed, 16)
            sp.wait_ge(regrouped_k, 2 + 7)
            sp.wait_ge(regrouped_v, 2 + 7)
            sp.dma_start(k.Hr[0:64, 0:4096], k.out["cmp_p"].rearrange("(n r) f -> n (r f)", r=16)).then_inc(prompt_in, 16)

        def turn(pe, b, n):
            for q in range(8):
                if q % 4 == 0:
                    pe.wait_ge((regrouped_k, regrouped_v)[q // 4], b + 3)
                pe.wait_ge(tp_copied, 8 * b + q + 1)
                for j in range(4):
                    f = (j % 2) * 1024 + (2 * (q % 4) + j // 2) * P
                    last = nc.tensor.transpose(tp[:, q % 4, j * P:j * P + n], RG[q // 4][0:n, f:f + P],
                                               k.ident[0:n, 0:n])
                last.then_inc(tr_done, 1)

        def hidden(pe, b, n):
            for i in range(2):
                pe.wait_ge(tp_copied, 8 * b + 4 * i + 8)
                pe.wait_ge(silu_done, 2 * b + i + 1)
                for c in range(16):
                    last = nc.tensor.matmul(pre[:, i, 0:2 * n].rearrange("p (g n) -> p g n", g=2), w1[:, i, c, :],
                                            TR[:, i, c % 8, :, c // 8:c // 8 + n], start=(c == 0), stop=(c == 15))
                last.then_inc(pre_done, 1)
            pe.wait_ge(silu_done, 2 * b + 4)
            pe.wait_ge(kv_copied, 2 * b + 1)
            for gr in range(2):
                last = nc.tensor.matmul(kv[:, 0, 0:n], w2k[:, gr, :], sh[:, 0, gr, 0:n], start=(gr == 0), stop=(gr == 1))
            last.then_inc(kv_done, 1)
            pe.wait_ge(kv_copied, 2 * b + 2)
            for gr in range(2):
                last = nc.tensor.matmul(kv[0:n, 1, gr * HD:(gr + 1) * HD], sh[:, 1, gr, 0:n], w2v, start=True, stop=True)
            last.then_inc(kv_done, 1)

        @block.tensor
        def _(pe):
            pe.sem_inc(tr_done, 16)
            pe.wait_ge(w_in, 80)
            for i in range(2):
                for c in range(16):
                    last = nc.tensor.matmul(pre[:, i, 0:1], w1[:, i, c, :], pos[:, i, c:c + 1], start=(c == 0), stop=(c == 15))
            last.then_inc(pe_done, 1)
            pe.wait_ge(pe_copied, 1)
            pe.wait_ge(w2_placed, 32)
            with pe.Fori(0, 4) as i:
                for s in range(2):
                    turn(pe, 2 * i + s, P)
                    hidden(pe, 2 * i + s, NCS)
            turn(pe, 8, 64)
            hidden(pe, 8, NCP)

        @block.scalar
        def _(act):
            act.sem_inc(silu_done, 2)
            act.sem_inc(kv_copied, 2)
            act.sem_inc(regrouped_k, 2)
            act.wait_ge(pe_copied, 1)

            def batch(s, b, rows_in, full, m, n, kc, vc):
                act.wait_ge(rows_in, full)
                act.wait_ge(tr_done, 8 * b + 12)
                nc.scalar.activation(RG[0][0:m].rearrange("p (g r d) -> p g r d", g=2, r=16),
                                     G[s][0:m, :, 0:P].rearrange("p r (g d) -> p g r d", g=2), ACT.Copy).then_inc(regrouped_k, 1)
                for i in range(2):
                    act.wait_ge(pre_done, 2 * b + i + 1)
                    act.wait_ge(kv_done, 2 * b + 2)
                    nc.scalar.activation(sh[:, i, :, 0:n], pre[:, i, 0:2 * n].rearrange("p (g n) -> p g n", g=2), ACT.Silu,
                                         bias=pe_b[:, i:i + 1]).then_inc(silu_done, 1)
                act.wait_ge(kv_done, 2 * b + 3)
                nc.scalar.activation(kc, kv[:, 0, 0:n], ACT.Copy).then_inc(kv_copied, 1)
                act.wait_ge(kv_done, 2 * b + 4)
                nc.scalar.activation(vc, kv[0:n, 1, 0:P], ACT.Copy).then_inc(kv_copied, 1)

            act.sem_inc(kv_done, 2)
            with act.Fori(0, 4) as i:
                for s in range(2):
                    b = 2 * i + s
                    batch(s, b, gathered[s], 16 * i + 16, P, NCS, k.KC[:, b, 0:NCS], k.VC[0:NCS, b, :])
            batch(0, 8, prompt_in, 16, 64, NCP, k.KC[:, 8, 0:NCP], k.VC[0:NCP, 8, :])
            act.wait_ge(kv_copied, 20)

        @block.vector
        def _(dve):
            dve.sem_inc(tp_copied, 4)
            dve.sem_inc(regrouped_v, 2)
            nc.vector.memset(w2k, 0.0).then_inc(w2_cleared, 1)
            dve.wait_ge(pe_done, 1)
            nc.vector.tensor_copy(pe_b, pre[:, :, 0]).then_inc(pe_copied, 1)

            def batch(s, b, rows_in, full, n):
                dve.wait_ge(rows_in, full)
                dve.wait_ge(tr_done, 8 * b + 16)
                nc.vector.tensor_copy(RG[1][0:n].rearrange("p (g r d) -> p g r d", g=2, r=16),
                                      G[s][0:n, :, P:2 * P].rearrange("p r (g d) -> p g r d", g=2)).then_inc(regrouped_v, 1)
                for q in range(8):
                    dve.wait_ge(tr_done, 8 * b + q + 17)
                    dve.wait_ge(silu_done, 2 * b + q // 4 + 1)
                    nc.vector.tensor_copy(TR[:, q // 4, 2 * (q % 4):2 * (q % 4) + 2, :, 0:n],
                                          tp[:, q % 4, :].rearrange("p (c g n) -> p c g n", c=2, g=2)[:, :, :, 0:n]).then_inc(tp_copied, 1)

            with dve.Fori(0, 4) as i:
                for s in range(2):
                    batch(s, 2 * i + s, gathered[s], 16 * i + 16, P)
            batch(0, 8, prompt_in, 16, 64)
            dve.wait_ge(tp_copied, 76)


def select_blocks(k):
    nc, g = k.nc, k.g
    R = B * H
    with Stage(k, "sel") as st:
        ps = st.psum("ps", [P, 8, 512])
        cleared, q_placed, const_in, scored, negated, exped, inverted, scaled, turned, turned_out, imp1, imp1_out, imp, imp_out, placed, out_c, ranked, row, mg, mg_out, bias_out, lg, qf = st.sems(
            "cleared q_placed const_in scored negated exped inverted scaled turned turned_out imp1 imp1_out imp imp_out placed "
            "out_c ranked row mg mg_out bias_out lg qf")
        at = [0]

        def room(words, rows=P):
            a = at[0]
            at[0] += words
            return k.Hr[0:rows, a:a + words]

        QS = room(576)
        relb64 = room(64, 33)
        oh = room(768, 33)
        LG = room(64, 24)
        head_of, branch_of = room(8, 24), room(4, 24)[:, 0:3]
        S = room(128, R)[:, 0:NCS]
        SG = room(128, R)[:, 0:NCS]
        PCT, PCG = room(64, NCS), room(64, NCS)
        OV = room(36, NCS)[:, 0:NSEL]
        G64 = room(64, R)
        IM = room(36, R)[:, 0:NSEL]
        SC = room(36, R)[:, 0:NSEL]
        before = room(NSEL * NSEL, R)
        C1, C2 = room(NSEL * NSEL, R), room(NSEL * NSEL, R)
        cnt = room(36, R)[:, 0:NSEL]
        row_ = room(36, R)
        nm, l, li = room(1, R), room(1, R), room(1, R)
        block = st.block()
        sq = "p (j i) -> p j i"

        @block.sync
        def _(sp):
            for dst, n in ((oh, "oh_samples"), (head_of, "head_of"), (branch_of, "branch_of"), (OV, "overlap"), (G64, "same_group")):
                sp.dma_start(dst, g[n]).then_inc(const_in, 16)
            sp.dma_start(before, g["before"].to_broadcast([R, NSEL * NSEL])).then_inc(const_in, 16)
            sp.dma_start(k.e8, g["eye"][0:B, 0:B].unsqueeze(0).to_broadcast([B, B, B])).then_inc(const_in, 16)

        @block.tensor
        def _(pe):
            pe.wait_ge(const_in, 112)
            pe.wait_ge(qf, 1)
            pe.wait_ge(lg, 2)
            for b in range(B):
                nc.tensor.matmul(ps[0:R, 0, 0:NCS], QS[:, b * R:(b + 1) * R], k.KC[:, b, 0:NCS], start=(b == 0), stop=False)
            nc.tensor.matmul(ps[0:R, 0, 0:NCS], relb64, oh[:, OH_CMP:OH_CMP + NCS], start=False, stop=True).then_inc(scored, 1)
            nc.tensor.matmul(ps[0:R, 1, 0:3], LG, branch_of, start=True, stop=True).then_inc(scored, 1)
            nc.tensor.matmul(ps[0:H, 2, 0:129], k.relb[:], oh[:, OH_SELF:OH_WIN], start=True, stop=True).then_inc(scored, 1)
            nc.tensor.matmul(ps[0:H, 3, :], k.relb[:], oh[:, OH_WIN:768], start=True, stop=True).then_inc(scored, 1)
            pe.wait_ge(scaled, 1)
            nc.tensor.transpose(ps[0:NCS, 4, 0:R], S, k.ident[0:R, 0:R]).then_inc(turned, 1)
            pe.wait_ge(scaled, 2)
            nc.tensor.transpose(ps[0:NCS, 5, 0:R], SG, k.ident[0:R, 0:R]).then_inc(turned, 1)
            pe.wait_ge(turned_out, 1)
            nc.tensor.matmul(ps[0:R, 6, 0:NSEL], PCT, OV, start=True, stop=True).then_inc(imp1, 1)
            pe.wait_ge(imp1_out, 1)
            nc.tensor.matmul(ps[0:R, 7, 0:NSEL], G64, IM, start=True, stop=True).then_inc(imp, 1)
            pe.wait_ge(turned_out, 2)
            for b in range(B):
                last = nc.tensor.matmul(ps[:, 4, b * H:(b + 1) * H], k.VC[0:NCS, b, :], PCG[:, b * H:(b + 1) * H],
                                        start=True, stop=True)
            last.then_inc(out_c, 1)
            pe.wait_ge(row, 2)
            for b in range(B):
                last = nc.tensor.matmul(ps[0:H, 5, b * 36:(b + 1) * 36], k.ident[0:R, b * H:(b + 1) * H], row_, start=True, stop=True)
            last.then_inc(mg, 1)

        @block.scalar
        def _(act):
            act.wait_ge(negated, 1)
            nc.scalar.activation(S, ps[0:R, 0, 0:NCS], ACT.Exp, bias=nm, accum_out=l).then_inc(exped, 1)

        @block.vector
        def _(dve):
            nc.vector.memset(QS, 0.0).then_inc(cleared, 1)
            nc.vector.memset(k.QS8, 0.0).then_inc(cleared, 1)
            nc.vector.tensor_copy(relb64.rearrange("p (b h) -> p b h", b=B), k.relb[:].unsqueeze(1).to_broadcast([33, B, H])).then_inc(lg, 1)
            dve.wait_ge(cleared, 2)
            for i in range(2):
                nc.vector.tensor_copy(k.QS8[i * HD:(i + 1) * HD, :, 4 * i:4 * i + 4],
                                      k.Q[i * HD:(i + 1) * HD, :, T:N].rearrange("p c b -> p b c")).then_inc(q_placed, 1)
            dve.wait_ge(q_placed, 2)
            nc.vector.tensor_copy(QS.rearrange("p (b x) -> p b x", b=B)[:, :, 0:H], k.QS8).then_inc(qf, 1)
            dve.wait_ge(const_in, 112)
            nc.vector.tensor_tensor(LG.rearrange("p (b h) -> p b h", b=B), k.gfm[:].unsqueeze(2).to_broadcast([24, B, H]),
                                    head_of.unsqueeze(1).to_broadcast([24, B, H]), ALU.mult).then_inc(lg, 1)
            dve.wait_ge(scored, 1)
            nc.vector.tensor_reduce(nm, ps[0:R, 0, 0:NCS], AX, ALU.max, negate=True).then_inc(negated, 1)
            dve.wait_ge(scored, 4)
            nc.vector.tensor_copy(row_[:, 33:36], ps[0:R, 1, 0:3]).then_inc(row, 1)
            nc.vector.tensor_copy(k.near_b, ps[0:H, 2, 0:129]).then_inc(bias_out, 1)
            nc.vector.tensor_copy(k.win_b, ps[0:H, 3, :]).then_inc(bias_out, 1)
            dve.wait_ge(exped, 1)
            nc.vector.reciprocal(li, l).then_inc(inverted, 1)
            dve.wait_ge(inverted, 1)
            nc.vector.tensor_scalar(S, S, li, None, ALU.mult).then_inc(scaled, 1)
            dve.wait_ge(scaled, 1)
            dve.wait_ge(row, 1)
            nc.vector.tensor_scalar(SG, S, row_[:, 33:34], None, ALU.mult).then_inc(scaled, 1)
            dve.wait_ge(turned, 1)
            nc.vector.tensor_copy(PCT, ps[0:NCS, 4, 0:R]).then_inc(turned_out, 1)
            dve.wait_ge(turned, 2)
            nc.vector.tensor_copy(PCG, ps[0:NCS, 5, 0:R]).then_inc(turned_out, 1)
            dve.wait_ge(imp1, 1)
            nc.vector.tensor_copy(IM, ps[0:R, 6, 0:NSEL]).then_inc(imp1_out, 1)
            dve.wait_ge(imp, 1)
            nc.vector.tensor_copy(SC, ps[0:R, 7, 0:NSEL]).then_inc(imp_out, 1)
            dve.wait_ge(imp_out, 1)
            nc.vector.memset(SC[:, 0:1], FORCE).then_inc(placed, 1)
            nc.vector.memset(SC[:, NSEL - 2:NSEL], FORCE).then_inc(placed, 1)
            dve.wait_ge(placed, 2)
            one = SC.unsqueeze(1).to_broadcast([R, NSEL, NSEL])
            other = SC.unsqueeze(2).to_broadcast([R, NSEL, NSEL])
            nc.vector.tensor_tensor(C1.rearrange(sq, j=NSEL), one, other, ALU.is_gt).then_inc(ranked, 1)
            nc.vector.tensor_tensor(C2.rearrange(sq, j=NSEL), one, other, ALU.is_equal).then_inc(ranked, 1)
            dve.wait_ge(ranked, 2)
            nc.vector.tensor_tensor(C2, C2, before, ALU.mult).then_inc(ranked, 1)
            dve.wait_ge(ranked, 3)
            nc.vector.tensor_tensor(C1, C1, C2, ALU.add).then_inc(ranked, 1)
            dve.wait_ge(ranked, 4)
            nc.vector.tensor_reduce(cnt, C1.rearrange(sq, j=NSEL), AX, ALU.add).then_inc(ranked, 1)
            dve.wait_ge(ranked, 5)
            nc.vector.tensor_scalar(row_[:, 0:NSEL], cnt, float(TOPK) - 0.5, NEG, ALU.is_ge, ALU.mult).then_inc(row, 1)
            dve.wait_ge(out_c, 1)
            nc.vector.tensor_copy(k.OC, ps[:, 4, 0:64].rearrange("p (b h) -> p b h", b=B)).then_inc(mg_out, 1)
            dve.wait_ge(mg, 1)
            nc.vector.tensor_copy(k.MG, ps[0:H, 5, 0:288].rearrange("p (b x) -> p b x", b=B)).then_inc(mg_out, 1)
            dve.wait_ge(mg_out, 2)
            dve.wait_ge(bias_out, 2)


def sample_attention(k):
    nc, g = k.nc, k.g
    with Stage(k, "smp") as st:
        tp = st.psum("tp", [P, 2, 512])
        sc = st.psum("sc", [P, 4, 512])
        wsc = st.psum("wsc", [P, 512])
        misc = st.psum("misc", [P, 512])
        gathered = st.sems("gathered_0 gathered_1")
        turn_now, win_in, tr_done, tp_copied, q_staged, scored, summed, negated, exped, inverted, scaled, diag, turned, turned_out, pv_done, o_done, near = st.sems(
            "turn_now win_in tr_done tp_copied q_staged scored summed negated exped inverted scaled diag turned turned_out pv_done o_done near")
        Gr = [k.Hr[:, 0:4096], k.Hr[:, 4096:8192]]
        G = [x.rearrange("p (r f) -> p r f", r=16) for x in Gr]
        kT = k.CW[:, 0:2560].rearrange("p (q n) -> p q n", q=5)
        GW = k.CW[:, 2560:3584].rearrange("p (r f) -> p r f", r=4)
        S, SW = k.E[0:H, 2304:2304 + 2049], k.E[0:H, 4368:4368 + 513]
        PT, MS, MD = k.E[:, 5456:5616], k.tiny[0:B, 0:16], k.small[0:H, 0:16]
        nm, l, cc = k.small[0:H, 16:18], k.small[0:H, 18:20], k.small[0:H, 20:22]
        QB = k.small[:, 24:32]
        vnew = [k.kvtok[0:B, TT, 384:512], k.kvtok[0:B, TT, 640:768]]
        block = st.block()

        @block.gpsimd
        def _(pool):
            for b in range(B):
                pool.wait_ge(pv_done, b + 1)
                pool.indirect_dma_start(
                    out=Gr[b % 2], out_offset=None, in_=g["cache_slc_kv"],
                    in_offset=bass.IndirectOffsetOnAxis(ap=k.pid[:, b:b + 1], axis=0)).then_inc(gathered[b % 2], 16)

        @block.sync
        def _(sp):
            with sp.Fori(0, 8) as b:
                sp.wait_ge(pv_done, b + 2)
                sp.dma_start(GW, g["state_win_kv"][bass.ds(b, 1), :, :].rearrange("b (n r) f -> n (b r) f", r=4)).then_inc(win_in, 16)

        @block.tensor
        def _(pe):
            pe.sem_inc(pv_done, 2)
            with pe.Fori(0, 4) as i:
                for s in range(2):
                    b = 2 * i + s
                    pe.wait_ge(gathered[s], 16 * i + 16)
                    for q in range(5):
                        if q == 4:
                            pe.wait_ge(win_in, 16 * b + 16)
                        pe.wait_ge(tp_copied, 5 * b + q + 1)
                        for j in range(4):
                            src = G[s][:, 4 * q + j, 0:P] if q < 4 else GW[:, j, 0:P]
                            last = nc.tensor.transpose(tp[:, (5 * s + q) % 2, j * P:(j + 1) * P], src, k.ident[:])
                        last.then_inc(tr_done, 1)
                    pe.wait_ge(tp_copied, 5 * b + 7)
                    pe.wait_ge(q_staged, b + 1)
                    pe.wait_ge(summed, b + 1)
                    pe.wait_ge(o_done, 2 * b + 2)
                    for q in range(4):
                        nc.tensor.matmul(sc[0:H, q, :], QB, kT[:, q, :], start=True, stop=True)
                    nc.tensor.matmul(wsc[0:H, :], QB, kT[:, 4, :], start=True, stop=True)
                    nc.tensor.matmul(misc[0:H, 0:2], QB, k.KT[:, :, bass.ds(b + T, 1)].rearrange("p a t -> p (a t)"),
                                     start=True, stop=True).then_inc(scored, 1)
                    pe.wait_ge(scaled, 2 * b + 2)
                    pe.wait_ge(diag, 2 * b + 2)
                    pe.sem_inc(turn_now, 1)
                    for r in range(16):
                        nc.tensor.transpose(misc[:, r * H:(r + 1) * H], S[:, r * P:(r + 1) * P], k.ident[0:H, 0:H])
                    for r in range(4):
                        nc.tensor.transpose(misc[:, P + r * H:P + (r + 1) * H], SW[:, r * P:(r + 1) * P], k.ident[0:H, 0:H])
                    for r in range(2):
                        last = nc.tensor.transpose(misc[0:B, 160 + r * B:160 + (r + 1) * B], MD[:, r * B:(r + 1) * B], k.ident[0:H, 0:H])
                    last.then_inc(turned, 1)
                    pe.wait_ge(turned_out, 2 * b + 2)
                    for r in range(16):
                        nc.tensor.matmul(misc[:, 256:264], G[s][:, r, P:2 * P], PT[:, r * H:(r + 1) * H], start=(r == 0), stop=False)
                    for r in range(4):
                        nc.tensor.matmul(misc[:, 256:264], GW[:, r, P:2 * P], PT[:, P + r * H:P + (r + 1) * H], start=False, stop=False)
                    for r in range(2):
                        last = nc.tensor.matmul(misc[:, 256:264], vnew[r], MS[:, r * H:(r + 1) * H], start=False, stop=(r == 1))
                    last.then_inc(pv_done, 1)

        @block.scalar
        def _(act):
            with act.Fori(0, 8) as b:
                act.wait_ge(negated, 2 * b + 1)
                nc.scalar.activation(S, S, ACT.Exp, bias=nm[:, 0:1], accum_out=l[:, 0:1]).then_inc(exped, 1)
                act.wait_ge(negated, 2 * b + 2)
                nc.scalar.activation(SW, SW, ACT.Exp, bias=nm[:, 1:2], accum_out=l[:, 1:2]).then_inc(exped, 1)

        @block.vector
        def _(dve):
            dve.sem_inc(tp_copied, 2)
            dve.sem_inc(summed, 1)
            dve.sem_inc(o_done, 2)
            dve.sem_inc(near, 1)
            with dve.Fori(0, 4) as i:
                for s in range(2):
                    b = 2 * i + s
                    nc.vector.tensor_copy(QB, k.QS8[:, b, :]).then_inc(q_staged, 1)
                    for q in range(5):
                        dve.wait_ge(tr_done, 5 * b + q + 1)
                        nc.vector.tensor_copy(kT[:, q, :], tp[:, (5 * s + q) % 2, :]).then_inc(tp_copied, 1)
                    dve.wait_ge(scored, b + 1)
                    nc.vector.tensor_tensor(S[:, 0:2048].rearrange("p (r j x) -> p r j x", r=16, x=4),
                                            sc[0:H].rearrange("p a (r j x) -> p (a r) j x", r=4, x=4),
                                            k.MG[:, b, 0:32].unsqueeze(2).unsqueeze(1).to_broadcast([H, 16, 32, 4]),
                                            ALU.add).then_inc(near, 1)
                    nc.vector.tensor_tensor(SW[:, 0:512], wsc[0:H, :], k.win_b, ALU.add).then_inc(near, 1)
                    nc.vector.tensor_scalar(S[:, 2048:2049], misc[0:H, 0:1], k.near_b[:, 0:1], None, ALU.add).then_inc(near, 1)
                    nc.vector.tensor_scalar(SW[:, 512:513], misc[0:H, 1:2], k.near_b[:, 0:1], None, ALU.add).then_inc(summed, 1)
                    dve.wait_ge(near, 4 * b + 4)
                    sn = S[:, 0:2048].rearrange("p (r n) -> p r n", r=16)[:, :, 120:128]
                    nc.vector.tensor_tensor(sn, sn, k.near_b[:, 1:129].rearrange("p (r n) -> p r n", r=16), ALU.add).then_inc(near, 1)
                    dve.wait_ge(near, 4 * b + 5)
                    dve.wait_ge(summed, b + 2)
                    nc.vector.tensor_reduce(nm[:, 0:1], S, AX, ALU.max, negate=True).then_inc(negated, 1)
                    nc.vector.tensor_reduce(nm[:, 1:2], SW, AX, ALU.max, negate=True).then_inc(negated, 1)
                    dve.wait_ge(exped, 2 * b + 2)
                    nc.vector.reciprocal(cc, l).then_inc(inverted, 1)
                    dve.wait_ge(inverted, 2 * b + 1)
                    nc.vector.tensor_tensor(cc, cc, k.MG[:, b, 34:36], ALU.mult).then_inc(inverted, 1)
                    dve.wait_ge(inverted, 2 * b + 2)
                    nc.vector.tensor_scalar(S, S, cc[:, 0:1], None, ALU.mult).then_inc(scaled, 1)
                    nc.vector.tensor_scalar(SW, SW, cc[:, 1:2], None, ALU.mult).then_inc(scaled, 1)
                    dve.wait_ge(scaled, 2 * b + 2)
                    nc.vector.tensor_scalar(MD[:, 0:B], k.e8[:, b, :], S[:, 2048:2049], None, ALU.mult).then_inc(diag, 1)
                    nc.vector.tensor_scalar(MD[:, B:2 * B], k.e8[:, b, :], SW[:, 512:513], None, ALU.mult).then_inc(diag, 1)
                    dve.wait_ge(turned, b + 1)
                    nc.vector.tensor_copy(PT, misc[:, 0:160]).then_inc(turned_out, 1)
                    nc.vector.tensor_copy(MS, misc[0:B, 160:176]).then_inc(turned_out, 1)
                    dve.wait_ge(pv_done, b + 3)
                    for gr in range(2):
                        h0 = slice(gr * HD, (gr + 1) * HD)
                        nc.vector.tensor_tensor(k.ON[h0, :, bass.ds(b + T, 1)].rearrange("p c t -> p (c t)"),
                                                misc[h0, 256 + 4 * gr:260 + 4 * gr], k.OC[h0, b, 4 * gr:4 * gr + 4],
                                                ALU.add).then_inc(o_done, 1)
            dve.wait_ge(o_done, 18)


def bias_tables(k):
    nc, g = k.nc, k.g
    with Stage(k, "bias") as st:
        ps = st.psum("ps", [P, 4, 512])
        pc = st.psum("pc", [P, 512])
        const_in, repeated, row_done, row_out, shifted, turned_in, cmp_done, cmp_set, cmp_out, gates = st.sems(
            "const_in repeated row_done row_out shifted turned_in cmp_done cmp_set cmp_out gates")
        RB = k.Hr[0:33, 0:1024].rearrange("p (h m) -> p h m", h=H)
        ohn = k.Hr[0:33, 1024:1408]
        TB = k.Hr[:, 1408:4480].rearrange("p (h x) -> p h x", h=H)
        ohc = k.Hr[0:33, 4480:6400]
        hb = k.tiny[:, 0:1]
        block = st.block()

        @block.sync
        def _(sp):
            sp.dma_start(ohn, g["oh_near"]).then_inc(const_in, 16)
            sp.dma_start(ohc, g["oh_cmp"]).then_inc(const_in, 16)
            sp.dma_start(k.WM, g["window_edge"]).then_inc(const_in, 16)
            sp.dma_start(hb, g["has_block"]).then_inc(const_in, 16)
            sp.wait_ge(row_out, H)
            sp.dma_start(k.scratch.rearrange("h (i x) -> i h x", i=P), TB).then_inc(shifted, 16)
            sp.wait_ge(shifted, 16)
            sp.dma_start(k.NB, k.scratch[:, 127:127 + P * 383].rearrange("h (i w) -> i h w", w=383)[:, :, 0:256]).then_inc(turned_in, 16)
            sp.wait_ge(turned_in, 16)

        @block.tensor
        def _(pe):
            pe.wait_ge(const_in, 64)
            for m in range(15):
                last = nc.tensor.matmul(pc[:, m * H:(m + 1) * H], ohc[:, m * P:(m + 1) * P], k.relb[:], start=True, stop=True)
            last.then_inc(cmp_done, 1)
            pe.wait_ge(repeated, 1)
            for h in range(H):
                if h >= 4:
                    pe.wait_ge(row_out, h - 3)
                nc.tensor.matmul(ps[:, h % 4, 0:384], RB[:, h, :], ohn, start=True, stop=True).then_inc(row_done, 1)

        @block.scalar
        def _(act):
            for h in range(H):
                act.wait_ge(row_done, h + 1)
                nc.scalar.activation(TB[:, h, :], ps[:, h % 4, 0:384], ACT.Copy).then_inc(row_out, 1)

        @block.vector
        def _(dve):
            nc.vector.tensor_copy(RB, k.relb[:].unsqueeze(2).to_broadcast([33, H, P])).then_inc(repeated, 1)
            nc.vector.memset(k.BC[:, :, 0:48], 0.0).then_inc(cmp_set, 1)
            nc.vector.memset(k.BC[:, :, 63:119], NEG).then_inc(cmp_set, 1)
            dve.wait_ge(cmp_done, 1)
            nc.vector.tensor_copy(k.BC[:, :, 48:63], pc[:, 0:120].rearrange("p (m h) -> p h m", h=H)).then_inc(cmp_set, 1)
            dve.wait_ge(const_in, 64)
            g0 = k.gtok[:, 0, :].rearrange("p (h r) -> p h r", r=3)[:, :, 0]
            nc.vector.tensor_scalar(g0, g0, hb, None, ALU.mult).then_inc(gates, 1)
            dve.wait_ge(gates, 1)
            dve.wait_ge(cmp_set, 3)


def prompt_attention(k):
    nc = k.nc
    with Stage(k, "att") as st:
        sS = st.psum("slc", [P, 1024])
        sW = st.psum("win", [P, 1024])
        tp = st.psum("tp", [P, 2, 512])
        op = st.psum("op", [P, 512])
        q_ready, scored_s, scored_w, exp_s, exp_w, exp_c, biased, negated, factor, p_ready, pt_done, pt_copied, pv_done, o_copied, turn_cmp = st.sems(
            "q_ready scored_s scored_w exp_s exp_w exp_c biased negated factor p_ready pt_done pt_copied pv_done o_copied turn_cmp")
        PR = [k.Hr[:, 0:1728], k.Hr[:, 1728:3456]]
        PT = [k.Hr[:, 3456:5248], k.Hr[:, 5248:7040]]
        QB = k.Hr[:, 7040:7168]
        nm = [k.Hr[:, 7168:7171], k.Hr[:, 7176:7179]]
        l = [k.Hr[:, 7184:7187], k.Hr[:, 7192:7195]]
        cc = [k.Hr[:, 7200:7203], k.Hr[:, 7208:7211]]
        CMP = 640
        plan, groups = [], 0
        for t in range(TT):
            wb = list(range(max(0, t - 4), t + 1))
            ng = -(-(t + 1 + len(wb)) // 4) + 1
            plan.append((t, wb, ng, groups))
            groups += 8 * ng
        x_back, = st.sems("x_back")
        block = st.block()


        @block.sync
        def _(sp):
            sp.dma_start(k.X[:].rearrange("p c t -> p (c t)"), k.kept).then_inc(x_back, 16)
            sp.wait_ge(x_back, 16)

        @block.tensor
        def _(pe):
            def scores(tile, c, gr):
                t, wb, ng, g0 = tile
                s = 2 * c + gr + 8 * t
                rows = slice(gr * HD, (gr + 1) * HD)
                if gr == 0:
                    pe.wait_ge(q_ready, c + 4 * t + 1)
                pe.wait_ge(exp_s, s + 1)
                w = (t + 1) * P
                for a in range(0, w, 512):
                    e = min(w, a + 512)
                    last = nc.tensor.matmul(sS[:, a:e], QB[rows, :], k.KT[rows, 0, a:e], start=True, stop=True)
                last.then_inc(scored_s, 1)
                pe.wait_ge(exp_w, s + 1)
                pe.wait_ge(exp_c, s + 1)
                w = len(wb) * P
                for a in range(0, w, 512):
                    e = min(w, a + 512)
                    nc.tensor.matmul(sW[:, a:e], QB[rows, :], k.KT[rows, 1, wb[0] * P + a:wb[0] * P + e], start=True, stop=True)
                nc.tensor.matmul(sW[:, CMP:CMP + NCP], QB[rows, :], k.KC[rows, 8, 0:NCP], start=True, stop=True).then_inc(scored_w, 1)

            def turns_and_products(tile, c, gr):
                t, wb, ng, g0 = tile
                s = 2 * c + gr + 8 * t
                pe.wait_ge(p_ready, 3 * s + 3)
                cols = [P * j for j in range(t + 1)] + [1024 + P * j for j in range(len(wb))]
                for q in range(ng):
                    pe.wait_ge(pt_copied, (2 * c + gr) * ng + (g0 + q + 1))
                    bank = (gr * ng + q) % 2
                    if q < ng - 1:
                        for j, a in enumerate(cols[4 * q:4 * q + 4]):
                            last = nc.tensor.transpose(tp[:, bank, j * P:(j + 1) * P], PR[gr][:, a:a + P], k.ident[:])
                    else:
                        pe.sem_inc(turn_cmp, 1)
                        last = nc.tensor.transpose(tp[0:NCP, bank, 0:P], PR[gr][:, 1664:1664 + NCP], k.ident[:])
                    last.then_inc(pt_done, 1)
                if gr == 0:
                    pe.wait_ge(o_copied, c + 4 * t + 1)
                o = op[gr * HD:(gr + 1) * HD, 0:P]
                kv = [(b, 384) for b in range(t + 1)] + [(b, 640) for b in wb]
                for j, (b, f) in enumerate(kv):
                    if j % 4 == 0:
                        pe.wait_ge(pt_copied, (2 * c + gr) * ng + g0 + 3 + j // 4 + (j // 4 == ng - 2))
                    nc.tensor.matmul(o, k.kvtok[:, b, f + gr * HD:f + (gr + 1) * HD], PT[gr][:, j * P:(j + 1) * P],
                                     start=(j == 0), stop=False)
                nc.tensor.matmul(o, k.VC[0:NCP, 8, gr * HD:(gr + 1) * HD], PT[gr][0:NCP, len(kv) * P:(len(kv) + 1) * P],
                                 start=False, stop=True).then_inc(pv_done, 1)

            pe.sem_inc(scored_w, 1)
            pe.sem_inc(pv_done, 2)
            for tile in plan:
                scores(tile, 0, 0)
                if tile[0]:
                    turns_and_products(plan[tile[0] - 1], 3, 1)
                scores(tile, 0, 1)
                turns_and_products(tile, 0, 0)
                with pe.Fori(1, 4) as c:
                    scores(tile, c, 0)
                    turns_and_products(tile, c - 1, 1)
                    scores(tile, c, 1)
                    turns_and_products(tile, c, 0)
            turns_and_products(plan[-1], 3, 1)

        @block.scalar
        def _(act):
            def exps(tile, c, gr):
                t, wb, ng, g0 = tile
                s = 2 * c + gr + 8 * t
                act.wait_ge(pv_done, s + 1)
                for j, (done, src, dst) in enumerate((
                        (exp_s, sS[:, 0:(t + 1) * P], PR[gr][:, 0:(t + 1) * P]),
                        (exp_w, sW[:, 0:len(wb) * P], PR[gr][:, 1024:1024 + len(wb) * P]),
                        (exp_c, sW[:, CMP:CMP + NCP], PR[gr][:, 1664:1664 + NCP]))):
                    act.wait_ge(negated, 3 * s + (1, 3, 3)[j])
                    nc.scalar.activation(dst, src, ACT.Exp, bias=nm[gr][:, j:j + 1],
                                         accum_out=l[gr][:, (j + 1) % 3:(j + 1) % 3 + 1]).then_inc(done, 1)

            def copies(tile, c, gr):
                t, wb, ng, g0 = tile
                nb = t + 1 + len(wb)
                for q in range(ng):
                    act.wait_ge(pt_done, (2 * c + gr) * ng + (g0 + q + 1))
                    bank = (gr * ng + q) % 2
                    if q < ng - 1:
                        m = min(4, nb - 4 * q) * P
                        nc.scalar.activation(PT[gr][:, 512 * q:512 * q + m], tp[:, bank, 0:m], ACT.Copy).then_inc(pt_copied, 1)
                    else:
                        nc.scalar.activation(PT[gr][0:NCP, nb * P:(nb + 1) * P], tp[0:NCP, bank, 0:P], ACT.Copy).then_inc(pt_copied, 1)

            def output(tile, c):
                t = tile[0]
                act.wait_ge(pv_done, 2 * c + 8 * t + 4)
                nc.scalar.activation(k.ON[:, bass.ds(c, 1), t * P:(t + 1) * P].rearrange("p a t -> p (a t)"), op[:, 0:P],
                                     ACT.Copy).then_inc(o_copied, 1)

            for x in (exp_s, exp_w, exp_c, o_copied):
                act.sem_inc(x, 1)
            act.sem_inc(pt_copied, 2)
            for tile in plan:
                if tile[0]:
                    copies(plan[tile[0] - 1], 3, 1)
                exps(tile, 0, 0)
                if tile[0]:
                    output(plan[tile[0] - 1], 3)
                copies(tile, 0, 0)
                exps(tile, 0, 1)
                with act.Fori(1, 4) as c:
                    copies(tile, c - 1, 1)
                    exps(tile, c, 0)
                    output(tile, c - 1)
                    copies(tile, c, 0)
                    exps(tile, c, 1)
            copies(plan[-1], 3, 1)
            output(plan[-1], 3)

        @block.vector
        def _(dve):
            def queries(tile, c):
                t = tile[0]
                dve.wait_ge(scored_w, 2 * c + 8 * t + 1)
                nc.vector.tensor_copy(QB, k.Q[:, bass.ds(c, 1), t * P:(t + 1) * P].rearrange("p a t -> p (a t)")).then_inc(q_ready, 1)

            def biases_and_maxima(tile, c, gr):
                t, wb, ng, g0 = tile
                s = 2 * c + gr + 8 * t
                near = min(t + 1, 2) * P
                adds = 3 + (len(wb) == 5)
                ab = (2 * c + gr) * adds + sum(8 * (3 + (x >= 4)) for x in range(t))
                hd = bass.ds(c + 4 * gr, 1)
                nb = k.NB[:, hd, 256 - near:256].rearrange("p a j -> p (a j)")
                dve.wait_ge(scored_s, s + 1)
                x = sS[:, (t + 1) * P - near:(t + 1) * P]
                nc.vector.tensor_tensor(x, x, nb, ALU.add).then_inc(biased, 1)
                dve.wait_ge(biased, ab + 1)
                nc.vector.tensor_reduce(nm[gr][:, 0:1], sS[:, 0:(t + 1) * P], AX, ALU.max, negate=True).then_inc(negated, 1)
                dve.wait_ge(scored_w, s + 2)
                w = len(wb) * P
                x = sW[:, w - near:w]
                nc.vector.tensor_tensor(x, x, nb, ALU.add).then_inc(biased, 1)
                if len(wb) == 5:
                    nc.vector.tensor_tensor(sW[:, 0:P], sW[:, 0:P], k.WM, ALU.add).then_inc(biased, 1)
                x = sW[:, CMP:CMP + NCP]
                a = 56 - 8 * t
                nc.vector.tensor_tensor(x, x, k.BC[:, hd, a:a + NCP].rearrange("p a m -> p (a m)"), ALU.add).then_inc(biased, 1)
                dve.wait_ge(biased, ab + adds)
                nc.vector.tensor_reduce(nm[gr][:, 1:2], sW[:, 0:w], AX, ALU.max, negate=True).then_inc(negated, 1)
                nc.vector.tensor_reduce(nm[gr][:, 2:3], x, AX, ALU.max, negate=True).then_inc(negated, 1)

            def scaling(tile, c, gr):
                t, wb, ng, g0 = tile
                s = 2 * c + gr + 8 * t
                for done in (exp_s, exp_w, exp_c):
                    dve.wait_ge(done, s + 2)
                nc.vector.reciprocal(cc[gr], l[gr]).then_inc(factor, 1)
                dve.wait_ge(factor, 2 * s + 1)
                gates = k.gtok[:, t, :].rearrange("p (h r) -> p h r", r=3)[:, bass.ds(c + 4 * gr, 1), :]
                nc.vector.tensor_tensor(cc[gr], cc[gr], gates.rearrange("p a r -> p (a r)"), ALU.mult).then_inc(factor, 1)
                dve.wait_ge(factor, 2 * s + 2)
                for j, (a, w) in enumerate(((0, (t + 1) * P), (1024, len(wb) * P), (1664, NCP))):
                    x = PR[gr][:, a:a + w]
                    f = (j + 1) % 3
                    nc.vector.tensor_scalar(x, x, cc[gr][:, f:f + 1], None, ALU.mult).then_inc(p_ready, 1)

            queries(plan[0], 0)
            for tile in plan:
                if tile[0]:
                    scaling(plan[tile[0] - 1], 3, 1)
                biases_and_maxima(tile, 0, 0)
                scaling(tile, 0, 0)
                biases_and_maxima(tile, 0, 1)
                with dve.Fori(1, 4) as c:
                    queries(tile, c)
                    scaling(tile, c - 1, 1)
                    biases_and_maxima(tile, c, 0)
                    scaling(tile, c, 0)
                    biases_and_maxima(tile, c, 1)
                if tile[0] < TT - 1:
                    queries(plan[tile[0] + 1], 0)
            scaling(plan[-1], 3, 1)


def merge(k):
    nc, g, w = k.nc, k.g, k.g["w_in"]
    with Stage(k, "merge") as st:
        acc = st.psum("acc", [P, 2, NT, 512])
        mm = st.sems("gates_done branch_done")
        sig, gated, merged, slot_open, hi_done, split_done, slot_ok = st.sems(
            "sig gated merged slot_open hi_done split_done slot_ok")
        SA = chunks(k.E[:, 0:2 * N], 2)
        TM = chunks(k.E[:, 2 * N:4 * N], 2)
        base = list(k.wcount)
        k.wcount[0] += 8 * 32
        k.wcount[1] += 8 * 48
        nsa = g["w_branch_nsa"].rearrange("(gr c d) m -> gr d c m", gr=2, d=HD)
        block = st.block()

        @block.sync
        def _(sp):
            with sp.Fori(0, 8) as m:
                for j in range(2):
                    sp.wait_ge(split_done, 2 * m + j + 1)
                    sp.dma_start(k.W[:, 0, 0:8, :], weight(w, m * P + (GA0, GB0)[j])).then_inc(k.wfull[0], 16)
                    sp.wait_ge(mm[1], 2 * m + j + 1)
                    sp.sem_inc(slot_open, 1)
                    if j == 0:
                        for gr in range(2):
                            sp.dma_start(k.W[gr * HD:(gr + 1) * HD, 1, 0:4, :], nsa[gr][:, :, bass.ds(m * P, P)]).then_inc(k.wfull[1], 16)
                    else:
                        sp.dma_start(k.W[:, 1, 0:4, :], weight(g["w_branch_gm"], m * P)).then_inc(k.wfull[1], 16)

        @block.tensor
        def _(pe):
            pe.sem_inc(mm[0], 1)
            pe.sem_inc(mm[1], 1)
            with pe.Fori(0, 8) as m:
                for j in range(2):
                    pe.wait_ge(split_done, 2 * m + j + 2)
                    pe.wait_ge(sig, 2 * m + j + 2)
                    split_tile(k, acc, 0, j, k.HH, k.HL, DC).then_inc(mm[0], 1)
                    pe.wait_ge(k.wfull[1], 48 * m + base[1] + (32, 48)[j])
                    pe.wait_ge(gated, 2 * m + j + 2)
                    gemm_tile(k, acc, 1, (k.ON, k.OG)[j], 4).then_inc(mm[1], 1)

        @block.gpsimd
        def _(pool):
            pool.sem_inc(split_done, 1)
            with pool.Fori(0, 8) as m:
                for j in range(2):
                    pool.wait_ge(k.wfull[0], 32 * m + base[0] + 16 * j + 16)
                    pool.wait_ge(sig, 2 * m + j + 1)
                    pool.sem_inc(slot_ok, 1)
                    split_weights(k, pool, 0, j, DC, hi_done, 2 * m + j, split_done)

        @block.scalar
        def _(act):
            act.sem_inc(sig, 2)
            with act.Fori(0, 8) as m:
                for j in range(2):
                    act.wait_ge(mm[0], 2 * m + j + 2)
                    act.wait_ge(gated, 2 * m + j + 1)
                    nc.scalar.activation(tokens(SA[:, j, :]), acc[:, 0, :, 0:NW], ACT.Sigmoid).then_inc(sig, 1)

        @block.vector
        def _(dve):
            dve.sem_inc(gated, 2)
            dve.sem_inc(merged, 1)
            with dve.Fori(0, 8) as m:
                dve.wait_ge(merged, m + 1)
                for j in range(2):
                    dve.wait_ge(sig, 2 * m + j + 3)
                    dve.wait_ge(mm[1], 2 * m + j + 2)
                    nc.vector.tensor_tensor(tokens(TM[:, j, :]), tokens(SA[:, j, :]), acc[:, 1, :, 0:NW], ALU.mult).then_inc(gated, 1)
                dve.wait_ge(gated, 2 * m + 4)
                nc.vector.tensor_tensor(k.MT[:, bass.ds(m, 1), :].rearrange("p a t -> p (a t)"), TM[:, 0, :], TM[:, 1, :],
                                        ALU.add).then_inc(merged, 1)
            dve.wait_ge(merged, 9)


def one(ap, m):
    return tokens(ap[:, bass.ds(m, 1), :].rearrange("p a t -> p (a t)"))


def out_projection(k):
    nc, g = k.nc, k.g
    with Stage(k, "out") as st:
        acc = st.psum("acc", [P, 2, NT, 512])
        mm_done, acc_free, hi_done, split_done, slot_ok, m_hi, m_lo, x_back = st.sems(
            "mm_done acc_free hi_done split_done slot_ok m_hi m_lo x_back")
        base = list(k.wcount)
        for s in range(2):
            k.wcount[s] += 4 * 16
        block = st.block()

        @block.sync
        def _(sp):
            with sp.Fori(0, 4) as i:
                for s in range(2):
                    sp.wait_ge(split_done, 2 * i + s + 1)
                    sp.dma_start(k.W[:, s, :, :], weight(g["w_out"], (2 * i + s) * P)).then_inc(k.wfull[s], 16)
            sp.wait_ge(m_lo, DC)
            sp.dma_start(k.Z[:, 0:DC * N], k.kept).then_inc(x_back, 16)
            sp.wait_ge(x_back, 16)

        @block.gpsimd
        def _(pool):
            pool.sem_inc(split_done, 2)
            with pool.Fori(0, 4) as i:
                for s in range(2):
                    pool.wait_ge(k.wfull[s], 16 * i + base[s] + 16)
                    pool.wait_ge(mm_done, 2 * i + s + 1)
                    pool.sem_inc(slot_ok, 1)
                    split_weights(k, pool, s, s, DC, hi_done, 2 * i + s, split_done)

        @block.tensor
        def _(pe):
            pe.sem_inc(mm_done, 2)
            pe.wait_ge(m_lo, DC)
            with pe.Fori(0, 4) as i:
                for s in range(2):
                    pe.wait_ge(split_done, 2 * i + s + 3)
                    pe.wait_ge(acc_free, 2 * i + s + 1)
                    split_tile(k, acc, s, s, k.HH, k.HL, DC).then_inc(mm_done, 1)

        @block.scalar
        def _(act):
            act.sem_inc(acc_free, 2)
            for c in range(DC):
                nc.scalar.activation(k.HH[:, c, :], k.MT[:, c, :], ACT.Copy).then_inc(m_hi, 1)
            with act.Fori(0, 4) as i:
                for s in range(2):
                    act.wait_ge(mm_done, 2 * i + s + 3)
                    nc.scalar.activation(one(k.MX, 2 * i + s), acc[:, s, :, 0:NW], ACT.Copy).then_inc(acc_free, 1)
            act.wait_ge(acc_free, 10)

        @block.vector
        def _(dve):
            for c in range(DC):
                dve.wait_ge(m_hi, c + 1)
                nc.vector.tensor_tensor(k.HL[:, c, :], k.MT[:, c, :], k.HH[:, c, :].bitcast(F32), ALU.subtract).then_inc(m_lo, 1)


def ffn(k, part):
    nc, g = k.nc, k.g
    nf = FFN_PARTS[part]
    at = sum(FFN_PARTS[:part]) * P
    last_part = part == len(FFN_PARTS) - 1
    with Stage(k, f"ffn{part}") as st:
        acc = st.psum("acc", [P, 2, NT, 512])
        gate_done, up_done, silu_done, gated, down_done, acc_free, hi_done, split_done, slot_ok, a_hi, a_lo, x_back = st.sems(
            "gate_done up_done silu_done gated down_done acc_free hi_done split_done slot_ok a_hi a_lo x_back")
        done = (gate_done, up_done)
        free = (silu_done, gated)
        SL = k.E[:, 0:N]
        GU = k.E[:, N:2 * N]
        base = list(k.wcount)
        for s in range(2):
            k.wcount[s] += (nf + 4) * 16
        block = st.block()

        @block.sync
        def _(sp):
            with sp.Fori(0, nf) as m:
                for s in range(2):
                    sp.wait_ge(split_done, 2 * m + s + 1)
                    sp.dma_start(k.W[:, s, :, :], weight(g[("w_ffn_gate", "w_ffn_up")[s]], m * P + at)).then_inc(k.wfull[s], 16)
            with sp.Fori(0, 4) as i:
                for s in range(2):
                    sp.wait_ge(split_done, 2 * i + s + 1 + 2 * nf)
                    sp.dma_start(k.W[:, s, 0:nf, :], weight(g["w_ffn_down"][at:at + nf * P, :], (2 * i + s) * P)).then_inc(k.wfull[s], 16)
            if last_part:
                sp.wait_ge(gate_done, nf + 1)
                sp.wait_ge(up_done, nf + 1)
                sp.dma_start(k.X[:].rearrange("p c t -> p (c t)"), k.kept).then_inc(x_back, 16)
                sp.wait_ge(x_back, 16)

        @block.gpsimd
        def _(pool):
            pool.sem_inc(split_done, 2)
            with pool.Fori(0, nf) as m:
                for s in range(2):
                    pool.wait_ge(k.wfull[s], 16 * m + base[s] + 16)
                    pool.wait_ge(done[s], m + 1)
                    pool.sem_inc(slot_ok, 1)
                    split_weights(k, pool, s, s, DC, hi_done, 2 * m + s, split_done)
            for s in range(2):
                pool.wait_ge(done[s], nf + 1)
            with pool.Fori(0, 4) as i:
                for s in range(2):
                    pool.wait_ge(k.wfull[s], 16 * i + base[s] + nf * 16 + 16)
                    pool.wait_ge(down_done, 2 * i + s + 1)
                    pool.sem_inc(slot_ok, 1)
                    split_weights(k, pool, s, s, nf, hi_done, 2 * i + s + 2 * nf, split_done)

        @block.tensor
        def _(pe):
            pe.sem_inc(gate_done, 1)
            pe.sem_inc(up_done, 1)
            pe.sem_inc(down_done, 2)
            with pe.Fori(0, nf) as m:
                for s in range(2):
                    pe.wait_ge(split_done, 2 * m + s + 3)
                    pe.wait_ge(free[s], m + 1)
                    split_tile(k, acc, s, s, k.HH, k.HL, DC).then_inc(done[s], 1)
            for s in range(2):
                pe.wait_ge(free[s], nf + 1)
            pe.wait_ge(a_lo, nf + 1)
            with pe.Fori(0, 4) as i:
                for s in range(2):
                    pe.wait_ge(split_done, 2 * i + s + 3 + 2 * nf)
                    pe.wait_ge(acc_free, 2 * i + s + 1)
                    split_tile(k, acc, s, s, k.AH, k.AL, nf).then_inc(down_done, 1)

        @block.scalar
        def _(act):
            act.sem_inc(silu_done, 1)
            with act.Fori(0, nf) as m:
                act.wait_ge(gate_done, m + 2)
                act.wait_ge(gated, m + 1)
                nc.scalar.activation(tokens(SL), acc[:, 0, :, 0:NW], ACT.Silu).then_inc(silu_done, 1)
                act.wait_ge(gated, m + 2)
                nc.scalar.activation(one(k.AH, m), tokens(GU), ACT.Copy).then_inc(a_hi, 1)
            if part == 0:
                act.sem_inc(acc_free, 2)
                with act.Fori(0, 4) as i:
                    for s in range(2):
                        act.wait_ge(down_done, 2 * i + s + 3)
                        nc.scalar.activation(one(k.F, 2 * i + s), acc[:, s, :, 0:NW], ACT.Copy).then_inc(acc_free, 1)
                act.wait_ge(acc_free, 10)

        @block.vector
        def _(dve):
            dve.sem_inc(gated, 1)
            dve.sem_inc(a_lo, 1)
            with dve.Fori(0, nf) as m:
                dve.wait_ge(silu_done, m + 2)
                dve.wait_ge(up_done, m + 2)
                dve.wait_ge(a_lo, m + 1)
                nc.vector.tensor_tensor(tokens(GU), tokens(SL), acc[:, 1, :, 0:NW], ALU.mult).then_inc(gated, 1)
                dve.wait_ge(a_hi, m + 1)
                nc.vector.tensor_tensor(one(k.AL, m), tokens(GU), one(k.AH, m).bitcast(F32), ALU.subtract).then_inc(a_lo, 1)
            if part:
                dve.sem_inc(acc_free, 2)
                with dve.Fori(0, 4) as i:
                    for s in range(2):
                        dve.wait_ge(down_done, 2 * i + s + 3)
                        nc.vector.tensor_tensor(one(k.F, 2 * i + s), one(k.F, 2 * i + s), acc[:, s, :, 0:NW],
                                                ALU.add).then_inc(acc_free, 1)
                dve.wait_ge(acc_free, 10)


def ple(k):
    nc, g = k.nc, k.g
    with Stage(k, "ple") as st:
        acc = st.psum("acc", [P, 2, NT, 512])
        tp = st.psum("tp", [P, 2, 512])
        p_in, tr_done, tr_copied, gate_done, e_done, sig, gated, hi_done, split_done, slot_ok, x_hi, x_lo = st.sems(
            "p_in tr_done tr_copied gate_done e_done sig gated hi_done split_done slot_ok x_hi x_lo")
        ptok = k.E[:, 2 * N:2 * N + 9 * 256].rearrange("p (t f) -> p t f", f=256)
        pT = chunks(k.Z[:, 8 * N:10 * N], 2)
        SA = k.E[:, 0:N]
        base = list(k.wcount)
        for s in range(2):
            k.wcount[s] += 8 * 16
        block = st.block()

        @block.sync
        def _(sp):
            sp.dma_start(ptok[:, 0:TT, :], g["p_prompt"].rearrange("(t p) f -> p t f", p=P)).then_inc(p_in, 16)
            sp.dma_start(ptok[0:B, TT, :], g["p_sample"]).then_inc(p_in, 16)
            with sp.Fori(0, 8) as m:
                sp.wait_ge(split_done, m + 1)
                sp.dma_start(k.W[:, 0, 0:8, :], weight(g["w_ple_gate"], m * P)).then_inc(k.wfull[0], 16)
                sp.wait_ge(e_done, m + 1)
                sp.dma_start(k.W[:, 1, 0:2, :], weight(g["w_ple"], m * P)).then_inc(k.wfull[1], 16)

        @block.tensor
        def _(pe):
            pe.sem_inc(gate_done, 1)
            pe.sem_inc(e_done, 1)
            pe.wait_ge(p_in, 32)
            for c in range(2):
                for q in range(3):
                    n = 3 * c + q
                    if n >= 2:
                        pe.wait_ge(tr_copied, n - 1)
                    if q < 2:
                        for t in range(4):
                            last = nc.tensor.transpose(tp[:, n % 2, t * P:(t + 1) * P], ptok[:, 4 * q + t, c * P:(c + 1) * P], k.ident[:])
                    else:
                        last = nc.tensor.transpose(tp[:, n % 2, 0:B], ptok[0:B, TT, c * P:(c + 1) * P], k.ident[0:B, 0:B])
                    last.then_inc(tr_done, 1)
            pe.wait_ge(tr_copied, 6)
            pe.wait_ge(x_lo, DC)
            with pe.Fori(0, 8) as m:
                pe.wait_ge(split_done, m + 2)
                pe.wait_ge(sig, m + 1)
                split_tile(k, acc, 0, 0, k.HH, k.XL, DC).then_inc(gate_done, 1)
                pe.wait_ge(k.wfull[1], 16 * m + base[1] + 16)
                pe.wait_ge(gated, m + 1)
                gemm_tile(k, acc, 1, pT, 2).then_inc(e_done, 1)

        @block.gpsimd
        def _(pool):
            pool.sem_inc(split_done, 1)
            with pool.Fori(0, 8) as m:
                pool.wait_ge(k.wfull[0], 16 * m + base[0] + 16)
                pool.wait_ge(gate_done, m + 1)
                pool.sem_inc(slot_ok, 1)
                split_weights(k, pool, 0, 0, DC, hi_done, m, split_done)

        @block.scalar
        def _(act):
            act.sem_inc(sig, 1)
            for c in range(DC):
                nc.scalar.activation(k.HH[:, c, :], k.X[:, c, :], ACT.Copy).then_inc(x_hi, 1)
            with act.Fori(0, 8) as m:
                act.wait_ge(gate_done, m + 2)
                act.wait_ge(gated, m + 1)
                nc.scalar.activation(tokens(SA), acc[:, 0, :, 0:NW], ACT.Sigmoid).then_inc(sig, 1)

        @block.vector
        def _(dve):
            dve.sem_inc(gated, 1)
            for c in range(DC):
                dve.wait_ge(x_hi, c + 1)
                nc.vector.tensor_tensor(k.XL[:, c, :], k.X[:, c, :], k.HH[:, c, :].bitcast(F32), ALU.subtract).then_inc(x_lo, 1)
            for c in range(2):
                for q in range(3):
                    n = 3 * c + q
                    dve.wait_ge(tr_done, n + 1)
                    a, w = (q * 512, 512) if q < 2 else (T, B)
                    nc.vector.tensor_copy(pT[:, c, a:a + w], tp[:, n % 2, 0:w]).then_inc(tr_copied, 1)
            with dve.Fori(0, 8) as m:
                dve.wait_ge(sig, m + 2)
                dve.wait_ge(e_done, m + 2)
                nc.vector.tensor_tensor(one(k.F, m), tokens(SA), acc[:, 1, :, 0:NW], ALU.mult).then_inc(gated, 1)
            dve.wait_ge(gated, 9)


def store_y(k):
    nc = k.nc
    with Stage(k, "store") as st:
        ps = st.psum("ps", [P, 4, 1024])
        turned, copied, stores = st.sems("turned copied stores")
        yt = k.Z[:, 0:9 * D].rearrange("p (t f) -> p t f", f=D)
        block = st.block()

        @block.tensor
        def _(pe):
            for t in range(9):
                m = P if t < TT else B
                if t >= 4:
                    pe.wait_ge(copied, t - 3)
                for c in range(DC):
                    last = nc.tensor.transpose(ps[0:m, t % 4, c * P:(c + 1) * P], k.X[:, c, t * P:t * P + m], k.ident[:])
                last.then_inc(turned, 1)

        @block.vector
        def _(dve):
            for t in range(9):
                m = P if t < TT else B
                dve.wait_ge(turned, t + 1)
                nc.vector.tensor_copy(yt[0:m, t, :], ps[0:m, t % 4, :]).then_inc(copied, 1)

        @block.sync
        def _(sp):
            for t in range(9):
                sp.wait_ge(copied, t + 1)
                if t < TT:
                    sp.dma_start(k.out["y_p"][t * P:(t + 1) * P, :], yt[:, t, :]).then_inc(stores, 16)
                else:
                    sp.dma_start(k.out["y_s"], yt[0:B, TT, :]).then_inc(stores, 16)
            sp.wait_ge(stores, 9 * 16)


def _bucket(dist):
    import numpy as np
    dist = np.asarray(dist)
    near = np.maximum(dist, 0)
    ratio = np.log(np.maximum(near, 1).astype(np.float32) / np.float32(16)) / np.float32(np.log(128 / 16))
    large = np.minimum(16 + (ratio * 16).astype(np.int32), 31)
    return np.where(dist < 0, 32, np.where(near < 16, near, large))


def _one_hot(dist):
    import numpy as np
    b = _bucket(dist)
    return np.ascontiguousarray((np.arange(33).reshape((33,) + (1,) * b.ndim) == b[None]).astype(np.float32))


def _constants():
    import numpy as np
    f = np.float32
    i, j = np.arange(128)[:, None], np.arange(128)[None, :]
    n33 = np.arange(33)
    row = np.arange(64)
    kk = np.arange(24)
    ci, sj = np.arange(127)[:, None] * 16, n33[None, :] * 64
    r, n = np.arange(16)[:, None], np.arange(120, 128)[None, :]
    wr, wn = np.arange(4)[:, None], np.arange(128)[None, :]
    smp = np.concatenate([2048 - (16 * np.arange(127) + 31), [0], (2048 - 16 * n - r).ravel(), (512 - 4 * wn - wr).ravel()])
    m = np.arange(48, 63)
    return {
        "eye": np.eye(128, dtype=f),
        "sixteenth": (np.arange(128) % 8).astype(np.int32)[:, None],
        "upper": (i <= j).astype(f),
        "oh_samples": _one_hot(smp),
        "oh_near": _one_hot(255 - np.arange(384)),
        "oh_cmp": _one_hot(np.arange(128)[None, :] - 16 * (m[:, None] - 56) - 31).reshape(33, 15 * 128),
        "overlap": ((ci <= sj + 63) & (ci + 31 >= sj)).astype(f),
        "same_group": (row[:, None] // 4 == row[None, :] // 4).astype(f),
        "before": (n33[None, :] < n33[:, None]).astype(f).reshape(1, 33 * 33),
        "head_of": (kk[:, None] // 3 == np.arange(8)[None, :]).astype(f),
        "branch_of": (kk[:, None] % 3 == np.arange(3)[None, :]).astype(f),
        "window_edge": np.where(j >= i, 0, -1e30).astype(f),
        "has_block": (np.arange(128) >= 31).astype(f)[:, None],
    }


_VIEWS = {
    "x_prompt": (1024, 1024), "x_sample": (8, 1024), "cache_cmp_kv": (160 * 8, 4096), "cache_slc_kv": (160 * 8, 4096),
    "state_win_kv": (8, 512, 256), "page_table": (8, 16), "p_prompt": (1024, 256), "p_sample": (8, 256),
    "rel_bias": (32, 8), "ln_mix_pre": (1, 1024), "w_in": (1024, 4376), "cmp_pe_k": (1, 2048), "cmp_w1_k": (2048, 128),
    "cmp_w2_k": (128, 64), "cmp_pe_v": (1, 2048), "cmp_w1_v": (2048, 128), "cmp_w2_v": (128, 64), "gm_ln_g": (1, 512),
    "gm_ln_b": (1, 512), "gm_ws": (512, 128), "gm_bs": (4, 128), "w_branch_nsa": (512, 1024), "w_branch_gm": (512, 1024),
    "w_out": (1024, 1024), "ln_mix_post": (1, 1024), "ln_ffn_pre": (1, 1024), "w_ffn_gate": (1024, 2816),
    "w_ffn_up": (1024, 2816), "w_ffn_down": (2816, 1024), "ln_ffn_post": (1, 1024), "w_ple": (256, 1024),
    "w_ple_gate": (1024, 1024), "ln_ple_post": (1, 1024),
}
_OUTS = [
    ("y_p", (1024, 1024), (1, 1024, 1024)), ("y_s", (8, 1024), (8, 1, 1024)),
    ("cmp_p", (1024, 256), (1, 1, 1024, 2, 2, 64)), ("slc_p", (1024, 256), (1, 1, 1024, 2, 2, 64)),
    ("win_p", (512, 256), (1, 1, 512, 2, 2, 64)), ("cmp_s", (8, 256), (1, 8, 1, 2, 2, 64)),
    ("slc_s", (8, 256), (1, 8, 1, 2, 2, 64)), ("win_s", (8, 512, 256), (1, 8, 512, 2, 2, 64)),
    ("gm_v", (8, 512), (1, 8, 1, 512)),
]


def kernel(**inputs):
    import numpy as _np
    import concourse.bacc as _bacc
    from concourse import mybir as _mybir
    from concourse.bass_utils import run_bass_kernel_spmd as _run

    nc = _bacc.Bacc("TRN2", target_bir_lowering=False, num_devices=1)
    arrays, g, out = {}, {}, {}
    data = {n: _np.ascontiguousarray(inputs[n]).reshape(s) for n, s in _VIEWS.items()}
    data.update(_constants())
    for n, a in data.items():
        arrays[f"in_{n}"] = a
        g[n] = nc.dram_tensor(f"in_{n}", a.shape, _mybir.dt.from_np(a.dtype), kind="ExternalInput").ap()
    for n, shape, _ in _OUTS:
        out[n] = nc.dram_tensor(f"out_{n}", shape, _mybir.dt.float32, kind="ExternalOutput").ap()
    scratch = nc.dram_tensor("bias_rows", (8, 128 * 384), _mybir.dt.float32, kind="Internal").ap()
    kept = nc.dram_tensor("kept_x", (128, 8 * 1032), _mybir.dt.float32, kind="Internal").ap()
    build(nc, g, out, scratch, kept)
    r = _run(nc, [arrays], core_ids=[0])
    return tuple(_np.asarray(r.results[0][f"out_{n}"]).reshape(full) for n, _, full in _OUTS)
```

```python
from contextlib import ExitStack

import concourse.bass as bass
from concourse import mybir

F32 = mybir.dt.float32
F32R = mybir.dt.float32r
I32 = mybir.dt.int32
ALU = mybir.AluOpType
ACT = mybir.ActivationFunctionType
AX = mybir.AxisListType.X

P = 128
D = 1024
T = 1024
B = 8
N = T + B
NT = 3
NW = N // NT
DC = D // P
TT = T // P
FFN_PARTS = (6, 6, 5, 5)
FP = max(FFN_PARTS)
KV = 768
H = 8
HD = 64
NCP = 63
NCS = 127
NSEL = 33
TOPK = 16
EPS = 1e-6
NEG = -1e30
FORCE = 1e6
Q0, KV0, GATE0, U0, V0, GA0, GB0 = 0, 512, 1280, 1304, 1816, 2328, 3352
GM = 512
OH_CMP, OH_SELF, OH_WIN = 0, NCS, NCS + B
OH_SLC = OH_WIN + 512
OH_ALL = OH_SLC + 2048


def tokens(ap):
    return ap.rearrange("p (n w) -> p n w", n=NT)


def chunks(ap, n):
    return ap.rearrange("p (c t) -> p c t", c=n)


class Core:
    pass


class Stage:

    def __init__(self, k, name):
        self.k, self.name, self.stack, self.mine = k, name, ExitStack(), []

    def __enter__(self):
        self.stack.__enter__()
        return self

    def sems(self, names):
        new = [self.k.nc.alloc_semaphore(f"{self.name}_{n}") for n in names.split()]
        self.mine += new
        return new

    def psum(self, what, shape):
        return self.stack.enter_context(self.k.nc.psum_tensor(f"{self.name}_{what}", shape, F32))

    def block(self):
        return self.stack.enter_context(self.k.nc.Block())

    def __exit__(self, *a):
        self.stack.__exit__(*a)
        self.k.used += self.mine


def build(nc, g, out, scratch, kept):
    with ExitStack() as ctx:
        k = Core()
        k.nc, k.g, k.out, k.scratch, k.kept = nc, g, out, scratch, kept

        def sb(name, shape, dt=F32):
            return ctx.enter_context(nc.sbuf_tensor(name, shape, dt))

        base = -(-nc.sbuf_base // 32) * 32
        sizes = {"X": DC * N, "H": DC * N, "Z": 21360, "W": 2048, "CW": 4096}
        sb("slab", [P, sum(sizes.values()) + 8])
        start, at = {}, base
        for n, words in sizes.items():
            start[n] = at
            at += 4 * words

        def place(name, region, shape, dt=F32, skip=0):
            return nc.alloc_sbuf_tensor_at(name, shape, dt, offset=start[region] + 4 * skip)

        k.X = place("X", "X", [P, DC, N])
        k.HL = place("HL", "X", [P, DC, N], F32R)
        k.Hr = place("Hr", "H", [P, DC * N])
        k.HH = place("HH", "H", [P, DC, N], F32R)
        k.Z = place("Z", "Z", [P, 21360])
        k.AH = place("AH", "Z", [P, FP, N], F32R)
        k.AL = place("AL", "Z", [P, FP, N], F32R, FP * N)
        k.XL = place("XL", "Z", [P, DC, N], F32R)
        k.W = place("W", "W", [P, 2, DC, P])
        k.CW = place("CW", "CW", [P, 4096])
        k.WS = place("WS", "CW", [P, 2, 2, DC, P], F32R)
        k.E = sb("E", [P, 5632])
        k.R1 = sb("R1", [P, N])
        k.ident = sb("ident", [P, P])
        k.ones = sb("ones", [P, P])
        k.gains = sb("gains", [P, 5, DC])
        k.gtok = sb("gtok", [P, TT, 24])
        k.gfm = sb("gfm", [24, B])
        k.pid = sb("pid", [P, B], I32)
        k.relb = sb("relb", [33, H])
        k.tiny = sb("tiny", [P, 16])
        k.kvtok = k.Z[:, 0:9 * KV].rearrange("p (t f) -> p t f", f=KV)
        o = 9 * KV
        k.Q = chunks(k.Z[:, o:o + 4 * N], 4)
        k.KT3 = chunks(k.Z[:, o + 3 * N:o + 6 * N], 3)
        o += 4 * N
        k.KT = chunks(k.Z[:, o:o + 2 * N], 2)
        o += 2 * N
        k.OG = chunks(k.Z[:, o:o + 4 * N], 4)
        o += 4 * N
        k.ON = chunks(k.Z[:, o:o + 4 * N], 4)
        k.ONr = k.Z[:, o:o + 4 * N]
        k.MT = chunks(k.Z[:, 0:8 * N], 8)
        k.MX = chunks(k.Z[:, 8 * N:16 * N], 8)
        k.F = chunks(k.Z[:, 2 * FP * N:(2 * FP + 8) * N], 8)
        k.sq = chunks(k.E[:, 2 * N:4 * N], 2)
        k.ssq = k.E[:, 4 * N:5 * N]
        k.wfull = [ctx.enter_context(nc.semaphore(f"weights_full_{i}")) for i in range(2)]
        k.wcount = [0, 0]
        k.vtok = k.E[:, 0:9 * GM].rearrange("p (t f) -> p t f", f=GM)
        k.KC = k.E[:, 0:9 * P].rearrange("p (b n) -> p b n", b=9)
        k.VC = k.E[:, 9 * P:18 * P].rearrange("p (b n) -> p b n", b=9)
        k.QS8 = k.Hr[:, 8192:8256].rearrange("p (b h) -> p b h", b=B)
        k.OC = k.E[:, 5176:5240].rearrange("p (b h) -> p b h", b=B)
        k.BB = k.ON[:, 0:2, 0:704]
        k.S = samples(k.ONr[:, 2 * N:2 * N + 704])
        k.unit = k.ONr[:, 704:832]
        k.GT = k.ONr[:, 832:960]
        k.cmp_past = [k.ONr[:, 0:4096], k.Hr[:, 0:4096]]
        k.w1 = k.CW[:].rearrange("p (kv c m) -> p kv c m", kv=2, c=16)
        k.cmp_gathered = [ctx.enter_context(nc.semaphore(f"cmp_gathered_{i}")) for i in range(2)]
        k.w1_in = ctx.enter_context(nc.semaphore("w1_in"))
        k.kv_stored = ctx.enter_context(nc.semaphore("kv_stored"))
        xr = k.X[:].rearrange("p c t -> p (c t)")
        k.past = [x[:, 4096 * i:4096 * (i + 1)] for x in (xr, k.Hr) for i in range(2)]
        k.gathered = [ctx.enter_context(nc.semaphore(f"gathered_{i}")) for i in range(4)]
        k.NB = k.E[:, 2304:4352].rearrange("p (h j) -> p h j", h=H)
        k.BC = k.E[:, 4352:5304].rearrange("p (h m) -> p h m", h=H)
        k.WM = k.E[:, 5304:5432]
        k.used = []
        load_x(k)
        norm_stage(k, "norm1", k.X, spill=True)
        project_kv(k)
        project_quv(k)
        spatial_gate(k)
        compress(k)
        forget_semaphores(k)
        select_blocks(k)
        sample_attention(k)
        bias_tables(k)
        prompt_attention(k)
        forget_semaphores(k)
        merge(k)
        out_projection(k)
        norm_stage(k, "mix_post", k.MX, residual=1, onto=k.MT, known=True)
        norm_stage(k, "ffn_pre", k.X, spill=True)
        ffn(k)
        norm_stage(k, "ffn_post", k.F, residual=3, onto=k.X, known=True)
        ple(k)
        norm_stage(k, "ple_post", k.F, residual=4, onto=k.X, known=True)
        store_y(k)


def load_x(k):
    nc, g = k.nc, k.g
    with Stage(k, "load") as st:
        xtok = k.Z[:, 0:9 * D].rearrange("p (t f) -> p t f", f=D)
        ps = st.psum("ps", [P, 4, 1024])
        x_in = st.sems(" ".join(f"x_in_{t}" for t in range(9)))
        eye_in, const_in, ones_set, transposed, copied_even, copied_odd, rel_in, rel_sub, pid_in, pid_mul = st.sems(
            "eye_in const_in ones_set transposed copied_even copied_odd rel_in rel_sub pid_in pid_mul")
        pid1 = st.stack.enter_context(nc.sbuf_tensor("pid1", [P, B + 1], I32))
        far = st.stack.enter_context(nc.sbuf_tensor("far", [32, H], F32))
        copied = (copied_even, copied_odd)
        block = st.block()

        @block.sync
        def _(sp):
            sp.dma_start(k.ident[:], g["eye"]).then_inc(eye_in, 16)
            for t in range(TT):
                sp.dma_start(xtok[:, t, :], g["x_prompt"][t * P:(t + 1) * P, :]).then_inc(x_in[t], 16)
            sp.dma_start(xtok[0:B, TT, :], g["x_sample"]).then_inc(x_in[TT], 16)
            for i, n in enumerate(("ln_mix_pre", "ln_mix_post", "ln_ffn_pre", "ln_ffn_post", "ln_ple_post")):
                sp.dma_start(k.gains[:, i, :], g[n].rearrange("a (c p) -> p (a c)", p=P),
                             allow_slow_non_contiguous=True).then_inc(const_in, 16)
            sp.wait_ge(const_in, 5 * 16)

        @block.scalar
        def _(act):
            act.dma_start(k.relb[0:32, :], g["rel_bias"]).then_inc(rel_in, 16)
            act.dma_start(far[:], g["rel_bias"][31:32, :].to_broadcast([32, H])).then_inc(rel_in, 16)
            for i in range(16):
                act.dma_start(pid1[8 * i:8 * i + 8, 0:B],
                              g["page_table"][:, i:i + 1].rearrange("b i -> i b").to_broadcast([8, B]),
                              allow_slow_non_contiguous=True).then_inc(pid_in, 16)
            act.dma_start(pid1[:, B:B + 1], g["sixteenth"]).then_inc(pid_in, 16)
            for t in range(1, 9, 2):
                act.wait_ge(transposed, t + 1)
                nc.scalar.activation(k.X[:, :, t * P:(t + 1) * P], ps[:, t % 4].rearrange("p (c t) -> p c t", c=DC),
                                     ACT.Copy).then_inc(copied_odd, 1)
            act.wait_ge(copied_odd, 4)

        @block.gpsimd
        def _(pool):
            pool.wait_ge(pid_in, 17 * 16)
            nc.gpsimd.tensor_scalar(pid1[:, 0:B], pid1[:, 0:B], 8, None, ALU.mult).then_inc(pid_mul, 1)
            pool.wait_ge(pid_mul, 1)
            nc.gpsimd.tensor_tensor(k.pid[:], pid1[:, 0:B], pid1[:, B:B + 1].to_broadcast([P, B]),
                                    ALU.add).then_inc(pid_mul, 1)
            pool.wait_ge(pid_mul, 2)

        @block.tensor
        def _(pe):
            pe.wait_ge(eye_in, 16)
            for t in range(9):
                m = P if t < TT else B
                pe.wait_ge(x_in[t], 16)
                if t >= 4:
                    pe.wait_ge(copied[t % 2], t // 2 - 1)
                for c in range(DC):
                    last = nc.tensor.transpose(ps[:, t % 4, c * P:c * P + m], xtok[0:m, t, c * P:(c + 1) * P],
                                               k.ident[0:m, 0:m])
                last.then_inc(transposed, 1)

        @block.vector
        def _(dve):
            nc.vector.memset(k.ones[:], 1.0 / D).then_inc(ones_set, 1)
            nc.vector.memset(k.relb[32:33, :], NEG).then_inc(ones_set, 1)
            for t in range(0, 9, 2):
                m = P if t < TT else B
                dve.wait_ge(transposed, t + 1)
                nc.vector.tensor_copy(k.X[:, :, t * P:t * P + m],
                                      ps[:, t % 4].rearrange("p (c t) -> p c t", c=DC)[:, :, 0:m]).then_inc(copied_even, 1)
            dve.wait_ge(rel_in, 32)
            nc.vector.tensor_tensor(k.relb[0:32, :], k.relb[0:32, :], far[:], ALU.subtract).then_inc(rel_sub, 1)
            dve.wait_ge(rel_sub, 1)
            dve.wait_ge(ones_set, 2)
            dve.wait_ge(copied_even, 5)


def forget_semaphores(k):
    k.nc.clear_and_free_semaphores(k.used)
    k.nc.all_engine_barrier()
    k.used = []


class SquareSum:

    def __init__(self, k, st):
        self.k = k
        self.go, self.squared, self.summed = st.sems("ssq_go ssq_squared ssq_summed")

    def start(self, dve):
        dve.sem_inc(self.summed, 1)
        dve.wait_ge(self.summed, 1)
        self.k.nc.vector.memset(self.k.ssq, 0.0).then_inc(self.summed, 1)

    def square(self, act, chunk, m, s):
        act.wait_ge(self.summed, m + 1)
        act.sem_inc(self.go, 1)
        self.k.nc.scalar.activation(tokens(self.k.sq[:, s, :]), chunk, ACT.Square).then_inc(self.squared, 1)

    def add(self, dve, m, s):
        k = self.k
        dve.wait_ge(self.squared, m + 1)
        dve.wait_ge(self.summed, m + 2)
        k.nc.vector.tensor_tensor(k.ssq, k.ssq, k.sq[:, s, :], ALU.add).then_inc(self.summed, 1)


def norm_stage(k, name, src, residual=None, onto=None, spill=False, known=False):
    nc = k.nc
    with Stage(k, name) as st:
        ps = st.psum("ps", [P, NT, 512])
        squared, summed, mean, inverse, root, scaled, added_pool, added, spilled = st.sems(
            "squared summed mean inverse root scaled added_pool added spilled")
        sq, ssq = k.sq, k.ssq
        rstd = k.R1[:] if name == "norm1" else k.E[:, 0:N]
        ring = chunks(k.E[:, N:5 * N], 4)
        on_pool = (0, 2, 3, 5, 6)

        def adds_before(c, pool):
            return sum((x in on_pool) == pool for x in range(c + 1))

        block = st.block()

        @block.sync
        def _(sp):
            if spill:
                sp.dma_start(k.kept, k.X[:].rearrange("p c t -> p (c t)")).then_inc(spilled, 16)
                sp.wait_ge(spilled, 16)

        @block.scalar
        def _(act):
            for c in range(0 if known else DC):
                if c >= 2:
                    act.wait_ge(summed, c - 1)
                nc.scalar.activation(sq[:, c % 2, :], src[:, c, :], ACT.Square).then_inc(squared, 1)
            act.wait_ge(inverse, 2)
            nc.scalar.activation(rstd, rstd, ACT.Sqrt).then_inc(root, 1)

        @block.tensor
        def _(pe):
            if not known:
                pe.wait_ge(summed, DC)
            for n in range(NT):
                last = nc.tensor.matmul(ps[:, n, 0:NW], k.ones[:], ssq[:, n * NW:(n + 1) * NW], start=True, stop=True)
            last.then_inc(mean, 1)

        @block.vector
        def _(dve):
            for c in range(0 if known else DC):
                dve.wait_ge(squared, c + 1)
                if c == 0:
                    nc.vector.tensor_copy(ssq, sq[:, 0, :]).then_inc(summed, 1)
                else:
                    dve.wait_ge(summed, c)
                    nc.vector.tensor_tensor(ssq, ssq, sq[:, c % 2, :], ALU.add).then_inc(summed, 1)
            dve.wait_ge(mean, 1)
            nc.vector.tensor_scalar(tokens(rstd), ps[:, :, 0:NW], EPS, None, ALU.add).then_inc(inverse, 1)
            dve.wait_ge(inverse, 1)
            nc.vector.reciprocal(rstd, rstd).then_inc(inverse, 1)
            dve.wait_ge(root, 1)
            if residual is None:
                return
            gain = k.gains[:, residual, :]

            def add(c):
                dve.wait_ge(scaled, c + 1)
                nc.vector.tensor_tensor(k.X[:, c, :], onto[:, c, :], ring[:, c % 4, :], ALU.add).then_inc(added, 1)

            for c in range(DC):
                if c >= 4:
                    if c - 4 in on_pool:
                        dve.wait_ge(added_pool, adds_before(c - 4, True))
                    else:
                        dve.wait_ge(added, adds_before(c - 4, False))
                nc.vector.scalar_tensor_tensor(out=ring[:, c % 4, :], in0=src[:, c, :], scalar=gain[:, c:c + 1],
                                               in1=rstd, op0=ALU.mult, op1=ALU.mult).then_inc(scaled, 1)
                if c and c - 1 not in on_pool:
                    add(c - 1)
            add(DC - 1)
            dve.wait_ge(added, DC - len(on_pool))

        @block.gpsimd
        def _(pool):
            if residual is not None:
                for n, c in enumerate(on_pool):
                    pool.wait_ge(scaled, c + 1)
                    nc.gpsimd.tensor_tensor(k.X[:, c, :], onto[:, c, :], ring[:, c % 4, :], ALU.add).then_inc(added_pool, 1)
                pool.wait_ge(added_pool, len(on_pool))


class NormSplit:

    def __init__(self, k, st, gain, rstd):
        self.k, self.gain, self.rstd = k, gain, rstd
        self.scaled, self.hi_done, self.lo_done = st.sems("h_scaled h_hi h_lo")
        self.ring = chunks(k.E[:, 2 * N:5 * N], 3)

    def vector(self, dve):
        k, nc = self.k, self.k.nc

        def scale(c):
            if c >= 3:
                dve.wait_ge(self.lo_done, c - 2)
            nc.vector.scalar_tensor_tensor(out=self.ring[:, c % 3, :], in0=k.X[:, c, :], scalar=k.gains[:, self.gain, c:c + 1],
                                           in1=self.rstd, op0=ALU.mult, op1=ALU.mult).then_inc(self.scaled, 1)

        scale(0)
        scale(1)
        for c in range(DC):
            dve.wait_ge(self.hi_done, c + 1)
            nc.vector.tensor_tensor(k.HL[:, c, :], self.ring[:, c % 3, :], k.HH[:, c, :].bitcast(F32),
                                    ALU.subtract).then_inc(self.lo_done, 1)
            if c + 2 < DC:
                scale(c + 2)

    def scalar(self, act):
        for c in range(DC):
            act.wait_ge(self.scaled, c + 1)
            self.k.nc.scalar.activation(self.k.HH[:, c, :], self.ring[:, c % 3, :], ACT.Copy).then_inc(self.hi_done, 1)


def weight(ap, at, cols=P):
    return ap[:, bass.ds(at, cols)].rearrange("(c p) m -> p c m", p=P)


def gemm_tile(k, acc, s, src, nk):
    for c in range(nk):
        for n in range(NT):
            last = k.nc.tensor.matmul(acc[:, s, n, 0:NW], k.W[:, s, c, :], src[:, c, n * NW:(n + 1) * NW],
                                      start=(c == 0), stop=(c == nk - 1))
    return last


def split_tile(k, acc, s, ws, hi, lo, nk, first=0, more=False, wait=None):
    for c in range(first, nk):
        if wait is not None:
            wait[0].wait_ge(wait[1], c + 1)
        for part, src in ((0, hi), (0, lo), (1, hi)):
            for n in range(NT):
                last = k.nc.tensor.matmul(acc[:, s, n, 0:NW], k.WS[:, ws, part, c, :], src[:, c, n * NW:(n + 1) * NW],
                                          start=(c == 0 and part == 0 and src is hi), stop=(c == nk - 1 and part == 1 and not more))
    return last


def split_weights(k, pool, s, ws, nk, hi_done, count, split_done):
    w = k.W[:, s, 0:nk, :]
    k.nc.gpsimd.tensor_copy(k.WS[:, ws, 0, 0:nk, :], w).then_inc(hi_done, 1)
    pool.wait_ge(hi_done, count + 1)
    k.nc.gpsimd.tensor_tensor(k.WS[:, ws, 1, 0:nk, :], w, k.WS[:, ws, 0, 0:nk, :].bitcast(F32),
                              ALU.subtract).then_inc(split_done, 1)


def project_kv(k):
    nc, g, out, w = k.nc, k.g, k.out, k.g["w_in"]
    with Stage(k, "kv") as st:
        acc = st.psum("acc", [P, 2, NT, 512])
        tp = st.psum("tp", [P, 2, 512])
        mm_done, acc_free, evacuated, tr_done, tp_free, samples_copied, hi_done, split_done, slot_ok = st.sems(
            "mm_done acc_free evacuated tr_done tp_free samples_copied hi_done split_done slot_ok")
        tmp = chunks(k.E[:, 0:2 * N], 2)
        h = NormSplit(k, st, 0, k.R1[:])
        base = list(k.wcount)
        k.wcount[0] += 4 * 16
        k.wcount[1] += 3 * 16
        block = st.block()

        @block.sync
        def _(sp):
            with sp.Fori(0, 3) as i:
                for s in range(2):
                    sp.wait_ge(split_done, 2 * i + s + 1)
                    sp.dma_start(k.W[:, s, 0:8, :], weight(w, KV0 + (2 * i + s) * P)).then_inc(k.wfull[s], 16)
            sp.wait_ge(split_done, 7)
            sp.dma_start(k.W[:, 0, 0:8, :], weight(w, GATE0)).then_inc(k.wfull[0], 16)
            sp.wait_ge(tp_free, 2 + 18)
            for j, n in enumerate(("cmp_p", "slc_p")):
                sp.dma_start(out[n].rearrange("(t p) f -> p t f", p=P),
                             k.kvtok[:, 0:TT, 256 * j:256 * j + 256]).then_inc(k.kv_stored, 16)
            sp.dma_start(out["win_p"].rearrange("(t p) f -> p t f", p=P), k.kvtok[:, 4:TT, 512:768]).then_inc(k.kv_stored, 16)
            for j, n in enumerate(("cmp_s", "slc_s")):
                sp.dma_start(out[n], k.kvtok[0:B, TT, 256 * j:256 * j + 256]).then_inc(k.kv_stored, 16)
            sp.dma_start(out["win_s"][:, 511, :], k.kvtok[0:B, TT, 512:768]).then_inc(k.kv_stored, 16)
            sp.dma_start(out["win_s"][:, 0:511, :], g["state_win_kv"][:, 1:512, :]).then_inc(k.kv_stored, 16)

        def transposes(pe, b, m, first_bank, j):
            for q in range(3):
                bank = (first_bank + q) % 2
                pe.wait_ge(tp_free, j + q + 1)
                if q < 2:
                    for t in range(4):
                        last = nc.tensor.transpose(tp[:, bank, t * P:t * P + m],
                                                   tmp[0:m, b, (4 * q + t) * P:(4 * q + t + 1) * P], k.ident[0:m, 0:m])
                else:
                    last = nc.tensor.transpose(tp[0:B, bank, 0:m], tmp[0:m, b, T:N], k.ident[0:m, 0:m])
                last.then_inc(tr_done, 1)

        @block.tensor
        def _(pe):
            pe.sem_inc(mm_done, 2)
            pe.sem_inc(tr_done, 6)
            with pe.Fori(0, 3) as i:
                for s in range(2):
                    pe.wait_ge(split_done, 2 * i + s + 3)
                    pe.wait_ge(acc_free, 2 * i + s + 1)
                    split_tile(k, acc, s, s, k.HH, k.HL, DC, wait=(pe, h.lo_done) if s == 0 else None).then_inc(mm_done, 1)
                for s in range(2):
                    pe.wait_ge(evacuated, 2 * i + s + 1)
                    transposes(pe, s, P, s, 6 * i + 3 * s)
            pe.wait_ge(split_done, 9)
            pe.wait_ge(acc_free, 7)
            split_tile(k, acc, 0, 0, k.HH, k.HL, DC).then_inc(mm_done, 1)
            pe.wait_ge(evacuated, 7)
            transposes(pe, 0, 24, 0, 18)

        @block.gpsimd
        def _(pool):
            pool.sem_inc(split_done, 2)
            with pool.Fori(0, 3) as i:
                for s in range(2):
                    pool.wait_ge(k.wfull[s], 16 * i + base[s] + 16)
                    pool.wait_ge(mm_done, 2 * i + s + 1)
                    pool.sem_inc(slot_ok, 1)
                    split_weights(k, pool, s, s, DC, hi_done, 2 * i + s, split_done)
            pool.wait_ge(k.wfull[0], base[0] + 64)
            pool.wait_ge(mm_done, 7)
            split_weights(k, pool, 0, 0, DC, hi_done, 6, split_done)

        @block.scalar
        def _(act):
            act.sem_inc(acc_free, 2)
            h.scalar(act)
            with act.Fori(0, 3) as i:
                for s in range(2):
                    act.wait_ge(mm_done, 2 * i + s + 3)
                    act.wait_ge(tr_done, 6 * i + 3 * s + 3)
                    nc.scalar.activation(tokens(tmp[:, s, :]), acc[:, s, :, 0:NW], ACT.Copy).then_inc(evacuated, 1)
                    if s == 0:
                        nc.scalar.activation(tokens(k.KT3[:, i, :]), acc[:, s, :, 0:NW], ACT.Copy).then_inc(acc_free, 1)
                    else:
                        act.wait_ge(evacuated, 2 * i + s + 1)
                        act.sem_inc(acc_free, 1)
            act.wait_ge(mm_done, 9)
            act.wait_ge(tr_done, 6 + 15)
            nc.scalar.activation(tokens(tmp[0:24, 0, :]), acc[0:24, 0, :, 0:NW], ACT.Sigmoid).then_inc(evacuated, 1)

        @block.vector
        def _(dve):
            dve.sem_inc(tp_free, 2)
            h.vector(dve)
            with dve.Fori(0, 3) as i:
                for s in range(2):
                    f = bass.ds((2 * i + s) * P, P)
                    for q in range(3):
                        dve.wait_ge(tr_done, 6 * i + 3 * s + q + 7)
                        if q < 2:
                            nc.vector.tensor_copy(k.kvtok[:, 4 * q:4 * q + 4, f],
                                                  tp[:, (s + q) % 2, :].rearrange("p (t f) -> p t f", t=4)).then_inc(tp_free, 1)
                        else:
                            nc.vector.tensor_copy(k.kvtok[0:B, TT, f], tp[0:B, (s + q) % 2, 0:P]).then_inc(tp_free, 1)
            for q in range(2):
                dve.wait_ge(tr_done, 18 + q + 7)
                nc.vector.tensor_copy(k.gtok[:, 4 * q:4 * q + 4, :],
                                      tp[:, q, :].rearrange("p (t f) -> p t f", t=4)[:, :, 0:24]).then_inc(tp_free, 1)
            dve.wait_ge(evacuated, 7)
            nc.vector.tensor_copy(k.gfm[:], tmp[0:24, 0, T:N]).then_inc(samples_copied, 1)
            dve.wait_ge(samples_copied, 1)
            dve.wait_ge(tp_free, 22)


def project_quv(k):
    nc, w = k.nc, k.g["w_in"]
    with Stage(k, "quv") as st:
        acc = st.psum("acc", [P, 2, NT, 512])
        tp = st.psum("tp", [P, 2, 512])
        mm_done, acc_free, tr_done, tp_free, hi_done, split_done, slot_ok = st.sems(
            "mm_done acc_free tr_done tp_free hi_done split_done slot_ok")
        tmp = chunks(k.ONr[:, 0:2 * N], 2)
        base = list(k.wcount)
        for s in range(2):
            k.wcount[s] += 2 * 32 + 4 * 16
        block = st.block()

        @block.sync
        def _(sp):
            with sp.Fori(0, 2) as i:
                for s in range(2):
                    sp.wait_ge(split_done, 2 * i + s + 1)
                    sp.sem_inc(slot_ok, 1)
                    for half in range(2):
                        sp.dma_start(k.W[:, s, 0:8, half * HD:(half + 1) * HD],
                                     weight(w, (2 * i + s) * HD + 4 * HD * half, HD)).then_inc(k.wfull[s], 16)
            with sp.Fori(0, 4) as i:
                for s in range(2):
                    sp.wait_ge(split_done, 2 * i + s + 5)
                    sp.dma_start(k.W[:, s, 0:8, :], weight(w, U0 + (2 * i + s) * P)).then_inc(k.wfull[s], 16)
            sp.wait_ge(k.kv_stored, 7 * 16)

        @block.tensor
        def _(pe):
            pe.sem_inc(mm_done, 2)
            pe.sem_inc(tr_done, 6)
            with pe.Fori(0, 2) as i:
                for s in range(2):
                    pe.wait_ge(split_done, 2 * i + s + 3)
                    pe.wait_ge(acc_free, 2 * i + s + 1)
                    split_tile(k, acc, s, s, k.HH, k.HL, DC).then_inc(mm_done, 1)
            with pe.Fori(0, 2) as i:
                for s in range(2):
                    pe.wait_ge(split_done, 2 * i + s + 7)
                    pe.wait_ge(acc_free, 2 * i + s + 5)
                    split_tile(k, acc, s, s, k.HH, k.HL, DC).then_inc(mm_done, 1)
            with pe.Fori(0, 2) as i:
                for s in range(2):
                    pe.wait_ge(split_done, 2 * i + s + 11)
                    pe.wait_ge(acc_free, 2 * i + s + 9)
                    split_tile(k, acc, s, s, k.HH, k.HL, DC).then_inc(mm_done, 1)
                for s in range(2):
                    pe.wait_ge(acc_free, 2 * i + s + 2 + 8 + 1)
                    for q in range(3):
                        bank = (s + q) % 2
                        pe.wait_ge(tp_free, 6 * i + 3 * s + q + 1)
                        if q < 2:
                            for t in range(4):
                                last = nc.tensor.transpose(tp[:, bank, t * P:(t + 1) * P],
                                                           tmp[:, s, (4 * q + t) * P:(4 * q + t + 1) * P], k.ident[:])
                        else:
                            last = nc.tensor.transpose(tp[0:B, bank, 0:P], tmp[:, s, T:N], k.ident[:])
                        last.then_inc(tr_done, 1)

        @block.gpsimd
        def _(pool):
            pool.sem_inc(split_done, 2)
            for n, first, step, tiles in ((2, 0, 32, 0), (4, 64, 16, 4)):
                with pool.Fori(0, n) as i:
                    for s in range(2):
                        pool.wait_ge(k.wfull[s], step * i + (base[s] + first + step))
                        pool.wait_ge(mm_done, 2 * i + s + 1 + tiles)
                        pool.sem_inc(slot_ok, 1)
                        split_weights(k, pool, s, s, DC, hi_done, 2 * i + s + tiles, split_done)

        @block.scalar
        def _(act):
            act.sem_inc(acc_free, 2)
            with act.Fori(0, 2) as i:
                for s in range(2):
                    act.wait_ge(mm_done, 2 * i + s + 3)
                    nc.scalar.activation(tokens(k.Q[:, 2 * i + s, :]), acc[:, s, :, 0:NW], ACT.Copy,
                                         scale=HD ** -0.5).then_inc(acc_free, 1)
            with act.Fori(0, 2) as i:
                for s in range(2):
                    act.wait_ge(mm_done, 2 * i + s + 7)
                    nc.scalar.activation(tokens(k.OG[:, 2 * i + s, :]), acc[:, s, :, 0:NW],
                                         ACT.Gelu_apprx_tanh).then_inc(acc_free, 1)
            with act.Fori(0, 2) as i:
                for s in range(2):
                    act.wait_ge(mm_done, 2 * i + s + 11)
                    act.wait_ge(tr_done, 6 * i + 3 * s + 3)
                    nc.scalar.activation(tokens(tmp[:, s, :]), acc[:, s, :, 0:NW],
                                         ACT.Gelu_apprx_tanh).then_inc(acc_free, 1)

        @block.vector
        def _(dve):
            dve.sem_inc(tp_free, 2)
            with dve.Fori(0, 2) as i:
                for s in range(2):
                    f = bass.ds((2 * i + s) * P, P)
                    for q in range(3):
                        dve.wait_ge(tr_done, 6 * i + 3 * s + q + 7)
                        if q < 2:
                            nc.vector.tensor_copy(k.vtok[:, 4 * q:4 * q + 4, f],
                                                  tp[:, (s + q) % 2, :].rearrange("p (t f) -> p t f", t=4)).then_inc(tp_free, 1)
                        else:
                            nc.vector.tensor_copy(k.vtok[0:B, TT, f], tp[0:B, (s + q) % 2, 0:P]).then_inc(tp_free, 1)
            dve.wait_ge(tp_free, 14)


def spatial_gate(k):
    nc, g, out = k.nc, k.g, k.out
    NG = 4
    with Stage(k, "gm") as st:
        ps = st.psum("ps", [P, 2, 1024])
        wp = st.psum("wp", [P, 512])
        sp_ = st.psum("sp", [P, 512])
        const_in, w_turned, w_masked, stats, norm, v_ready, mixed, biased, mixed_free, smp_t, smp, stores = st.sems(
            "const_in w_turned w_masked stats norm v_ready mixed biased mixed_free smp_t smp stores")
        gb = k.Hr[:, 0:GM]
        bb = k.Hr[:, GM:2 * GM]
        wraw = k.Hr[:, 1024:1536].rearrange("p (g s) -> p g s", g=NG)
        wT = k.Hr[:, 1536:2048].rearrange("p (g s) -> p g s", g=NG)
        upper = k.Hr[:, 2048:2176]
        bs = k.Hr[:, 2176:2688].rearrange("p (g t) -> p g t", g=NG)
        mix = k.Hr[:, 2688:4736].rearrange("p (b t) -> p b t", b=2)
        bst = k.Hr[:, 4736:4736 + 54].rearrange("p (t s) -> p t s", s=6)
        mv = k.Hr[:, 4800:4818].rearrange("p (t s) -> p t s", s=2)
        rs = k.Hr[:, 4832:4841]
        w00 = k.Hr[:, 4848:4852]
        vs = k.Hr[:, 4864:4896].rearrange("p (g b) -> p g b", g=NG)
        block = st.block()

        @block.sync
        def _(sp):
            sp.dma_start(gb, g["gm_ln_g"].to_broadcast([P, GM])).then_inc(const_in, 16)
            sp.dma_start(bb, g["gm_ln_b"].to_broadcast([P, GM])).then_inc(const_in, 16)
            sp.dma_start(wraw, g["gm_ws"].rearrange("(g t) s -> t g s", g=NG)).then_inc(const_in, 16)
            sp.dma_start(upper, g["upper"]).then_inc(const_in, 16)
            sp.dma_start(bs, g["gm_bs"].rearrange("g t -> (g t)").unsqueeze(0).to_broadcast([P, 512])
                         .rearrange("p (g t) -> p g t", g=NG)).then_inc(const_in, 16)
            sp.dma_start(w00, g["gm_ws"].rearrange("(g t) s -> g t s", g=NG)[:, 0, 0].unsqueeze(0).to_broadcast([P, NG]),
                         allow_slow_non_contiguous=True).then_inc(const_in, 16)
            for i, n in enumerate("kv"):
                sp.dma_start(k.w1[:, i], g[f"cmp_w1_{n}"].rearrange("(c p) m -> p c m", p=P)).then_inc(k.w1_in, 16)
            sp.wait_ge(v_ready, 1)
            sp.dma_start(out["gm_v"], k.vtok[0:B, TT, :]).then_inc(stores, 16)
            sp.wait_ge(stores, 16)

        @block.gpsimd
        def _(pool):
            gather_rows(k, pool, 0)

        @block.tensor
        def _(pe):
            pe.wait_ge(const_in, 96)
            for q in range(NG):
                last = nc.tensor.transpose(wp[:, q * P:(q + 1) * P], wraw[:, q, :], k.ident[:])
            last.then_inc(w_turned, 1)
            pe.wait_ge(w_masked, 1)
            pe.wait_ge(v_ready, 1)
            for q in range(NG):
                if q >= 2:
                    pe.wait_ge(mixed_free, q - 1)
                for t in range(TT):
                    last = nc.tensor.matmul(ps[:, q % 2, t * P:(t + 1) * P], k.vtok[:, t, q * P:(q + 1) * P], wT[:, q, :],
                                            start=True, stop=True)
                last.then_inc(mixed, 1)
            for q in range(NG):
                last = nc.tensor.transpose(sp_[:, q * B:(q + 1) * B], k.vtok[0:B, TT, q * P:(q + 1) * P], k.ident[0:B, 0:B])
            last.then_inc(smp_t, 1)

        @block.scalar
        def _(act):
            act.wait_ge(norm, 2)
            nc.scalar.activation(rs, rs, ACT.Sqrt).then_inc(norm, 1)

        @block.vector
        def _(dve):
            for t in range(9):
                m = P if t < TT else B
                nc.vector.bn_stats(bst[0:m, t, :], k.vtok[0:m, t, :]).then_inc(stats, 1)
            dve.wait_ge(stats, 9)
            nc.vector.memset(mv[:, TT, :], 1.0).then_inc(stats, 1)
            dve.wait_ge(stats, 10)
            for t in range(9):
                m = P if t < TT else B
                nc.vector.bn_aggr(mv[0:m, t, :], bst[0:m, t, :]).then_inc(stats, 1)
            dve.wait_ge(stats, 19)
            nc.vector.tensor_scalar(rs, mv[:, :, 1], EPS, None, ALU.add).then_inc(norm, 1)
            dve.wait_ge(norm, 1)
            nc.vector.reciprocal(rs, rs).then_inc(norm, 1)
            dve.wait_ge(const_in, 96)
            dve.wait_ge(w_turned, 1)
            nc.vector.tensor_tensor(wT, wp[:].rearrange("p (g t) -> p g t", g=NG),
                                    upper.unsqueeze(1).to_broadcast([P, NG, P]), ALU.mult).then_inc(w_masked, 1)
            dve.wait_ge(norm, 3)
            for t in range(9):
                m = P if t < TT else B
                nc.vector.tensor_scalar(k.vtok[0:m, t, :], k.vtok[0:m, t, :], mv[0:m, t, 0:1], rs[0:m, t:t + 1],
                                        ALU.subtract, ALU.mult).then_inc(stats, 1)
            dve.wait_ge(stats, 28)
            for a, b, m in ((0, TT, P), (TT, 9, B)):
                v = k.vtok[0:m, a:b, :]
                nc.vector.tensor_tensor(v, v, gb[0:m, :].unsqueeze(1).to_broadcast([m, b - a, GM]), ALU.mult).then_inc(stats, 1)
            dve.wait_ge(stats, 30)
            for a, b, m in ((0, TT, P), (TT, 9, B)):
                v = k.vtok[0:m, a:b, :]
                last = nc.vector.tensor_tensor(v, v, bb[0:m, :].unsqueeze(1).to_broadcast([m, b - a, GM]), ALU.add)
                last.then_inc(stats if a == 0 else v_ready, 1)
            dve.wait_ge(stats, 31)
            for q in range(NG):
                dve.wait_ge(mixed, q + 1)
                nc.vector.tensor_tensor(mix[:, q % 2, :].rearrange("p (c t) -> p c t", c=TT),
                                        ps[:, q % 2].rearrange("p (c t) -> p c t", c=TT),
                                        bs[:, q, :].unsqueeze(1).to_broadcast([P, TT, P]), ALU.add).then_inc(mixed_free, 1)
                dve.wait_ge(mixed_free, q + 1)
                nc.vector.tensor_tensor(k.OG[:, q, 0:T], k.OG[:, q, 0:T], mix[:, q % 2, :], ALU.mult).then_inc(biased, 1)
            dve.wait_ge(smp_t, 1)
            for q in range(NG):
                nc.vector.tensor_scalar(vs[:, q, :], sp_[:, q * B:(q + 1) * B], w00[:, q:q + 1], bs[:, q, 0:1],
                                        ALU.mult, ALU.add).then_inc(smp, 1)
            dve.wait_ge(smp, NG)
            nc.vector.tensor_tensor(k.OG[:, :, T:N], k.OG[:, :, T:N], vs, ALU.mult).then_inc(smp, 1)
            dve.wait_ge(smp, NG + 1)
            dve.wait_ge(biased, NG)


def gather_rows(k, pool, b):
    pool.indirect_dma_start(out=k.cmp_past[b % 2], out_offset=None, in_=k.g["cache_cmp_kv"],
                            in_offset=bass.IndirectOffsetOnAxis(ap=k.pid[:, b:b + 1], axis=0)).then_inc(k.cmp_gathered[b % 2], 16)


def compress(k):
    nc, g = k.nc, k.g
    with Stage(k, "cmp") as st:
        tp = st.psum("tp", [P, 4, 512])
        pre = st.psum("pre", [P, 2, 512])
        kv = st.psum("kv", [P, 2, 512])
        gathered = k.cmp_gathered
        prompt_in, regrouped_k, regrouped_v, w_in, w2_cleared, w2_placed, pe_done, pe_copied, tr_done, tp_copied, pre_done, silu_done, kv_done, kv_copied = st.sems(
            "prompt_in regrouped_k regrouped_v w_in w2_cleared w2_placed pe_done pe_copied tr_done tp_copied pre_done silu_done kv_done kv_copied")
        G = [x.rearrange("p (r f) -> p r f", r=16) for x in k.cmp_past]
        RG = [k.W[:].rearrange("p a c m -> p (a c m)")[:, 0:2048], k.E[:, 3584:5632]]
        TR = k.Hr[:, 4096:8192].rearrange("p (kv c g n) -> p kv c g n", kv=2, c=8, g=2)
        w1 = k.w1
        sh = k.E[:, 2304:2816].rearrange("p (kv g n) -> p kv g n", kv=2, g=2)
        w2k = k.E[:, 2816:3072].rearrange("p (g m) -> p g m", g=2)
        w2v = k.E[:, 3072:3136]
        pos = k.E[:, 3136:3168].rearrange("p (kv c) -> p kv c", kv=2)
        pe_b = k.tiny[:, 0:2]
        block = st.block()

        @block.gpsimd
        def _(pool):
            for b in range(1, B):
                pool.wait_ge(regrouped_k, b + 1)
                pool.wait_ge(regrouped_v, b + 1)
                gather_rows(k, pool, b)

        @block.sync
        def _(sp):
            for i, n in enumerate("kv"):
                sp.dma_start(pos[:, i, :], g[f"cmp_pe_{n}"].rearrange("a (c p) -> p (a c)", p=P),
                             allow_slow_non_contiguous=True).then_inc(w_in, 16)
            sp.dma_start(w2v, g["cmp_w2_v"]).then_inc(w_in, 16)
            sp.wait_ge(w2_cleared, 1)
            for i in range(2):
                sp.dma_start(w2k[:, i, i * HD:(i + 1) * HD], g["cmp_w2_k"]).then_inc(w2_placed, 16)
            sp.wait_ge(regrouped_k, 2 + 7)
            sp.wait_ge(regrouped_v, 2 + 7)
            sp.dma_start(k.ONr[0:64, 0:4096], k.out["cmp_p"].rearrange("(n r) f -> n (r f)", r=16)).then_inc(prompt_in, 16)

        def turn(pe, b, i, n):
            for q in range(4 * i, 4 * i + 4):
                if q % 4 == 0:
                    pe.wait_ge((regrouped_k, regrouped_v)[i], b + 3)
                pe.wait_ge(tp_copied, 8 * b + q + 1)
                for j in range(4):
                    f = (j % 2) * 1024 + (2 * (q % 4) + j // 2) * P
                    last = nc.tensor.transpose(tp[:, q % 4, j * P:j * P + n], RG[i][0:n, f:f + P],
                                               k.ident[0:n, 0:n])
                last.then_inc(tr_done, 1)

        def hidden(pe, b, i, n):
            pe.wait_ge(tp_copied, 8 * b + 4 * i + 8)
            pe.wait_ge(silu_done, 2 * b + i + 1)
            for c in range(16):
                last = nc.tensor.matmul(pre[:, i, 0:2 * n].rearrange("p (g n) -> p g n", g=2), w1[:, i, c, :],
                                        TR[:, i, c % 8, :, c // 8:c // 8 + n], start=(c == 0), stop=(c == 15))
            last.then_inc(pre_done, 1)

        def project(pe, b, n):
            pe.wait_ge(silu_done, 2 * b + 4)
            pe.wait_ge(kv_copied, 2 * b + 1)
            for gr in range(2):
                last = nc.tensor.matmul(kv[:, 0, 0:n], w2k[:, gr, :], sh[:, 0, gr, 0:n], start=(gr == 0), stop=(gr == 1))
            last.then_inc(kv_done, 1)
            pe.wait_ge(kv_copied, 2 * b + 2)
            for gr in range(2):
                last = nc.tensor.matmul(kv[0:n, 1, gr * HD:(gr + 1) * HD], sh[:, 1, gr, 0:n], w2v, start=True, stop=True)
            last.then_inc(kv_done, 1)

        def step(pe, b, n, following):
            hidden(pe, b, 0, n)
            if following:
                turn(pe, b + 1, 0, following)
            hidden(pe, b, 1, n)
            if following:
                turn(pe, b + 1, 1, following)
            project(pe, b, n)

        @block.tensor
        def _(pe):
            pe.sem_inc(tr_done, 16)
            pe.wait_ge(k.w1_in, 32)
            pe.wait_ge(w_in, 48)
            for i in range(2):
                for c in range(16):
                    last = nc.tensor.matmul(pre[:, i, 0:1], w1[:, i, c, :], pos[:, i, c:c + 1], start=(c == 0), stop=(c == 15))
            last.then_inc(pe_done, 1)
            pe.wait_ge(pe_copied, 1)
            pe.wait_ge(w2_placed, 32)
            turn(pe, 0, 0, P)
            turn(pe, 0, 1, P)
            with pe.Fori(0, 7) as b:
                step(pe, b, NCS, P)
            step(pe, 7, NCS, 64)
            step(pe, 8, NCP, None)

        @block.scalar
        def _(act):
            act.sem_inc(silu_done, 2)
            act.sem_inc(kv_copied, 2)
            act.sem_inc(regrouped_k, 2)
            act.wait_ge(pe_copied, 1)

            def regroup(s, b, rows_in, full, m):
                act.wait_ge(rows_in, full)
                act.wait_ge(tr_done, 8 * b + 12)
                nc.scalar.activation(RG[0][0:m].rearrange("p (g r d) -> p g r d", g=2, r=16),
                                     G[s][0:m, :, 0:P].rearrange("p r (g d) -> p g r d", g=2), ACT.Copy).then_inc(regrouped_k, 1)

            def outputs(b, n, kc, vc):
                for i in range(2):
                    act.wait_ge(pre_done, 2 * b + i + 1)
                    act.wait_ge(kv_done, 2 * b + 2)
                    nc.scalar.activation(sh[:, i, :, 0:n], pre[:, i, 0:2 * n].rearrange("p (g n) -> p g n", g=2), ACT.Silu,
                                         bias=pe_b[:, i:i + 1]).then_inc(silu_done, 1)
                act.wait_ge(kv_done, 2 * b + 3)
                nc.scalar.activation(kc, kv[:, 0, 0:n], ACT.Copy).then_inc(kv_copied, 1)
                act.wait_ge(kv_done, 2 * b + 4)
                nc.scalar.activation(vc, kv[0:n, 1, 0:P], ACT.Copy).then_inc(kv_copied, 1)

            act.sem_inc(kv_done, 2)
            regroup(0, 0, gathered[0], 16, P)
            with act.Fori(0, 3) as i:
                for s in range(2):
                    b = 2 * i + s
                    regroup(1 - s, b + 1, gathered[1 - s], 16 * i + (16, 32)[s], P)
                    outputs(b, NCS, k.KC[:, b, 0:NCS], k.VC[0:NCS, b, :])
            regroup(1, 7, gathered[1], 64, P)
            outputs(6, NCS, k.KC[:, 6, 0:NCS], k.VC[0:NCS, 6, :])
            regroup(0, 8, prompt_in, 16, 64)
            outputs(7, NCS, k.KC[:, 7, 0:NCS], k.VC[0:NCS, 7, :])
            outputs(8, NCP, k.KC[:, 8, 0:NCP], k.VC[0:NCP, 8, :])
            act.wait_ge(kv_copied, 20)

        @block.vector
        def _(dve):
            dve.sem_inc(tp_copied, 4)
            dve.sem_inc(regrouped_v, 2)
            nc.vector.memset(w2k, 0.0).then_inc(w2_cleared, 1)
            dve.wait_ge(pe_done, 1)
            nc.vector.tensor_copy(pe_b, pre[:, :, 0]).then_inc(pe_copied, 1)

            def batch(s, b, rows_in, full, n):
                dve.wait_ge(rows_in, full)
                dve.wait_ge(tr_done, 8 * b + 16)
                nc.vector.tensor_copy(RG[1][0:n].rearrange("p (g r d) -> p g r d", g=2, r=16),
                                      G[s][0:n, :, P:2 * P].rearrange("p r (g d) -> p g r d", g=2)).then_inc(regrouped_v, 1)
                for q in range(8):
                    dve.wait_ge(tr_done, 8 * b + q + 17)
                    dve.wait_ge(silu_done, 2 * b + q // 4 + 1)
                    nc.vector.tensor_copy(TR[:, q // 4, 2 * (q % 4):2 * (q % 4) + 2, :, 0:n],
                                          tp[:, q % 4, :].rearrange("p (c g n) -> p c g n", c=2, g=2)[:, :, :, 0:n]).then_inc(tp_copied, 1)

            with dve.Fori(0, 4) as i:
                for s in range(2):
                    batch(s, 2 * i + s, gathered[s], 16 * i + 16, P)
            batch(0, 8, prompt_in, 16, 64)
            dve.wait_ge(tp_copied, 76)


def select_blocks(k):
    nc, g = k.nc, k.g
    R = B * H
    with Stage(k, "sel") as st:
        ps = st.psum("ps", [P, 8, 512])
        cleared, q_placed, const_in, scored, negated, exped, inverted, scaled, turned, turned_out, imp1, imp1_out, imp, imp_out, placed, out_c, ranked, row, widened, mask_turned, mask_out, bias_out, tables, cleared_self, oc_out, lg, qf = st.sems(
            "cleared q_placed const_in scored negated exped inverted scaled turned turned_out imp1 imp1_out imp imp_out placed "
            "out_c ranked row widened mask_turned mask_out bias_out tables cleared_self oc_out lg qf")
        at = [0]

        def room(words, rows=P):
            a = at[0]
            at[0] += words
            return k.Hr[0:rows, a:a + words]

        QS = room(576)
        relb64 = room(64, 33)
        oh = room(OH_ALL, 33)
        LG = room(64, 24)
        head_of, branch_of = room(8, 24), room(4, 24)[:, 0:3]
        S = room(128, R)[:, 0:NCS]
        SG = room(128, R)[:, 0:NCS]
        PCT, PCG = room(64, NCS), room(64, NCS)
        OV = room(36, NCS)[:, 0:NSEL]
        G64 = room(64, R)
        IM = room(36, R)[:, 0:NSEL]
        SC = room(36, R)[:, 0:NSEL]
        before = room(NSEL * NSEL, R)
        C1, C2 = room(NSEL * NSEL, R), room(NSEL * NSEL, R)
        cnt = room(36, R)[:, 0:NSEL]
        row_ = room(36, R)
        nm, l, li = room(1, R), room(1, R), room(1, R)
        WIDE = room(P, R)
        spread = room(2 * P, 24).rearrange("p (r n) -> p r n", r=2)
        MASK = room(64)
        own = room(64, B)
        block = st.block()
        sq = "p (j i) -> p j i"

        @block.sync
        def _(sp):
            for dst, n in ((oh, "oh_samples"), (head_of, "head_of"), (branch_of, "branch_of"), (OV, "overlap"), (G64, "same_group"),
                           (own, "not_own")):
                sp.dma_start(dst, g[n]).then_inc(const_in, 16)
            sp.dma_start(before, g["before"].to_broadcast([R, NSEL * NSEL])).then_inc(const_in, 16)

        @block.gpsimd
        def _(pool):
            for b in range(2):
                gather_past(k, pool, b)

        @block.tensor
        def _(pe):
            pe.wait_ge(const_in, 112)
            pe.wait_ge(qf, 1)
            pe.wait_ge(lg, 3)
            for b in range(B):
                nc.tensor.matmul(ps[0:R, 0, 0:NCS], QS[:, b * R:(b + 1) * R], k.KC[:, b, 0:NCS], start=(b == 0), stop=False)
            nc.tensor.matmul(ps[0:R, 0, 0:NCS], relb64, oh[:, OH_CMP:OH_CMP + NCS], start=False, stop=True).then_inc(scored, 1)
            nc.tensor.matmul(ps[0:R, 1, 0:3], LG, branch_of, start=True, stop=True).then_inc(scored, 1)
            for i in range(20):
                at_ = OH_SLC + i * P if i < 16 else OH_WIN + (i - 16) * P
                nc.tensor.matmul(ps[:, 2, i * H:(i + 1) * H], oh[:, at_:at_ + P], k.relb[:], start=True, stop=True)
            nc.tensor.matmul(ps[0:B, 2, 160:168], oh[:, OH_SELF:OH_SELF + B], k.relb[:], start=True, stop=True).then_inc(scored, 1)
            for i in range(2):
                last = nc.tensor.matmul(ps[:, 3, i * R:(i + 1) * R], spread[:, i, :], LG, start=True, stop=True)
            last.then_inc(scored, 1)
            pe.wait_ge(scaled, 1)
            nc.tensor.transpose(ps[0:NCS, 4, 0:R], S, k.ident[0:R, 0:R]).then_inc(turned, 1)
            pe.wait_ge(scaled, 2)
            nc.tensor.transpose(ps[0:NCS, 5, 0:R], SG, k.ident[0:R, 0:R]).then_inc(turned, 1)
            pe.wait_ge(turned_out, 1)
            nc.tensor.matmul(ps[0:R, 6, 0:NSEL], PCT, OV, start=True, stop=True).then_inc(imp1, 1)
            pe.wait_ge(imp1_out, 1)
            nc.tensor.matmul(ps[0:R, 7, 0:NSEL], G64, IM, start=True, stop=True).then_inc(imp, 1)
            pe.wait_ge(turned_out, 2)
            for b in range(B):
                last = nc.tensor.matmul(ps[:, 4, b * H:(b + 1) * H], k.VC[0:NCS, b, :], PCG[:, b * H:(b + 1) * H],
                                        start=True, stop=True)
            last.then_inc(out_c, 1)
            pe.wait_ge(widened, 1)
            nc.tensor.transpose(ps[:, 5, 0:R], WIDE, k.ident[0:R, 0:R]).then_inc(mask_turned, 1)

        @block.scalar
        def _(act):
            act.wait_ge(negated, 1)
            nc.scalar.activation(S, ps[0:R, 0, 0:NCS], ACT.Exp, bias=nm, accum_out=l).then_inc(exped, 1)

        @block.vector
        def _(dve):
            nc.vector.memset(QS, 0.0).then_inc(cleared, 1)
            nc.vector.memset(k.QS8, 0.0).then_inc(cleared, 1)
            nc.vector.tensor_copy(relb64.rearrange("p (b h) -> p b h", b=B), k.relb[:].unsqueeze(1).to_broadcast([33, B, H])).then_inc(lg, 1)
            dve.wait_ge(cleared, 2)
            for i in range(2):
                nc.vector.tensor_copy(k.QS8[i * HD:(i + 1) * HD, :, 4 * i:4 * i + 4],
                                      k.Q[i * HD:(i + 1) * HD, :, T:N].rearrange("p c b -> p b c")).then_inc(q_placed, 1)
            dve.wait_ge(q_placed, 2)
            nc.vector.tensor_copy(QS.rearrange("p (b x) -> p b x", b=B)[:, :, 0:H], k.QS8).then_inc(qf, 1)
            dve.wait_ge(const_in, 112)
            nc.vector.tensor_tensor(LG.rearrange("p (b h) -> p b h", b=B), k.gfm[:].unsqueeze(2).to_broadcast([24, B, H]),
                                    head_of.unsqueeze(1).to_broadcast([24, B, H]), ALU.mult).then_inc(lg, 1)
            nc.vector.tensor_copy(spread, branch_of[:, 1:3].unsqueeze(2).to_broadcast([24, 2, P])).then_inc(lg, 1)
            nc.vector.memset(k.S[:, :, 16, :], NEG).then_inc(cleared_self, 1)
            nc.vector.memset(k.S[:, :, 21, :], NEG).then_inc(cleared_self, 1)
            nc.vector.memset(k.unit, 1.0).then_inc(cleared_self, 1)
            dve.wait_ge(scored, 1)
            nc.vector.tensor_reduce(nm, ps[0:R, 0, 0:NCS], AX, ALU.max, negate=True).then_inc(negated, 1)
            dve.wait_ge(scored, 4)
            nc.vector.tensor_copy(row_[:, 33:36], ps[0:R, 1, 0:3]).then_inc(row, 1)
            nc.vector.tensor_copy(k.GT, ps[:, 3, 0:2 * R]).then_inc(bias_out, 1)
            for i in range(2):
                bb = samples(k.BB[:, i, :])
                nc.vector.tensor_copy(bb[:, :, 17:21, :], ps[:, 2, 128:160].rearrange("p (r h) -> p r h", h=H).unsqueeze(1)
                                      .to_broadcast([P, 4, 4, H])).then_inc(tables, 1)
                for x in (16, 21):
                    nc.vector.tensor_tensor(bb[0:B, :, x, :], own[:, 32 * i:32 * i + 32].rearrange("p (b h) -> p b h", h=H),
                                            ps[0:B, 2, 160:168].unsqueeze(1).to_broadcast([B, 4, H]), ALU.add).then_inc(tables, 1)
            dve.wait_ge(exped, 1)
            nc.vector.reciprocal(li, l).then_inc(inverted, 1)
            dve.wait_ge(inverted, 1)
            nc.vector.tensor_scalar(S, S, li, None, ALU.mult).then_inc(scaled, 1)
            dve.wait_ge(scaled, 1)
            dve.wait_ge(row, 1)
            nc.vector.tensor_scalar(SG, S, row_[:, 33:34], None, ALU.mult).then_inc(scaled, 1)
            dve.wait_ge(turned, 1)
            nc.vector.tensor_copy(PCT, ps[0:NCS, 4, 0:R]).then_inc(turned_out, 1)
            dve.wait_ge(turned, 2)
            nc.vector.tensor_copy(PCG, ps[0:NCS, 5, 0:R]).then_inc(turned_out, 1)
            dve.wait_ge(imp1, 1)
            nc.vector.tensor_copy(IM, ps[0:R, 6, 0:NSEL]).then_inc(imp1_out, 1)
            dve.wait_ge(imp, 1)
            nc.vector.tensor_copy(SC, ps[0:R, 7, 0:NSEL]).then_inc(imp_out, 1)
            dve.wait_ge(imp_out, 1)
            nc.vector.memset(SC[:, 0:1], FORCE).then_inc(placed, 1)
            nc.vector.memset(SC[:, NSEL - 2:NSEL], FORCE).then_inc(placed, 1)
            dve.wait_ge(placed, 2)
            one = SC.unsqueeze(1).to_broadcast([R, NSEL, NSEL])
            other = SC.unsqueeze(2).to_broadcast([R, NSEL, NSEL])
            nc.vector.tensor_tensor(C1.rearrange(sq, j=NSEL), one, other, ALU.is_gt).then_inc(ranked, 1)
            nc.vector.tensor_tensor(C2.rearrange(sq, j=NSEL), one, other, ALU.is_equal).then_inc(ranked, 1)
            dve.wait_ge(ranked, 2)
            nc.vector.tensor_tensor(C2, C2, before, ALU.mult).then_inc(ranked, 1)
            dve.wait_ge(ranked, 3)
            nc.vector.tensor_tensor(C1, C1, C2, ALU.add).then_inc(ranked, 1)
            dve.wait_ge(ranked, 4)
            nc.vector.tensor_reduce(cnt, C1.rearrange(sq, j=NSEL), AX, ALU.add).then_inc(ranked, 1)
            dve.wait_ge(ranked, 5)
            nc.vector.tensor_scalar(row_[:, 0:NSEL], cnt, float(TOPK) - 0.5, NEG, ALU.is_ge, ALU.mult).then_inc(row, 1)
            dve.wait_ge(row, 2)
            nc.vector.tensor_copy(WIDE.rearrange("p (j x) -> p j x", x=4),
                                  row_[:, 0:32].unsqueeze(2).to_broadcast([R, 32, 4])).then_inc(widened, 1)
            dve.wait_ge(out_c, 1)
            nc.vector.tensor_copy(k.OC, ps[:, 4, 0:64].rearrange("p (b h) -> p b h", b=B)).then_inc(oc_out, 1)
            dve.wait_ge(mask_turned, 1)
            nc.vector.tensor_copy(MASK, ps[:, 5, 0:R]).then_inc(mask_out, 1)
            dve.wait_ge(mask_out, 1)
            for i in range(2):
                nc.vector.tensor_tensor(samples(k.BB[:, i, :])[:, :, 0:16, :],
                                        ps[:, 2, 0:128].rearrange("p (r h) -> p r h", h=H).unsqueeze(1).to_broadcast([P, 4, 16, H]),
                                        MASK[:, 32 * i:32 * i + 32].rearrange("p (b h) -> p b h", h=H).unsqueeze(2)
                                        .to_broadcast([P, 4, 16, H]), ALU.add).then_inc(tables, 1)
            dve.wait_ge(tables, 8)
            dve.wait_ge(oc_out, 1)
            dve.wait_ge(bias_out, 1)
            dve.wait_ge(cleared_self, 3)


def samples(ap):
    return ap.rearrange("p (b c h) -> p b c h", b=4, h=H)


def gather_past(k, pool, b):
    pool.indirect_dma_start(out=k.past[b % 4], out_offset=None, in_=k.g["cache_slc_kv"],
                            in_offset=bass.IndirectOffsetOnAxis(ap=k.pid[:, b:b + 1], axis=0)).then_inc(k.gathered[b % 4], 16)


def sample_attention(k):
    nc, g = k.nc, k.g
    with Stage(k, "smp") as st:
        tp = st.psum("tp", [P, 4, 512])
        sc = st.psum("sc", [P, 2, 512])
        mt = st.psum("mt", [P, 512])
        misc = st.psum("misc", [P, 512])
        win_in = st.sems(" ".join(f"win_in_{j}" for j in range(4)))
        tr_done, copied_even, copied_odd, scored, added, maxed, max_turned, max_out, diag, max_spread, centred, exped, summed, sum_spread, inverted, factor, p_ready, pv_done, o_cleared, o_copied, o_turned, o_done, turn_now = st.sems(
            "tr_done copied_even copied_odd scored added maxed max_turned max_out diag max_spread centred exped summed sum_spread "
            "inverted factor p_ready pv_done o_cleared o_copied o_turned o_done turn_now")
        copied = (copied_even, copied_odd)
        G = [x.rearrange("p (r f) -> p r f", r=16) for x in k.past]
        GW = k.CW[:].rearrange("p (j r f) -> p j r f", j=4, r=4)
        kT = k.E[:, 2304:2304 + 2048].rearrange("p (u n) -> p u n", u=4)
        PE2 = k.ONr[:, 3 * N:3 * N + 704]
        pb = samples(PE2)
        o = N + 704
        M1, dg, L1, F = (k.ONr[:, o + 64 * i:o + 64 * (i + 1)] for i in range(4))
        m1 = k.ONr[0:64, o + 256:o + 257]
        dg = dg[0:64]
        OH = k.ONr[:, 2 * N + 704:2 * N + 832]
        vnew = [k.kvtok[0:B, TT, 384:512], k.kvtok[0:B, TT, 640:768]]
        by_branch = "p (r b h) -> p r b h"
        parts = ((0, 17), (17, 22))
        block = st.block()

        @block.gpsimd
        def _(pool):
            for b in range(2, B):
                if b >= 4:
                    pool.wait_ge(pv_done, b - 3)
                gather_past(k, pool, b)

        @block.sync
        def _(sp):
            for b in range(B):
                if b >= 4:
                    sp.wait_ge(pv_done, b - 3)
                sp.dma_start(GW[:, b % 4], g["state_win_kv"][b, :, :].rearrange("(n r) f -> n r f", r=4)).then_inc(win_in[b % 4], 16)

        def scores(i, u):
            j, q = u // 5, u % 5
            rhs = k.QS8[:, bass.ds(4 * i + j, 1), :].rearrange("p b h -> p (b h)")
            at = (j % 2) * 176
            for x in range(4):
                c = 4 * q + x if q < 4 else 17 + x
                last = nc.tensor.matmul(sc[:, j // 2, at + c * H:at + (c + 1) * H], kT[:, u % 4, x * P:(x + 1) * P], rhs,
                                        start=True, stop=True)
            if q == 4:
                for c, kv in ((16, 0), (21, 1)):
                    last = nc.tensor.matmul(sc[0:B, j // 2, at + c * H:at + (c + 1) * H], k.KT[:, kv, T:N], rhs, start=True, stop=True)
                last.then_inc(scored, 1)

        @block.tensor
        def _(pe):
            with pe.Fori(0, 2) as i:
                for u in range(20):
                    j, q = u // 5, u % 5
                    if q == 0:
                        pe.wait_ge(k.gathered[j], 16 * i + 16)
                    if q == 4:
                        pe.wait_ge(win_in[j], 16 * i + 16)
                    pe.wait_ge(copied[u % 2], 10 * i + u // 2 + 1)
                    pe.sem_inc(turn_now, 1)
                    for x in range(4):
                        src = G[j][:, 4 * q + x, 0:P] if q < 4 else GW[:, j, x, 0:P]
                        last = nc.tensor.transpose(tp[:, u % 4, x * P:(x + 1) * P], src, k.ident[:])
                    last.then_inc(tr_done, 1)
                    if u:
                        pe.wait_ge(copied[(u - 1) % 2], 10 * i + (u - 1) // 2 + 3)
                        scores(i, u - 1)
                pe.wait_ge(copied[1], 10 * i + 12)
                scores(i, 19)
                pe.wait_ge(maxed, 2 * i + 2)
                pe.sem_inc(turn_now, 1)
                nc.tensor.transpose(mt[0:64, 0:P], M1, k.ident[:]).then_inc(max_turned, 1)
                pe.wait_ge(diag, i + 1)
                pe.sem_inc(turn_now, 1)
                nc.tensor.matmul(misc[:, 0:64], k.unit[0:64, :], dg, start=True, stop=True).then_inc(max_spread, 1)
                pe.wait_ge(summed, 2 * i + 2)
                pe.sem_inc(turn_now, 1)
                nc.tensor.matmul(misc[:, 64:128], k.unit, L1, start=True, stop=True).then_inc(sum_spread, 1)
                pe.wait_ge(p_ready, 2 * i + 2)
                pe.sem_inc(turn_now, 1)
                for j in range(4):
                    dst = mt[32 * j:32 * j + H, P:2 * P]
                    for c in range(16):
                        nc.tensor.matmul(dst, pb[:, j, c, :], G[j][:, c, P:2 * P], start=(c == 0), stop=False)
                    for c in range(4):
                        nc.tensor.matmul(dst, pb[:, j, 17 + c, :], GW[:, j, c, P:2 * P], start=False, stop=False)
                    nc.tensor.matmul(dst, pb[0:B, j, 16, :], vnew[0], start=False, stop=False)
                    nc.tensor.matmul(dst, pb[0:B, j, 21, :], vnew[1], start=False, stop=True).then_inc(pv_done, 1)
                pe.wait_ge(o_copied, 4 * i + 4)
                pe.sem_inc(turn_now, 1)
                nc.tensor.transpose(misc[:, P:2 * P], OH, k.ident[:]).then_inc(o_turned, 1)

        @block.scalar
        def _(act):
            act.sem_inc(copied_even, 2)
            with act.Fori(0, 2) as i:
                for u in range(0, 20, 2):
                    act.wait_ge(tr_done, 20 * i + u + 1)
                    nc.scalar.activation(kT[:, u % 4, :], tp[:, u % 4, :], ACT.Copy).then_inc(copied_even, 1)
                act.wait_ge(centred, 2 * i + 2)
                nc.scalar.activation(PE2, PE2, ACT.Exp).then_inc(exped, 1)

        @block.vector
        def _(dve):
            dve.sem_inc(copied_odd, 2)
            nc.vector.memset(OH, 0.0).then_inc(o_cleared, 1)
            dve.wait_ge(o_cleared, 1)
            with dve.Fori(0, 2) as i:

                def add(pair):
                    dve.wait_ge(scored, 4 * i + 2 * pair + 2)
                    x = k.S[:, 2 * pair:2 * pair + 2]
                    y = sc[:, pair, 0:352].rearrange("p (b c h) -> p b c h", b=2, h=H)
                    z = k.BB[:, bass.ds(i, 1), pair * 352:(pair + 1) * 352].rearrange("p a (b c h) -> p (a b) c h", b=2, h=H)
                    for c0, c1, m in ((0, 16, P), (17, 21, P), (16, 17, B), (21, 22, B)):
                        nc.vector.tensor_tensor(x[0:m, :, c0:c1, :], y[0:m, :, c0:c1, :], z[0:m, :, c0:c1, :], ALU.add).then_inc(added, 1)

                for u in range(1, 20, 2):
                    dve.wait_ge(tr_done, 20 * i + u + 1)
                    nc.vector.tensor_copy(kT[:, u % 4, :], tp[:, u % 4, :]).then_inc(copied_odd, 1)
                    if u == 13:
                        add(0)
                add(1)
                dve.wait_ge(added, 8 * i + 8)
                for r, (c0, c1) in enumerate(parts):
                    nc.vector.tensor_reduce(M1.rearrange(by_branch, r=2, b=4)[:, r], k.S[:, :, c0:c1, :].rearrange("p b c h -> p b h c"),
                                            AX, ALU.max).then_inc(maxed, 1)
                dve.wait_ge(max_turned, i + 1)
                nc.vector.tensor_reduce(m1, mt[0:64, 0:P], AX, ALU.max).then_inc(max_out, 1)
                dve.wait_ge(max_out, i + 1)
                nc.vector.tensor_scalar(dg, k.ident[0:64, 0:64], m1, None, ALU.mult).then_inc(diag, 1)
                dve.wait_ge(max_spread, i + 1)
                for r, (c0, c1) in enumerate(parts):
                    mx = misc[:, 32 * r:32 * r + 32].rearrange("p (b h) -> p b h", b=4).unsqueeze(2).to_broadcast([P, 4, c1 - c0, H])
                    nc.vector.tensor_tensor(pb[:, :, c0:c1, :], k.S[:, :, c0:c1, :], mx, ALU.subtract).then_inc(centred, 1)
                dve.wait_ge(exped, i + 1)
                for r, (c0, c1) in enumerate(parts):
                    nc.vector.tensor_reduce(L1.rearrange(by_branch, r=2, b=4)[:, r], pb[:, :, c0:c1, :].rearrange("p b c h -> p b h c"),
                                            AX, ALU.add).then_inc(summed, 1)
                dve.wait_ge(sum_spread, i + 1)
                nc.vector.reciprocal(F, misc[:, 64:128]).then_inc(inverted, 1)
                dve.wait_ge(inverted, i + 1)
                gates = k.GT.rearrange("p (r x) -> p r x", r=2)[:, :, bass.ds(32 * i, 32)]
                nc.vector.tensor_tensor(F.rearrange("p (r x) -> p r x", r=2), F.rearrange("p (r x) -> p r x", r=2), gates,
                                        ALU.mult).then_inc(factor, 1)
                dve.wait_ge(factor, i + 1)
                for r, (c0, c1) in enumerate(parts):
                    f = F[:, 32 * r:32 * r + 32].rearrange("p (b h) -> p b h", b=4).unsqueeze(2).to_broadcast([P, 4, c1 - c0, H])
                    nc.vector.tensor_tensor(pb[:, :, c0:c1, :], pb[:, :, c0:c1, :], f, ALU.mult).then_inc(p_ready, 1)
                dve.wait_ge(pv_done, 4 * i + 4)
                for j in range(4):
                    rows = slice(32 * j, 32 * j + H)
                    nc.vector.tensor_copy(OH[rows], mt[rows, P:2 * P]).then_inc(o_copied, 1)
                dve.wait_ge(o_turned, i + 1)
                for gr in range(2):
                    h0 = slice(gr * HD, (gr + 1) * HD)
                    nc.vector.tensor_tensor(k.ON[h0, :, bass.ds(4 * i + T, 4)],
                                            misc[h0, P:2 * P].rearrange("p (b h) -> p h b", b=4)[:, 4 * gr:4 * gr + 4, :],
                                            k.OC[h0, bass.ds(4 * i, 4), 4 * gr:4 * gr + 4].rearrange("p b h -> p h b"),
                                            ALU.add).then_inc(o_done, 1)
            dve.wait_ge(o_done, 4)




def bias_tables(k):
    nc, g = k.nc, k.g
    with Stage(k, "bias") as st:
        ps = st.psum("ps", [P, 4, 512])
        pc = st.psum("pc", [P, 512])
        const_in, repeated, row_done, row_out, shifted, turned_in, cmp_done, cmp_set, cmp_out, gates = st.sems(
            "const_in repeated row_done row_out shifted turned_in cmp_done cmp_set cmp_out gates")
        RB = k.Hr[0:33, 0:1024].rearrange("p (h m) -> p h m", h=H)
        ohn = k.Hr[0:33, 1024:1408]
        TB = k.Hr[:, 1408:4480].rearrange("p (h x) -> p h x", h=H)
        ohc = k.Hr[0:33, 4480:6400]
        hb = k.tiny[:, 0:1]
        block = st.block()

        @block.sync
        def _(sp):
            sp.dma_start(ohn, g["oh_near"]).then_inc(const_in, 16)
            sp.dma_start(ohc, g["oh_cmp"]).then_inc(const_in, 16)
            sp.dma_start(k.WM, g["window_edge"]).then_inc(const_in, 16)
            sp.dma_start(hb, g["has_block"]).then_inc(const_in, 16)
            sp.wait_ge(row_out, H)
            sp.dma_start(k.scratch.rearrange("h (i x) -> i h x", i=P), TB).then_inc(shifted, 16)
            sp.wait_ge(shifted, 16)
            sp.dma_start(k.NB, k.scratch[:, 127:127 + P * 383].rearrange("h (i w) -> i h w", w=383)[:, :, 0:256]).then_inc(turned_in, 16)
            sp.wait_ge(turned_in, 16)

        @block.tensor
        def _(pe):
            pe.wait_ge(const_in, 64)
            for m in range(15):
                last = nc.tensor.matmul(pc[:, m * H:(m + 1) * H], ohc[:, m * P:(m + 1) * P], k.relb[:], start=True, stop=True)
            last.then_inc(cmp_done, 1)
            pe.wait_ge(repeated, 1)
            for h in range(H):
                if h >= 4:
                    pe.wait_ge(row_out, h - 3)
                nc.tensor.matmul(ps[:, h % 4, 0:384], RB[:, h, :], ohn, start=True, stop=True).then_inc(row_done, 1)

        @block.scalar
        def _(act):
            for h in range(H):
                act.wait_ge(row_done, h + 1)
                nc.scalar.activation(TB[:, h, :], ps[:, h % 4, 0:384], ACT.Copy).then_inc(row_out, 1)

        @block.vector
        def _(dve):
            nc.vector.tensor_copy(RB, k.relb[:].unsqueeze(2).to_broadcast([33, H, P])).then_inc(repeated, 1)
            nc.vector.memset(k.BC[:, :, 0:48], 0.0).then_inc(cmp_set, 1)
            nc.vector.memset(k.BC[:, :, 63:119], NEG).then_inc(cmp_set, 1)
            dve.wait_ge(cmp_done, 1)
            nc.vector.tensor_copy(k.BC[:, :, 48:63], pc[:, 0:120].rearrange("p (m h) -> p h m", h=H)).then_inc(cmp_set, 1)
            dve.wait_ge(const_in, 64)
            g0 = k.gtok[:, 0, :].rearrange("p (h r) -> p h r", r=3)[:, :, 0]
            nc.vector.tensor_scalar(g0, g0, hb, None, ALU.mult).then_inc(gates, 1)
            dve.wait_ge(gates, 1)
            dve.wait_ge(cmp_set, 3)


def prompt_attention(k):
    nc = k.nc
    with Stage(k, "att") as st:
        sS = st.psum("slc", [P, 1024])
        sW = st.psum("win", [P, 1024])
        tp = st.psum("tp", [P, 2, 512])
        op = st.psum("op", [P, 512])
        q_ready, scored_s, scored_w, exp_s, exp_w, exp_c, biased, negated, factor, p_ready, pt_done, pt_copied, pv_done, o_copied, turn_cmp = st.sems(
            "q_ready scored_s scored_w exp_s exp_w exp_c biased negated factor p_ready pt_done pt_copied pv_done o_copied turn_cmp")
        PR = [k.Hr[:, 0:1728], k.Hr[:, 1728:3456]]
        PT = [k.Hr[:, 3456:5248], k.Hr[:, 5248:7040]]
        QB = [k.Hr[:, 7040:7168], k.Hr[:, 7296:7424]]
        nm = [k.Hr[:, 7168:7171], k.Hr[:, 7176:7179]]
        l = [k.Hr[:, 7184:7187], k.Hr[:, 7192:7195]]
        cc = [k.Hr[:, 7200:7203], k.Hr[:, 7208:7211]]
        CMP = 640
        plan, groups = [], 0
        for t in range(TT):
            wb = list(range(max(0, t - 4), t + 1))
            ng = -(-(t + 1 + len(wb)) // 4) + 1
            plan.append((t, wb, ng, groups))
            groups += 8 * ng
        x_back, = st.sems("x_back")
        block = st.block()


        @block.sync
        def _(sp):
            sp.dma_start(k.X[:].rearrange("p c t -> p (c t)"), k.kept).then_inc(x_back, 16)
            sp.wait_ge(x_back, 16)

        @block.tensor
        def _(pe):
            def scores(tile, c, gr):
                t, wb, ng, g0 = tile
                s = 2 * c + gr + 8 * t
                if gr == 0:
                    pe.wait_ge(q_ready, 2 * c + 8 * t + 4)
                pe.wait_ge(exp_s, s + 1)
                w = (t + 1) * P
                for a in range(0, w, 512):
                    e = min(w, a + 512)
                    last = nc.tensor.matmul(sS[:, a:e], QB[gr], k.KT[:, 0, a:e], start=True, stop=True)
                last.then_inc(scored_s, 1)
                pe.wait_ge(exp_w, s + 1)
                pe.wait_ge(exp_c, s + 1)
                w = len(wb) * P
                for a in range(0, w, 512):
                    e = min(w, a + 512)
                    nc.tensor.matmul(sW[:, a:e], QB[gr], k.KT[:, 1, wb[0] * P + a:wb[0] * P + e], start=True, stop=True)
                nc.tensor.matmul(sW[:, CMP:CMP + NCP], QB[gr], k.KC[:, 8, 0:NCP], start=True, stop=True).then_inc(scored_w, 1)

            def turns_and_products(tile, c, gr):
                t, wb, ng, g0 = tile
                s = 2 * c + gr + 8 * t
                pe.wait_ge(p_ready, 3 * s + 3)
                cols = [P * j for j in range(t + 1)] + [1024 + P * j for j in range(len(wb))]
                for q in range(ng):
                    pe.wait_ge(pt_copied, (2 * c + gr) * ng + (g0 + q + 1))
                    bank = (gr * ng + q) % 2
                    if q < ng - 1:
                        for j, a in enumerate(cols[4 * q:4 * q + 4]):
                            last = nc.tensor.transpose(tp[:, bank, j * P:(j + 1) * P], PR[gr][:, a:a + P], k.ident[:])
                    else:
                        pe.sem_inc(turn_cmp, 1)
                        last = nc.tensor.transpose(tp[0:NCP, bank, 0:P], PR[gr][:, 1664:1664 + NCP], k.ident[:])
                    last.then_inc(pt_done, 1)
                if gr == 0:
                    pe.wait_ge(o_copied, c + 4 * t + 1)
                o = op[gr * HD:(gr + 1) * HD, 0:P]
                kv = [(b, 384) for b in range(t + 1)] + [(b, 640) for b in wb]
                for j, (b, f) in enumerate(kv):
                    if j % 4 == 0:
                        pe.wait_ge(pt_copied, (2 * c + gr) * ng + g0 + 3 + j // 4 + (j // 4 == ng - 2))
                    nc.tensor.matmul(o, k.kvtok[:, b, f + gr * HD:f + (gr + 1) * HD], PT[gr][:, j * P:(j + 1) * P],
                                     start=(j == 0), stop=False)
                nc.tensor.matmul(o, k.VC[0:NCP, 8, gr * HD:(gr + 1) * HD], PT[gr][0:NCP, len(kv) * P:(len(kv) + 1) * P],
                                 start=False, stop=True).then_inc(pv_done, 1)

            pe.sem_inc(scored_w, 1)
            pe.sem_inc(pv_done, 2)
            for tile in plan:
                scores(tile, 0, 0)
                if tile[0]:
                    turns_and_products(plan[tile[0] - 1], 3, 1)
                scores(tile, 0, 1)
                turns_and_products(tile, 0, 0)
                with pe.Fori(1, 4) as c:
                    scores(tile, c, 0)
                    turns_and_products(tile, c - 1, 1)
                    scores(tile, c, 1)
                    turns_and_products(tile, c, 0)
            turns_and_products(plan[-1], 3, 1)

        @block.scalar
        def _(act):
            def exps(tile, c, gr):
                t, wb, ng, g0 = tile
                s = 2 * c + gr + 8 * t
                act.wait_ge(pv_done, s + 1)
                for j, (done, src, dst) in enumerate((
                        (exp_s, sS[:, 0:(t + 1) * P], PR[gr][:, 0:(t + 1) * P]),
                        (exp_w, sW[:, 0:len(wb) * P], PR[gr][:, 1024:1024 + len(wb) * P]),
                        (exp_c, sW[:, CMP:CMP + NCP], PR[gr][:, 1664:1664 + NCP]))):
                    act.wait_ge(negated, 3 * s + (1, 3, 3)[j])
                    nc.scalar.activation(dst, src, ACT.Exp, bias=nm[gr][:, j:j + 1],
                                         accum_out=l[gr][:, (j + 1) % 3:(j + 1) % 3 + 1]).then_inc(done, 1)

            def copies(tile, c, gr):
                t, wb, ng, g0 = tile
                nb = t + 1 + len(wb)
                for q in range(ng):
                    act.wait_ge(pt_done, (2 * c + gr) * ng + (g0 + q + 1))
                    bank = (gr * ng + q) % 2
                    if q < ng - 1:
                        m = min(4, nb - 4 * q) * P
                        nc.scalar.activation(PT[gr][:, 512 * q:512 * q + m], tp[:, bank, 0:m], ACT.Copy).then_inc(pt_copied, 1)
                    else:
                        nc.scalar.activation(PT[gr][0:NCP, nb * P:(nb + 1) * P], tp[0:NCP, bank, 0:P], ACT.Copy).then_inc(pt_copied, 1)

            def output(tile, c):
                t = tile[0]
                act.wait_ge(pv_done, 2 * c + 8 * t + 4)
                nc.scalar.activation(k.ON[:, bass.ds(c, 1), t * P:(t + 1) * P].rearrange("p a t -> p (a t)"), op[:, 0:P],
                                     ACT.Copy).then_inc(o_copied, 1)

            for x in (exp_s, exp_w, exp_c, o_copied):
                act.sem_inc(x, 1)
            act.sem_inc(pt_copied, 2)
            for tile in plan:
                if tile[0]:
                    copies(plan[tile[0] - 1], 3, 1)
                exps(tile, 0, 0)
                if tile[0]:
                    output(plan[tile[0] - 1], 3)
                copies(tile, 0, 0)
                exps(tile, 0, 1)
                with act.Fori(1, 4) as c:
                    copies(tile, c - 1, 1)
                    exps(tile, c, 0)
                    output(tile, c - 1)
                    copies(tile, c, 0)
                    exps(tile, c, 1)
            copies(plan[-1], 3, 1)
            output(plan[-1], 3)

        @block.vector
        def _(dve):
            def queries(tile, c):
                t = tile[0]
                dve.wait_ge(scored_w, 2 * c + 8 * t + 1)
                for gr in range(2):
                    rows = slice(gr * HD, (gr + 1) * HD)
                    nc.vector.tensor_copy(QB[gr][rows], k.Q[rows, bass.ds(c, 1), t * P:(t + 1) * P].rearrange("p a t -> p (a t)")).then_inc(q_ready, 1)

            def biases_and_maxima(tile, c, gr):
                t, wb, ng, g0 = tile
                s = 2 * c + gr + 8 * t
                near = min(t + 1, 2) * P
                adds = 3 + (len(wb) == 5)
                ab = (2 * c + gr) * adds + sum(8 * (3 + (x >= 4)) for x in range(t))
                hd = bass.ds(c + 4 * gr, 1)
                nb = k.NB[:, hd, 256 - near:256].rearrange("p a j -> p (a j)")
                dve.wait_ge(scored_s, s + 1)
                x = sS[:, (t + 1) * P - near:(t + 1) * P]
                nc.vector.tensor_tensor(x, x, nb, ALU.add).then_inc(biased, 1)
                dve.wait_ge(biased, ab + 1)
                nc.vector.tensor_reduce(nm[gr][:, 0:1], sS[:, 0:(t + 1) * P], AX, ALU.max, negate=True).then_inc(negated, 1)
                dve.wait_ge(scored_w, s + 2)
                w = len(wb) * P
                x = sW[:, w - near:w]
                nc.vector.tensor_tensor(x, x, nb, ALU.add).then_inc(biased, 1)
                if len(wb) == 5:
                    nc.vector.tensor_tensor(sW[:, 0:P], sW[:, 0:P], k.WM, ALU.add).then_inc(biased, 1)
                x = sW[:, CMP:CMP + NCP]
                a = 56 - 8 * t
                nc.vector.tensor_tensor(x, x, k.BC[:, hd, a:a + NCP].rearrange("p a m -> p (a m)"), ALU.add).then_inc(biased, 1)
                dve.wait_ge(biased, ab + adds)
                nc.vector.tensor_reduce(nm[gr][:, 1:2], sW[:, 0:w], AX, ALU.max, negate=True).then_inc(negated, 1)
                nc.vector.tensor_reduce(nm[gr][:, 2:3], x, AX, ALU.max, negate=True).then_inc(negated, 1)

            def scaling(tile, c, gr):
                t, wb, ng, g0 = tile
                s = 2 * c + gr + 8 * t
                for done in (exp_s, exp_w, exp_c):
                    dve.wait_ge(done, s + 2)
                nc.vector.reciprocal(cc[gr], l[gr]).then_inc(factor, 1)
                dve.wait_ge(factor, 2 * s + 1)
                gates = k.gtok[:, t, :].rearrange("p (h r) -> p h r", r=3)[:, bass.ds(c + 4 * gr, 1), :]
                nc.vector.tensor_tensor(cc[gr], cc[gr], gates.rearrange("p a r -> p (a r)"), ALU.mult).then_inc(factor, 1)
                dve.wait_ge(factor, 2 * s + 2)
                for j, (a, w) in enumerate(((0, (t + 1) * P), (1024, len(wb) * P), (1664, NCP))):
                    x = PR[gr][:, a:a + w]
                    f = (j + 1) % 3
                    nc.vector.tensor_scalar(x, x, cc[gr][:, f:f + 1], None, ALU.mult).then_inc(p_ready, 1)

            for gr in range(2):
                nc.vector.memset(QB[gr][(1 - gr) * HD:(2 - gr) * HD], 0.0).then_inc(q_ready, 1)
            queries(plan[0], 0)
            for tile in plan:
                if tile[0]:
                    scaling(plan[tile[0] - 1], 3, 1)
                biases_and_maxima(tile, 0, 0)
                scaling(tile, 0, 0)
                biases_and_maxima(tile, 0, 1)
                with dve.Fori(1, 4) as c:
                    queries(tile, c)
                    scaling(tile, c - 1, 1)
                    biases_and_maxima(tile, c, 0)
                    scaling(tile, c, 0)
                    biases_and_maxima(tile, c, 1)
                if tile[0] < TT - 1:
                    queries(plan[tile[0] + 1], 0)
            scaling(plan[-1], 3, 1)


def merge(k):
    nc, g, w = k.nc, k.g, k.g["w_in"]
    with Stage(k, "merge") as st:
        acc = st.psum("acc", [P, 2, NT, 512])
        mm = st.sems("gates_done branch_done")
        sig, gated, merged, slot_open, hi_done, split_done, slot_ok = st.sems(
            "sig gated merged slot_open hi_done split_done slot_ok")
        SA = chunks(k.E[:, 0:2 * N], 2)
        TM = chunks(k.E[:, 2 * N:4 * N], 2)
        h = NormSplit(k, st, 0, k.R1[:])
        base = list(k.wcount)
        k.wcount[0] += 8 * 32
        k.wcount[1] += 8 * 48
        nsa = g["w_branch_nsa"].rearrange("(gr c d) m -> gr d c m", gr=2, d=HD)
        block = st.block()

        @block.sync
        def _(sp):
            with sp.Fori(0, 8) as m:
                for j in range(2):
                    sp.wait_ge(split_done, 2 * m + j + 1)
                    sp.dma_start(k.W[:, 0, 0:8, :], weight(w, m * P + (GA0, GB0)[j])).then_inc(k.wfull[0], 16)
                    sp.wait_ge(mm[1], 2 * m + j + 1)
                    sp.sem_inc(slot_open, 1)
                    if j == 0:
                        for gr in range(2):
                            sp.dma_start(k.W[gr * HD:(gr + 1) * HD, 1, 0:4, :], nsa[gr][:, :, bass.ds(m * P, P)]).then_inc(k.wfull[1], 16)
                    else:
                        sp.dma_start(k.W[:, 1, 0:4, :], weight(g["w_branch_gm"], m * P)).then_inc(k.wfull[1], 16)

        @block.tensor
        def _(pe):
            pe.sem_inc(mm[0], 1)
            pe.sem_inc(mm[1], 1)
            with pe.Fori(0, 8) as m:
                for j in range(2):
                    pe.wait_ge(split_done, 2 * m + j + 2)
                    pe.wait_ge(sig, 2 * m + j + 2)
                    split_tile(k, acc, 0, j, k.HH, k.HL, DC, wait=(pe, h.lo_done) if j == 0 else None).then_inc(mm[0], 1)
                    pe.wait_ge(k.wfull[1], 48 * m + base[1] + (32, 48)[j])
                    pe.wait_ge(gated, 2 * m + j + 2)
                    gemm_tile(k, acc, 1, (k.ON, k.OG)[j], 4).then_inc(mm[1], 1)

        @block.gpsimd
        def _(pool):
            pool.sem_inc(split_done, 1)
            with pool.Fori(0, 8) as m:
                for j in range(2):
                    pool.wait_ge(k.wfull[0], 32 * m + base[0] + 16 * j + 16)
                    pool.wait_ge(sig, 2 * m + j + 1)
                    pool.sem_inc(slot_ok, 1)
                    split_weights(k, pool, 0, j, DC, hi_done, 2 * m + j, split_done)

        @block.scalar
        def _(act):
            act.sem_inc(sig, 2)
            h.scalar(act)
            with act.Fori(0, 8) as m:
                for j in range(2):
                    act.wait_ge(mm[0], 2 * m + j + 2)
                    act.wait_ge(gated, 2 * m + j + 1)
                    nc.scalar.activation(tokens(SA[:, j, :]), acc[:, 0, :, 0:NW], ACT.Sigmoid).then_inc(sig, 1)

        @block.vector
        def _(dve):
            dve.sem_inc(gated, 2)
            dve.sem_inc(merged, 1)
            h.vector(dve)
            with dve.Fori(0, 8) as m:
                dve.wait_ge(merged, m + 1)
                for j in range(2):
                    dve.wait_ge(sig, 2 * m + j + 3)
                    dve.wait_ge(mm[1], 2 * m + j + 2)
                    nc.vector.tensor_tensor(tokens(TM[:, j, :]), tokens(SA[:, j, :]), acc[:, 1, :, 0:NW], ALU.mult).then_inc(gated, 1)
                dve.wait_ge(gated, 2 * m + 4)
                nc.vector.tensor_tensor(k.MT[:, bass.ds(m, 1), :].rearrange("p a t -> p (a t)"), TM[:, 0, :], TM[:, 1, :],
                                        ALU.add).then_inc(merged, 1)
            dve.wait_ge(merged, 9)


def one(ap, m):
    return tokens(ap[:, bass.ds(m, 1), :].rearrange("p a t -> p (a t)"))


def out_projection(k):
    nc, g = k.nc, k.g
    with Stage(k, "out") as st:
        acc = st.psum("acc", [P, 2, NT, 512])
        mm_done, acc_free, hi_done, split_done, slot_ok, m_hi, m_lo, x_back = st.sems(
            "mm_done acc_free hi_done split_done slot_ok m_hi m_lo x_back")
        squares = SquareSum(k, st)
        base = list(k.wcount)
        for s in range(2):
            k.wcount[s] += 4 * 16
        block = st.block()

        @block.sync
        def _(sp):
            with sp.Fori(0, 4) as i:
                for s in range(2):
                    sp.wait_ge(split_done, 2 * i + s + 1)
                    sp.dma_start(k.W[:, s, :, :], weight(g["w_out"], (2 * i + s) * P)).then_inc(k.wfull[s], 16)
            sp.wait_ge(m_lo, DC)
            sp.dma_start(k.Z[:, 0:DC * N], k.kept).then_inc(x_back, 16)
            sp.wait_ge(x_back, 16)

        @block.gpsimd
        def _(pool):
            pool.sem_inc(split_done, 2)
            with pool.Fori(0, 4) as i:
                for s in range(2):
                    pool.wait_ge(k.wfull[s], 16 * i + base[s] + 16)
                    pool.wait_ge(mm_done, 2 * i + s + 1)
                    pool.sem_inc(slot_ok, 1)
                    split_weights(k, pool, s, s, DC, hi_done, 2 * i + s, split_done)

        @block.tensor
        def _(pe):
            pe.sem_inc(mm_done, 2)
            with pe.Fori(0, 4) as i:
                for s in range(2):
                    pe.wait_ge(split_done, 2 * i + s + 3)
                    pe.wait_ge(acc_free, 2 * i + s + 1)
                    split_tile(k, acc, s, s, k.HH, k.HL, DC, wait=(pe, m_lo) if s == 0 else None).then_inc(mm_done, 1)

        @block.scalar
        def _(act):
            act.sem_inc(acc_free, 2)
            for c in range(DC):
                nc.scalar.activation(k.HH[:, c, :], k.MT[:, c, :], ACT.Copy).then_inc(m_hi, 1)
            with act.Fori(0, 4) as i:
                for s in range(2):
                    act.wait_ge(mm_done, 2 * i + s + 3)
                    nc.scalar.activation(one(k.MX, 2 * i + s), acc[:, s, :, 0:NW], ACT.Copy).then_inc(acc_free, 1)
                    act.wait_ge(acc_free, 2 * i + s + 3)
                    squares.square(act, one(k.MX, 2 * i + s), 2 * i + s, s)
            act.wait_ge(acc_free, 10)

        @block.vector
        def _(dve):
            for c in range(DC):
                dve.wait_ge(m_hi, c + 1)
                nc.vector.tensor_tensor(k.HL[:, c, :], k.MT[:, c, :], k.HH[:, c, :].bitcast(F32), ALU.subtract).then_inc(m_lo, 1)
            squares.start(dve)
            with dve.Fori(0, 4) as i:
                for s in range(2):
                    squares.add(dve, 2 * i + s, s)
            dve.wait_ge(squares.summed, DC + 2)


def ffn(k):
    nc, g = k.nc, k.g
    with Stage(k, "ffn") as st:
        acc = st.psum("acc", [P, 2, NT, 512])
        gate_done, up_done, silu_done, gated, down_done, acc_free, hi_done, split_done, slot_ok, a_hi, a_lo, x_back = st.sems(
            "gate_done up_done silu_done gated down_done acc_free hi_done split_done slot_ok a_hi a_lo x_back")
        done = (gate_done, up_done)
        free = (silu_done, gated)
        SL = k.E[:, 0:N]
        GU = k.E[:, N:2 * N]
        h = NormSplit(k, st, 2, k.E[:, 0:N])
        squares = SquareSum(k, st)
        base = list(k.wcount)
        parts = []
        for p, nf in enumerate(FFN_PARTS):
            m0 = sum(FFN_PARTS[:p])
            parts.append((nf, m0, 2 * m0 + 8 * p, m0 + 4 * p, 8 * p))
        for s in range(2):
            k.wcount[s] += (sum(FFN_PARTS) + 4 * len(FFN_PARTS)) * 16
        block = st.block()

        @block.sync
        def _(sp):
            for nf, m0, t0, s0, d0 in parts:
                with sp.Fori(0, nf) as m:
                    for s in range(2):
                        sp.wait_ge(split_done, 2 * m + (t0 + s + 1))
                        sp.dma_start(k.W[:, s, :, :], weight(g[("w_ffn_gate", "w_ffn_up")[s]], m * P + m0 * P)).then_inc(k.wfull[s], 16)
                with sp.Fori(0, 4) as i:
                    for s in range(2):
                        sp.wait_ge(split_done, 2 * i + (t0 + 2 * nf + s + 1))
                        sp.dma_start(k.W[:, s, 0:nf, :], weight(g["w_ffn_down"][m0 * P:(m0 + nf) * P, :], (2 * i + s) * P)).then_inc(k.wfull[s], 16)
            sp.wait_ge(gate_done, sum(FFN_PARTS) + 1)
            sp.wait_ge(up_done, sum(FFN_PARTS) + 1)
            sp.dma_start(k.X[:].rearrange("p c t -> p (c t)"), k.kept).then_inc(x_back, 16)
            sp.wait_ge(x_back, 16)

        @block.gpsimd
        def _(pool):
            pool.sem_inc(split_done, 2)
            for nf, m0, t0, s0, d0 in parts:
                for s in range(2):
                    pool.wait_ge(k.wfull[s], base[s] + 16 * s0 + 16)
                    pool.wait_ge(down_done, d0 + s + 1)
                    split_weights(k, pool, s, s, DC, hi_done, t0 + s, split_done)
                with pool.Fori(1, nf) as m:
                    for s in range(2):
                        pool.wait_ge(k.wfull[s], 16 * m + (base[s] + 16 * s0 + 16))
                        pool.wait_ge(done[s], m + (m0 + 1))
                        pool.sem_inc(slot_ok, 1)
                        split_weights(k, pool, s, s, DC, hi_done, 2 * m + (t0 + s), split_done)
                for s in range(2):
                    pool.wait_ge(k.wfull[s], base[s] + 16 * (s0 + nf) + 16)
                    pool.wait_ge(done[s], m0 + nf + 1)
                    split_weights(k, pool, s, s, nf, hi_done, t0 + 2 * nf + s, split_done)
                with pool.Fori(1, 4) as i:
                    for s in range(2):
                        pool.wait_ge(k.wfull[s], 16 * i + (base[s] + 16 * (s0 + nf) + 16))
                        pool.wait_ge(down_done, 2 * i + (d0 + s + 1))
                        pool.sem_inc(slot_ok, 1)
                        split_weights(k, pool, s, s, nf, hi_done, 2 * i + (t0 + 2 * nf + s), split_done)

        @block.tensor
        def _(pe):
            pe.sem_inc(gate_done, 1)
            pe.sem_inc(up_done, 1)
            pe.sem_inc(down_done, 2)
            for nf, m0, t0, s0, d0 in parts:
                for s in range(2):
                    pe.wait_ge(split_done, t0 + s + 3)
                    pe.wait_ge(acc_free, d0 + s + 1)
                    split_tile(k, acc, s, s, k.HH, k.HL, DC, wait=(pe, h.lo_done) if t0 + s == 0 else None).then_inc(done[s], 1)
                with pe.Fori(1, nf) as m:
                    for s in range(2):
                        pe.wait_ge(split_done, 2 * m + (t0 + s + 3))
                        pe.wait_ge(free[s], m + (m0 + 1))
                        split_tile(k, acc, s, s, k.HH, k.HL, DC).then_inc(done[s], 1)
                for s in range(2):
                    pe.wait_ge(split_done, t0 + 2 * nf + s + 3)
                    pe.wait_ge(free[s], m0 + nf + 1)
                    if s == 0:
                        pe.wait_ge(a_lo, m0 + nf)
                        split_tile(k, acc, s, s, k.AH, k.AL, nf - 1, more=True)
                        pe.wait_ge(a_lo, m0 + nf + 1)
                        split_tile(k, acc, s, s, k.AH, k.AL, nf, first=nf - 1).then_inc(down_done, 1)
                    else:
                        split_tile(k, acc, s, s, k.AH, k.AL, nf).then_inc(down_done, 1)
                with pe.Fori(1, 4) as i:
                    for s in range(2):
                        pe.wait_ge(split_done, 2 * i + (t0 + 2 * nf + s + 3))
                        pe.wait_ge(acc_free, 2 * i + (d0 + s + 1))
                        split_tile(k, acc, s, s, k.AH, k.AL, nf).then_inc(down_done, 1)

        @block.scalar
        def _(act):
            act.sem_inc(silu_done, 1)
            act.sem_inc(acc_free, 2)
            h.scalar(act)
            for nf, m0, t0, s0, d0 in parts:
                with act.Fori(0, nf) as m:
                    act.wait_ge(gate_done, m + (m0 + 2))
                    act.wait_ge(gated, m + (m0 + 1))
                    nc.scalar.activation(tokens(SL), acc[:, 0, :, 0:NW], ACT.Silu).then_inc(silu_done, 1)
                    act.wait_ge(gated, m + (m0 + 2))
                    nc.scalar.activation(one(k.AH, m), tokens(GU), ACT.Copy).then_inc(a_hi, 1)
                if d0 == 0:
                    with act.Fori(0, 4) as i:
                        for s in range(2):
                            act.wait_ge(down_done, 2 * i + s + 3)
                            nc.scalar.activation(one(k.F, 2 * i + s), acc[:, s, :, 0:NW], ACT.Copy).then_inc(acc_free, 1)
                if nf + m0 == sum(FFN_PARTS):
                    with act.Fori(0, 4) as i:
                        for s in range(2):
                            act.wait_ge(acc_free, 2 * i + (d0 + s + 3))
                            squares.square(act, one(k.F, 2 * i + s), 2 * i + s, s)

        @block.vector
        def _(dve):
            dve.sem_inc(gated, 1)
            dve.sem_inc(a_lo, 1)
            h.vector(dve)
            for nf, m0, t0, s0, d0 in parts:
                with dve.Fori(0, nf) as m:
                    dve.wait_ge(silu_done, m + (m0 + 2))
                    dve.wait_ge(up_done, m + (m0 + 2))
                    dve.wait_ge(a_lo, m + (m0 + 1))
                    nc.vector.tensor_tensor(tokens(GU), tokens(SL), acc[:, 1, :, 0:NW], ALU.mult).then_inc(gated, 1)
                    dve.wait_ge(a_hi, m + (m0 + 1))
                    nc.vector.tensor_tensor(one(k.AL, m), tokens(GU), one(k.AH, m).bitcast(F32), ALU.subtract).then_inc(a_lo, 1)
                last_part = nf + m0 == sum(FFN_PARTS)
                if last_part:
                    squares.start(dve)
                if d0:
                    with dve.Fori(0, 4) as i:
                        for s in range(2):
                            dve.wait_ge(down_done, 2 * i + (d0 + s + 3))
                            dve.wait_ge(acc_free, 2 * i + (d0 - 8 + s + 3))
                            nc.vector.tensor_tensor(one(k.F, 2 * i + s), one(k.F, 2 * i + s), acc[:, s, :, 0:NW],
                                                    ALU.add).then_inc(acc_free, 1)
                            if last_part:
                                squares.add(dve, 2 * i + s, s)
            dve.wait_ge(acc_free, 8 * len(parts) + 2)
            dve.wait_ge(squares.summed, DC + 2)


def ple(k):
    nc, g = k.nc, k.g
    with Stage(k, "ple") as st:
        acc = st.psum("acc", [P, 2, NT, 512])
        tp = st.psum("tp", [P, 2, 512])
        p_in, tr_done, tr_copied, gate_done, e_done, sig, gated, hi_done, split_done, slot_ok, x_hi, x_lo = st.sems(
            "p_in tr_done tr_copied gate_done e_done sig gated hi_done split_done slot_ok x_hi x_lo")
        ptok = k.E[:, 2 * N:2 * N + 9 * 256].rearrange("p (t f) -> p t f", f=256)
        pT = chunks(k.Z[:, 8 * N:10 * N], 2)
        SA = k.E[:, 0:N]
        squares = SquareSum(k, st)
        base = list(k.wcount)
        for s in range(2):
            k.wcount[s] += 8 * 16
        block = st.block()

        @block.sync
        def _(sp):
            sp.dma_start(ptok[:, 0:TT, :], g["p_prompt"].rearrange("(t p) f -> p t f", p=P)).then_inc(p_in, 16)
            sp.dma_start(ptok[0:B, TT, :], g["p_sample"]).then_inc(p_in, 16)
            with sp.Fori(0, 8) as m:
                sp.wait_ge(split_done, m + 1)
                sp.dma_start(k.W[:, 0, 0:8, :], weight(g["w_ple_gate"], m * P)).then_inc(k.wfull[0], 16)
                sp.wait_ge(e_done, m + 1)
                sp.dma_start(k.W[:, 1, 0:2, :], weight(g["w_ple"], m * P)).then_inc(k.wfull[1], 16)

        @block.tensor
        def _(pe):
            pe.sem_inc(gate_done, 1)
            pe.sem_inc(e_done, 1)
            pe.wait_ge(p_in, 32)
            for c in range(2):
                for q in range(3):
                    n = 3 * c + q
                    if n >= 2:
                        pe.wait_ge(tr_copied, n - 1)
                    if q < 2:
                        for t in range(4):
                            last = nc.tensor.transpose(tp[:, n % 2, t * P:(t + 1) * P], ptok[:, 4 * q + t, c * P:(c + 1) * P], k.ident[:])
                    else:
                        last = nc.tensor.transpose(tp[:, n % 2, 0:B], ptok[0:B, TT, c * P:(c + 1) * P], k.ident[0:B, 0:B])
                    last.then_inc(tr_done, 1)
            pe.wait_ge(tr_copied, 6)
            with pe.Fori(0, 8) as m:
                pe.wait_ge(split_done, m + 2)
                pe.wait_ge(sig, m + 1)
                split_tile(k, acc, 0, 0, k.HH, k.XL, DC, wait=(pe, x_lo)).then_inc(gate_done, 1)
                pe.wait_ge(k.wfull[1], 16 * m + base[1] + 16)
                pe.wait_ge(gated, m + 1)
                gemm_tile(k, acc, 1, pT, 2).then_inc(e_done, 1)

        @block.gpsimd
        def _(pool):
            pool.sem_inc(split_done, 1)
            with pool.Fori(0, 8) as m:
                pool.wait_ge(k.wfull[0], 16 * m + base[0] + 16)
                pool.wait_ge(gate_done, m + 1)
                pool.sem_inc(slot_ok, 1)
                split_weights(k, pool, 0, 0, DC, hi_done, m, split_done)

        @block.scalar
        def _(act):
            act.sem_inc(sig, 1)
            for c in range(DC):
                nc.scalar.activation(k.HH[:, c, :], k.X[:, c, :], ACT.Copy).then_inc(x_hi, 1)
            with act.Fori(0, 8) as m:
                act.wait_ge(gate_done, m + 2)
                act.wait_ge(gated, m + 1)
                nc.scalar.activation(tokens(SA), acc[:, 0, :, 0:NW], ACT.Sigmoid).then_inc(sig, 1)
                act.wait_ge(gated, m + 2)
                squares.square(act, one(k.F, m), m, 0)

        @block.vector
        def _(dve):
            dve.sem_inc(gated, 1)
            for c in range(DC):
                dve.wait_ge(x_hi, c + 1)
                nc.vector.tensor_tensor(k.XL[:, c, :], k.X[:, c, :], k.HH[:, c, :].bitcast(F32), ALU.subtract).then_inc(x_lo, 1)
            for c in range(2):
                for q in range(3):
                    n = 3 * c + q
                    dve.wait_ge(tr_done, n + 1)
                    a, w = (q * 512, 512) if q < 2 else (T, B)
                    nc.vector.tensor_copy(pT[:, c, a:a + w], tp[:, n % 2, 0:w]).then_inc(tr_copied, 1)
            squares.start(dve)
            with dve.Fori(0, 8) as m:
                dve.wait_ge(sig, m + 2)
                dve.wait_ge(e_done, m + 2)
                nc.vector.tensor_tensor(one(k.F, m), tokens(SA), acc[:, 1, :, 0:NW], ALU.mult).then_inc(gated, 1)
                squares.add(dve, m, 0)
            dve.wait_ge(gated, 9)
            dve.wait_ge(squares.summed, DC + 2)


def store_y(k):
    nc = k.nc
    with Stage(k, "store") as st:
        ps = st.psum("ps", [P, 4, 1024])
        turned, copied_even, copied_odd, stores = st.sems("turned copied_even copied_odd stores")
        copied = (copied_even, copied_odd)
        yt = k.Z[:, 0:9 * D].rearrange("p (t f) -> p t f", f=D)
        block = st.block()

        @block.tensor
        def _(pe):
            for t in range(9):
                m = P if t < TT else B
                if t >= 4:
                    pe.wait_ge(copied[t % 2], t // 2 - 1)
                for c in range(DC):
                    last = nc.tensor.transpose(ps[0:m, t % 4, c * P:(c + 1) * P], k.X[:, c, t * P:t * P + m], k.ident[:])
                last.then_inc(turned, 1)

        @block.vector
        def _(dve):
            for t in range(0, 9, 2):
                m = P if t < TT else B
                dve.wait_ge(turned, t + 1)
                nc.vector.tensor_copy(yt[0:m, t, :], ps[0:m, t % 4, :]).then_inc(copied_even, 1)

        @block.scalar
        def _(act):
            for t in range(1, 9, 2):
                act.wait_ge(turned, t + 1)
                nc.scalar.activation(yt[:, t, :], ps[:, t % 4, :], ACT.Copy).then_inc(copied_odd, 1)

        @block.sync
        def _(sp):
            for t in range(9):
                sp.wait_ge(copied[t % 2], t // 2 + 1)
                if t < TT:
                    sp.dma_start(k.out["y_p"][t * P:(t + 1) * P, :], yt[:, t, :]).then_inc(stores, 16)
                else:
                    sp.dma_start(k.out["y_s"], yt[0:B, TT, :]).then_inc(stores, 16)
            sp.wait_ge(stores, 9 * 16)


def _bucket(dist):
    import numpy as np
    dist = np.asarray(dist)
    near = np.maximum(dist, 0)
    ratio = np.log(np.maximum(near, 1).astype(np.float32) / np.float32(16)) / np.float32(np.log(128 / 16))
    large = np.minimum(16 + (ratio * 16).astype(np.int32), 31)
    return np.where(dist < 0, 32, np.where(near < 16, near, large))


def _one_hot(dist):
    import numpy as np
    b = _bucket(dist)
    return np.ascontiguousarray((np.arange(33).reshape((33,) + (1,) * b.ndim) == b[None]).astype(np.float32))


def _constants():
    import numpy as np
    f = np.float32
    i, j = np.arange(128)[:, None], np.arange(128)[None, :]
    n33 = np.arange(33)
    row = np.arange(64)
    kk = np.arange(24)
    ci, sj = np.arange(127)[:, None] * 16, n33[None, :] * 64
    r = np.arange(16)[:, None]
    wr, wn = np.arange(4)[:, None], np.arange(128)[None, :]
    smp = np.concatenate([2048 - (16 * np.arange(127) + 31), np.zeros(8, int), (512 - 4 * wn - wr).ravel(),
                          (2048 - 16 * wn - r).ravel()])
    m = np.arange(48, 63)
    return {
        "eye": np.eye(128, dtype=f),
        "sixteenth": (np.arange(128) % 8).astype(np.int32)[:, None],
        "upper": (i <= j).astype(f),
        "oh_samples": _one_hot(smp),
        "oh_near": _one_hot(255 - np.arange(384)),
        "oh_cmp": _one_hot(np.arange(128)[None, :] - 16 * (m[:, None] - 56) - 31).reshape(33, 15 * 128),
        "overlap": ((ci <= sj + 63) & (ci + 31 >= sj)).astype(f),
        "same_group": (row[:, None] // 4 == row[None, :] // 4).astype(f),
        "before": (n33[None, :] < n33[:, None]).astype(f).reshape(1, 33 * 33),
        "not_own": np.where(np.arange(8)[:, None] == row[None, :] // 8, 0, -1e30).astype(f),
        "head_of": (kk[:, None] // 3 == np.arange(8)[None, :]).astype(f),
        "branch_of": (kk[:, None] % 3 == np.arange(3)[None, :]).astype(f),
        "window_edge": np.where(j >= i, 0, -1e30).astype(f),
        "has_block": (np.arange(128) >= 31).astype(f)[:, None],
    }


_VIEWS = {
    "x_prompt": (1024, 1024), "x_sample": (8, 1024), "cache_cmp_kv": (160 * 8, 4096), "cache_slc_kv": (160 * 8, 4096),
    "state_win_kv": (8, 512, 256), "page_table": (8, 16), "p_prompt": (1024, 256), "p_sample": (8, 256),
    "rel_bias": (32, 8), "ln_mix_pre": (1, 1024), "w_in": (1024, 4376), "cmp_pe_k": (1, 2048), "cmp_w1_k": (2048, 128),
    "cmp_w2_k": (128, 64), "cmp_pe_v": (1, 2048), "cmp_w1_v": (2048, 128), "cmp_w2_v": (128, 64), "gm_ln_g": (1, 512),
    "gm_ln_b": (1, 512), "gm_ws": (512, 128), "gm_bs": (4, 128), "w_branch_nsa": (512, 1024), "w_branch_gm": (512, 1024),
    "w_out": (1024, 1024), "ln_mix_post": (1, 1024), "ln_ffn_pre": (1, 1024), "w_ffn_gate": (1024, 2816),
    "w_ffn_up": (1024, 2816), "w_ffn_down": (2816, 1024), "ln_ffn_post": (1, 1024), "w_ple": (256, 1024),
    "w_ple_gate": (1024, 1024), "ln_ple_post": (1, 1024),
}
_OUTS = [
    ("y_p", (1024, 1024), (1, 1024, 1024)), ("y_s", (8, 1024), (8, 1, 1024)),
    ("cmp_p", (1024, 256), (1, 1, 1024, 2, 2, 64)), ("slc_p", (1024, 256), (1, 1, 1024, 2, 2, 64)),
    ("win_p", (512, 256), (1, 1, 512, 2, 2, 64)), ("cmp_s", (8, 256), (1, 8, 1, 2, 2, 64)),
    ("slc_s", (8, 256), (1, 8, 1, 2, 2, 64)), ("win_s", (8, 512, 256), (1, 8, 512, 2, 2, 64)),
    ("gm_v", (8, 512), (1, 8, 1, 512)),
]


def kernel(**inputs):
    import numpy as _np
    import concourse.bacc as _bacc
    from concourse import mybir as _mybir
    from concourse.bass_utils import run_bass_kernel_spmd as _run

    nc = _bacc.Bacc("TRN2", target_bir_lowering=False, num_devices=1)
    arrays, g, out = {}, {}, {}
    data = {n: _np.ascontiguousarray(inputs[n]).reshape(s) for n, s in _VIEWS.items()}
    data.update(_constants())
    for n, a in data.items():
        arrays[f"in_{n}"] = a
        g[n] = nc.dram_tensor(f"in_{n}", a.shape, _mybir.dt.from_np(a.dtype), kind="ExternalInput").ap()
    for n, shape, _ in _OUTS:
        out[n] = nc.dram_tensor(f"out_{n}", shape, _mybir.dt.float32, kind="ExternalOutput").ap()
    scratch = nc.dram_tensor("bias_rows", (8, 128 * 384), _mybir.dt.float32, kind="Internal").ap()
    kept = nc.dram_tensor("kept_x", (128, 8 * 1032), _mybir.dt.float32, kind="Internal").ap()
    build(nc, g, out, scratch, kept)
    r = _run(nc, [arrays], core_ids=[0])
    return tuple(_np.asarray(r.results[0][f"out_{n}"]).reshape(full) for n, _, full in _OUTS)
```
